# Optimizing a Trainium2 kernel written in Bass

```python
import math
import jax
import jax.numpy as jnp
from jax import lax
import numpy as np

D_MODEL = 1024
BATCH = 1
SEQ = 512
DEPTH = 2

GRID_W = 64
CTX_LEN = 256
N_MIXERS = 2
CHUNK_A = 128
D_A = 2 * D_MODEL
GROUPS_A = 8
RET_HEADS = 4
RET_DK = D_MODEL // RET_HEADS
RET_DV = 2 * RET_DK
RET_CHUNK = 128
QK_W = RET_HEADS * RET_DK
V_W = RET_HEADS * RET_DV
B_IN_W = 2 * QK_W + 3 * V_W
ROPE_BASE = 10000.0
D_FF = 4 * D_MODEL
LN_EPS = 1e-5
DN_ALPHA = (2 * DEPTH) ** 0.25
DN_BETA = (8 * DEPTH) ** -0.25
N_A_LAYERS = (DEPTH + 1) // 2
N_B_LAYERS = DEPTH // 2

kernel_name = 'hybrid_gmlp_retention_deepnorm_dit'

def _layernorm(x, g, b):
    x32 = x.astype(jnp.float32)
    mu = jnp.mean(x32, -1, keepdims=True)
    var = jnp.mean(jnp.square(x32 - mu), -1, keepdims=True)
    return ((x32 - mu) * lax.rsqrt(var + LN_EPS)).astype(x.dtype) * g + b

def _headnorm(y):
    mu = jnp.mean(y, -1, keepdims=True)
    var = jnp.mean(jnp.square(y - mu), -1, keepdims=True)
    return (y - mu) * lax.rsqrt(var + LN_EPS)

def _sq_relu_mlp(h, w1, w2):
    return jnp.square(jax.nn.relu(h @ w1)) @ w2

def _chunk_gmlp(h, w_in, b_in, ln_g, ln_b, w_s, b_s, w_out):
    bn, L, _ = h.shape
    z = jax.nn.gelu(h @ w_in + b_in, approximate=False)
    u, v = z[..., :D_A], z[..., D_A:]
    v = _layernorm(v, ln_g, ln_b)
    v = v.reshape(bn, L // CHUNK_A, CHUNK_A, GROUPS_A, D_A // GROUPS_A)
    s = jnp.einsum('gij,bnjgc->bnigc', w_s, v) + b_s.T[:, :, None]
    return (u * s.reshape(bn, L, D_A)) @ w_out

def _rope_2d_tables(L, dtype):
    t = jnp.arange(L)
    row = (t // GRID_W).astype(jnp.float32)
    col = (t % GRID_W).astype(jnp.float32)
    n_freq = RET_DK // 4
    inv = ROPE_BASE ** (-jnp.arange(n_freq, dtype=jnp.float32) / n_freq)
    ang = jnp.concatenate([row[:, None] * inv, col[:, None] * inv], -1)
    return jnp.cos(ang).astype(dtype), jnp.sin(ang).astype(dtype)

def _rope(t, cos, sin):
    half = t.shape[-1] // 2
    t1, t2 = t[..., :half], t[..., half:]
    cs, sn = cos[None, :, None, :], sin[None, :, None, :]
    return jnp.concatenate([t1 * cs - t2 * sn, t1 * sn + t2 * cs], -1)

def _retention_scan(q, k, v, log_gamma, s0):
    bn, L, H, _ = q.shape
    dv = v.shape[-1]
    C = RET_CHUNK
    n = L // C
    pos = jnp.arange(C, dtype=jnp.float32)
    diff = pos[:, None] - pos[None, :]
    decay_in = jnp.where(diff[None] >= 0, jnp.exp(log_gamma[:, None, None] * jnp.maximum(diff, 0.0)[None]), 0.0)
    xi = jnp.exp(log_gamma[None, :] * (pos[:, None] + 1.0))
    zeta = jnp.exp(log_gamma[None, :] * (C - 1.0 - pos[:, None]))
    gamma_c = jnp.exp(log_gamma * C)

    def to_chunks(t):
        return t.astype(jnp.float32).reshape(bn, n, C, H, t.shape[-1]).swapaxes(0, 1)

    def step(S, qkv):
        qc, kc, vc = qkv
        scores = jnp.einsum('bihd,bjhd->bhij', qc, kc) * decay_in[None]
        intra = jnp.einsum('bhij,bjhe->bihe', scores, vc)
        inter = jnp.einsum('bihd,bhde->bihe', qc, S) * xi[None, :, :, None]
        S = S * gamma_c[None, :, None, None] + jnp.einsum('bjhd,bjhe->bhde', kc * zeta[None, :, :, None], vc)
        return S, intra + inter

    S, out = lax.scan(step, s0, (to_chunks(q), to_chunks(k), to_chunks(v)))
    return out.swapaxes(0, 1).reshape(bn, L, H, dv), S

def _retention_out(o_f, o_b, g_f, g_b, w_out):
    y = _headnorm(o_f) * jax.nn.silu(g_f.astype(jnp.float32)) + _headnorm(o_b) * jax.nn.silu(g_b.astype(jnp.float32))
    bn, L = y.shape[:2]
    return y.reshape(bn, L, V_W).astype(w_out.dtype) @ w_out

def _split_heads(p, bn, L):
    q = p[..., :QK_W].reshape(bn, L, RET_HEADS, RET_DK)
    k = p[..., QK_W:2 * QK_W].reshape(bn, L, RET_HEADS, RET_DK) * (RET_DK ** -0.5)
    v = p[..., 2 * QK_W:2 * QK_W + V_W].reshape(bn, L, RET_HEADS, RET_DV)
    return q, k, v

def _gates(p, bn, L):
    o = 2 * QK_W + V_W
    g_f = p[..., o:o + V_W].reshape(bn, L, RET_HEADS, RET_DV)
    g_b = p[..., o + V_W:o + 2 * V_W].reshape(bn, L, RET_HEADS, RET_DV)
    return g_f, g_b

def _retention_mixer(h_l, h_c, w_in, decay_p, w_out, need_ctx_out):
    bn, L, _ = h_l.shape
    lc = h_c.shape[1]
    log_gamma = jnp.log1p(-jnp.exp(decay_p.astype(jnp.float32)))
    flip = lambda t: jnp.flip(t, 1)

    p_c = h_c @ (w_in if need_ctx_out else w_in[:, :2 * QK_W + V_W])
    q_c, k_c, v_c = _split_heads(p_c, bn, lc)
    s0 = jnp.zeros((bn, RET_HEADS, RET_DK, RET_DV), jnp.float32)
    of_c, s_f = _retention_scan(q_c, k_c, v_c, log_gamma[0], s0)
    ob_c, s_b = _retention_scan(flip(q_c), flip(k_c), flip(v_c), log_gamma[1], s0)

    p_l = h_l @ w_in
    q_l, k_l, v_l = _split_heads(p_l, bn, L)
    cos, sin = _rope_2d_tables(L, q_l.dtype)
    q_l, k_l = _rope(q_l, cos, sin), _rope(k_l, cos, sin)
    of_l, _ = _retention_scan(q_l, k_l, v_l, log_gamma[0], s_f)
    ob_l, _ = _retention_scan(flip(q_l), flip(k_l), flip(v_l), log_gamma[1], s_b)
    gf_l, gb_l = _gates(p_l, bn, L)
    y_l = _retention_out(of_l, flip(ob_l), gf_l, gb_l, w_out)
    if need_ctx_out:
        gf_c, gb_c = _gates(p_c, bn, lc)
        y_c = _retention_out(of_c, flip(ob_c), gf_c, gb_c, w_out)
    else:
        y_c = None
    return y_l, y_c

def setup_inputs(seed: int = 0) -> dict:
    key = jax.random.key(seed)
    ks = jax.random.split(key, 26)
    f32 = jnp.float32

    def nrm(k, shape, scale=1.0):
        return jax.random.normal(k, shape, f32) * scale

    h_idx = jnp.arange(RET_HEADS, dtype=f32)
    decay_base = -(5.0 + h_idx) * jnp.log(2.0)
    return {
        'x': nrm(ks[0], (BATCH, SEQ, D_MODEL)),
        'c': nrm(ks[1], (BATCH, D_MODEL)),
        'ctx': nrm(ks[2], (BATCH, CTX_LEN, D_MODEL)),
        'c_ctx': nrm(ks[3], (D_MODEL,)),
        'ada_w': nrm(ks[4], (DEPTH, D_MODEL, 6 * D_MODEL), D_MODEL ** -0.5),
        'ada_b': nrm(ks[5], (DEPTH, 6 * D_MODEL), 0.02),
        'ln1_g': 1.0 + nrm(ks[6], (DEPTH, D_MODEL), 0.02),
        'ln1_b': nrm(ks[7], (DEPTH, D_MODEL), 0.02),
        'ln2_g': 1.0 + nrm(ks[8], (DEPTH, D_MODEL), 0.02),
        'ln2_b': nrm(ks[9], (DEPTH, D_MODEL), 0.02),
        'ffn_w1': nrm(ks[10], (DEPTH, D_MODEL, D_FF), D_MODEL ** -0.5),
        'ffn_w2': nrm(ks[11], (DEPTH, D_FF, D_MODEL), D_FF ** -0.5 * DN_BETA),
        'a_w_in': nrm(ks[12], (N_A_LAYERS, D_MODEL, 2 * D_A), D_MODEL ** -0.5),
        'a_b_in': nrm(ks[13], (N_A_LAYERS, 2 * D_A), 0.02),
        'a_ln_g': 1.0 + nrm(ks[14], (N_A_LAYERS, D_A), 0.02),
        'a_ln_b': nrm(ks[15], (N_A_LAYERS, D_A), 0.02),
        'a_w_s': nrm(ks[16], (N_A_LAYERS, GROUPS_A, CHUNK_A, CHUNK_A), CHUNK_A ** -0.5),
        'a_b_s': 1.0 + nrm(ks[17], (N_A_LAYERS, GROUPS_A, CHUNK_A), 0.02),
        'a_w_out': nrm(ks[18], (N_A_LAYERS, D_A, D_MODEL), D_A ** -0.5 * DN_BETA),
        'b_w_in': nrm(ks[19], (N_B_LAYERS, D_MODEL, B_IN_W), D_MODEL ** -0.5),
        'b_decay': jnp.broadcast_to(decay_base, (N_B_LAYERS, 2, RET_HEADS)) + nrm(ks[20], (N_B_LAYERS, 2, RET_HEADS), 0.05),
        'b_w_out': nrm(ks[21], (N_B_LAYERS, V_W, D_MODEL), V_W ** -0.5 * DN_BETA),
    }

def reference(x, c, ctx, c_ctx, ada_w, ada_b, ln1_g, ln1_b, ln2_g, ln2_b, ffn_w1, ffn_w2,
              a_w_in, a_b_in, a_ln_g, a_ln_b, a_w_s, a_b_s, a_w_out, b_w_in, b_decay, b_w_out):
    sc = jax.nn.silu(c)
    scc = jax.nn.silu(c_ctx)
    for i in range(DEPTH):
        need_ctx_out = i < DEPTH - 1
        mod_l = sc @ ada_w[i] + ada_b[i]
        sh1, s1, g1, sh2, s2, g2 = jnp.split(mod_l[:, None, :], 6, axis=-1)
        mod_c = scc @ ada_w[i] + ada_b[i]
        sh1c, s1c, g1c, sh2c, s2c, g2c = jnp.split(mod_c, 6, axis=-1)
        j = i // N_MIXERS
        h_l = x * (1.0 + s1) + sh1
        if i % N_MIXERS == 0:
            y_l = _chunk_gmlp(h_l, a_w_in[j], a_b_in[j], a_ln_g[j], a_ln_b[j], a_w_s[j], a_b_s[j], a_w_out[j])
            if need_ctx_out:
                y_c = _chunk_gmlp(ctx * (1.0 + s1c) + sh1c, a_w_in[j], a_b_in[j], a_ln_g[j], a_ln_b[j],
                                  a_w_s[j], a_b_s[j], a_w_out[j])
        else:
            y_l, y_c = _retention_mixer(h_l, ctx * (1.0 + s1c) + sh1c, b_w_in[j], b_decay[j], b_w_out[j],
                                        need_ctx_out)
        x = _layernorm(DN_ALPHA * x + g1 * y_l, ln1_g[i], ln1_b[i])
        x = _layernorm(DN_ALPHA * x + g2 * _sq_relu_mlp(x * (1.0 + s2) + sh2, ffn_w1[i], ffn_w2[i]),
                       ln2_g[i], ln2_b[i])
        if need_ctx_out:
            ctx = _layernorm(DN_ALPHA * ctx + g1c * y_c, ln1_g[i], ln1_b[i])
            ctx = _layernorm(DN_ALPHA * ctx + g2c * _sq_relu_mlp(ctx * (1.0 + s2c) + sh2c, ffn_w1[i], ffn_w2[i]),
                             ln2_g[i], ln2_b[i])
    return x


_drawn_inputs = setup_inputs


def setup_inputs(seed=0):
    import zlib

    import numpy as np

    out = dict(_drawn_inputs(seed))
    spreads = {}
    factors = {'a_b_in': 8.0, 'a_ln_g': 8.0, 'a_ln_b': 8.0, 'a_b_s': 8.0}
    for name, (base, spread) in spreads.items():
        noise = np.random.default_rng([zlib.crc32(name.encode()), seed]).standard_normal(out[name].shape)
        drawn = base * np.exp(spread * noise) if base else spread * noise
        out[name] = jnp.asarray(drawn.astype(out[name].dtype))
    for name, factor in factors.items():
        out[name] = (out[name] * factor).astype(out[name].dtype)
    return out
```

```python
import math
from contextlib import ExitStack

import concourse.bass as bass
from concourse import mybir

F32 = mybir.dt.float32
F32R = mybir.dt.float32r
ACT = mybir.ActivationFunctionType
ALU = mybir.AluOpType

P = 128
D = 1024
KC = D // P
LAT, CTX = 4, 2
TILES0 = LAT + CTX
TOK0 = TILES0 * P
TOKL = LAT * P
HALF0 = TOK0 // 2
DEPTH = 2
ALPHA = (2 * DEPTH) ** 0.25
EPS = 1e-5
HEADS, DK, DV = 4, 256, 512
CH = 4
PIECES_A = 2048 // 512
PIECES_F = 4096 // 512
UNIT = 1024
RAW, SPL = 4, 2
ADA_BLOCKS_L = 12



def _down(tiles, unit):
    out = []
    for half in range(2):
        out.append((f"unit{unit + 2 * half}", None, None))
        out += [(f"down{half}.{t}", t, "D") for t in range(tiles)]
    return out


def _ada(blocks):
    out = []
    for b in range(blocks):
        out += [(f"ada{4 * b + q}", None, None) for q in range(3)]
        out.append((f"rows{b}", 6 + b % 2, "A"))
        if b >= 1:
            out.append((f"cols{b - 1}", 4 + (b - 1) % 2, "D"))
    out.append((f"cols{blocks - 1}", 4 + (blocks - 1) % 2, "D"))
    return out


def _tokens(name, tiles, unit):
    return [(f"unit{unit + q}", None, None) for q in range(3)] + [(f"{name}{t}", t, {"v": "D"}.get(name, "A"))
                                                                  for t in range(tiles)]


def _ln(tiles):
    return [(f"ln{t}.{h}", [[6, 7], [4, 5]][t % 2][h], "A") for t in range(tiles) for h in range(2)]


_GMLP = []
for _c in range(CH):
    _GMLP += [(f"u{_c}.0", 6, "A"), (f"u{_c}.1", 7, "A"), (f"s{_c}.0", 4, "D"), (f"s{_c}.1", 5, "D")]
_FFN0 = [(f"up{c}.{g}", 6 + g, "A") for c in range(CH) for g in range(2)]
_FFN1 = [(f"up{c}.0", 4 + c, "A") for c in range(CH)]
_HEAD = [("q0", 4, "D"), ("q1", 5, "D"), ("k0", 6, "D"), ("kc0", 4, "D"), ("k1", 7, "D"), ("kc1", 5, "D")]
_HEAD += _tokens("v", TILES0, 4)
_HEAD += [(f"s{t}", [6, 7, 4, 5, 6, 7][t], "A") for t in range(TILES0)]
_HEAD += _tokens("gf", LAT, 8) + [(f"of{t}", 4 + t, "D") for t in range(LAT)]
_HEAD += _tokens("gb", LAT, 12) + [(f"ob{t}", 4 + t, "D") for t in reversed(range(LAT))]
_HEAD += [(f"y{t}", 4 + t, "D") for t in range(LAT)]

PHASES = [
    ("ada0a", 1, _ada(4), dict(ada=16)),
    ("h0", 1, [], dict(stage=2 * KC, full=2 * KC)),
    ("v", 4, _tokens("v", TILES0, 0), dict(units=4)),
    ("ada0b", 1, _ada(8), dict(ada=32)),
    ("gate0a", 1, [(f"gate{j}", j, "A") for j in range(4)], {}),
    ("rowsum", 1, [("rs0", 4, "A"), ("rs1", 5, "A")], {}),
    ("gmlp", PIECES_A, _GMLP + _down(TILES0, 4), dict(units=8, stage=2 * CH, full=2 * CH, add=2 * TILES0)),
    ("gate0b", 1, [(f"gate{j}", j, "A") for j in range(4)], {}),
    ("ada1", 1, _ada(12), dict(ada=48)),
    ("ln0a", 1, _ln(TILES0), dict(stage=2 * TILES0)),
    ("ffn0", PIECES_F, _FFN0 + _down(TILES0, 4), dict(units=8, stage=2 * CH, full=2 * CH, add=2 * TILES0)),
    ("gate1a", 1, [(f"gate{j}", j, "A") for j in range(2)], {}),
    ("ln0b", 1, _ln(TILES0), dict(stage=2 * TILES0)),
    ("heads", HEADS, _HEAD + _down(LAT, 16), dict(units=20, stage=18, full=16, add=2 * LAT)),
    ("gate1b", 1, [(f"gate{j}", j, "A") for j in range(2)], {}),
    ("ln1a", 1, _ln(LAT), dict(stage=2 * LAT)),
    ("ffn1", PIECES_F, _FFN1 + _down(LAT, 4), dict(units=8, stage=CH, full=CH, add=2 * LAT)),
    ("ln1b", 1, [], {}),
]
ORDER = [p[0] for p in PHASES]
TRIPS = {p[0]: p[1] for p in PHASES}
STEPS = {p[0]: p[2] for p in PHASES}
PER = {}
for _n, _t, _s, _k in PHASES:
    PER[_n] = dict(step=len(_s), A=sum(s[2] == "A" for s in _s), D=sum(s[2] == "D" for s in _s), units=0, ada=0,
                   stage=0, full=0, add=0)
    PER[_n].update(_k)
BASE = {}
_sum = dict.fromkeys(PER["v"], 0)
for _n in ORDER:
    BASE[_n] = dict(_sum)
    for _k in _sum:
        _sum[_k] += TRIPS[_n] * PER[_n][_k]
TOTAL = _sum


LATE = {"k0": 2, "k1": 3, "kc0": 4, "kc1": 5}


def count(kind, phase, i, j):
    return i * PER[phase][kind] + (BASE[phase][kind] + j + 1)


def before(kind, phase, i=0):
    return i * PER[phase][kind] + BASE[phase][kind]


def step_of(phase, i, label):
    return count("step", phase, i, [s[0] for s in STEPS[phase]].index(label))


def drained(phase, i, label):
    steps = STEPS[phase]
    at = [s[0] for s in steps].index(label)
    who = steps[at][2]
    mine = [s[0] for s in steps if s[2] == who]
    if label in LATE:
        return who, count(who, phase, i, LATE[label])
    return who, count(who, phase, i, mine.index(label))


def occupants(phase, i, label):
    steps = STEPS[phase]
    at = [s[0] for s in steps].index(label)
    bank = steps[at][1]
    for s in reversed(steps[:at]):
        if s[1] == bank:
            return [drained(phase, i, s[0])]
    found = []
    if not (isinstance(i, int) and i == 0):
        same = [s for s in steps if s[1] == bank][-1]
        who, value = drained(phase, i, same[0])
        found.append((who, value - PER[phase][who]))
        if isinstance(i, int) or phase == "v":
            return found
    for p in reversed(ORDER[:ORDER.index(phase)]):
        same = [s for s in STEPS[p] if s[1] == bank]
        if same:
            found.append(drained(p, TRIPS[p] - 1, same[-1][0]))
            break
    return found


def build(nc, w_units, ada_units, xT_d, x_d, ctx_d, cols_d, cvec_d, wsT_d, bs_d, bv_d, ln_d, decay_d, dist_d, rope_d,
          small_d, out_d):
    keep = ExitStack()
    with keep:
        def sem(name):
            return keep.enter_context(nc.semaphore(name))

        def sb(name, shape, dt=F32, scope=keep):
            return scope.enter_context(nc.sbuf_tensor(name, shape, dt))

        hT_hi = sb("hT_hi", [P, KC, TOK0], F32R)
        hT_lo = sb("hT_lo", [P, KC, TOK0], F32R)
        raw = sb("raw", [P, RAW, UNIT])
        w_hi = sb("w_hi", [P, SPL, UNIT], F32R)
        w_lo = sb("w_lo", [P, SPL, UNIT], F32R)
        res_lat = sb("res_lat", [P, LAT, D])
        gate_lat = sb("gate_lat", [P, D])
        stage = sb("stage", [P, 2, 512])
        rbuf = sb("rbuf", [P, 2, 512])
        gy = sb("gy", [P, 2, 512])
        ident = sb("ident", [P, P])
        ones = sb("ones", [P, P])
        mask = sb("mask", [P, 2, P])
        NCOL = cols_d.shape[1]
        cols = sb("cols", [P, NCOL])
        scT = sb("scT", [P, KC, 2])
        cvec = sb("cvec", [P, KC, 2])
        modc = sb("modc", [P, DEPTH, 48, 2])
        colS = sb("colS", [P, KC, 2])
        colB = sb("colB", [P, KC, 2])
        col1 = sb("col1", [P, KC, 2])
        dcol = sb("dcol", [P, P])
        bst = sb("bst", [P, 8, 4, 6])
        mv = sb("mv", [P, 8, 2])
        veps = sb("veps", [P, 8])
        rstd = sb("rstd", [P, 8])
        mhalf = sb("mhalf", [P, 8])
        lg = sb("lg", [P, 6, 8])
        lgh = sb("lgh", [P, 2])
        ADAB, LNC, BU, LNG, LNB = 0, 96, 160, 176, 192

        layer0 = ExitStack()
        res_ctx = sb("res_ctx", [P, CTX, D], scope=layer0)
        gate_ctx = sb("gate_ctx", [P, D], scope=layer0)
        act_hi0 = sb("act_hi0", [P, CH, TOK0], F32R, layer0)
        act_lo0 = sb("act_lo0", [P, CH, TOK0], F32R, layer0)
        in_gmlp = ExitStack()
        wsT = sb("wsT", [P, 8, P], scope=in_gmlp)
        rowsum = sb("rowsum", [P, 8, P], scope=in_gmlp)
        bs = sb("bs", [P, 8, P], scope=in_gmlp)
        bv = sb("bv", [P, 2048], scope=in_gmlp)
        at_start = ExitStack()
        xT = sb("xT", [P, KC, TOK0], scope=at_start)
        at_start.close()
        vtok = sb("vtok", [P, TILES0, 2048], scope=in_gmlp)
        in_gmlp.close()
        in_ffn0 = ExitStack()
        pad0 = sb("pad0", [P, 5120], scope=in_ffn0)
        lnbc0 = sb("lnbc0", [P, 2, D], scope=in_ffn0)
        in_ffn0.close()
        layer0.close()

        layer1 = ExitStack()
        PW = 2 * 512 + (512 + 384 + 256 + 128)
        pa_hi = sb("pa_hi", [P, PW], F32R, layer1)
        pa_lo = sb("pa_lo", [P, PW], F32R, layer1)
        act_hi1 = pa_hi[:, 0:CH * 512].rearrange("p (c t) -> p c t", c=CH)
        act_lo1 = pa_lo[:, 0:CH * 512].rearrange("p (c t) -> p c t", c=CH)
        in_heads = ExitStack()
        v_hi = sb("v_hi", [P, TILES0, DV], F32R, in_heads)
        v_lo = sb("v_lo", [P, TILES0, DV], F32R, in_heads)
        q_hi = sb("q_hi", [P, 2, TOKL], F32R, in_heads)
        q_lo = sb("q_lo", [P, 2, TOKL], F32R, in_heads)
        k_hi = sb("k_hi", [P, 2, TOK0], F32R, in_heads)
        k_lo = sb("k_lo", [P, 2, TOK0], F32R, in_heads)
        scr = sb("scr", [P, TILES0, TOKL], scope=in_heads)
        gs = sb("gs", [P, LAT, DV], scope=in_heads)
        y = sb("y", [P, LAT, DV], scope=in_heads)
        dec = sb("dec", [P, 2, 768], scope=in_heads)
        rope = sb("rope", [P, 2, TOKL], scope=in_heads)
        in_heads.close()
        lnbc1 = sb("lnbc1", [P, 2, D], scope=layer1)
        layer1.close()

        bank = [keep.enter_context(nc.psum_tensor(f"bank{b}", [P, 512], F32)) for b in range(8)]

        w_in = [sem(f"w_in{s}") for s in range(RAW)]
        ada_in = [sem(f"ada_in{s}") for s in range(RAW)]
        const_in = sem("const_in")
        cvec_in = sem("cvec_in")
        rope_in = sem("rope_in")
        xT_in = sem("xT_in")
        res_in = sem("res_in")
        lnbc_in = sem("lnbc_in")
        dec_in = sem("dec_in")
        out_done = sem("out_done")
        hi_done = sem("hi_done")
        lo_done = sem("lo_done")
        pe_step = sem("pe_step")
        act_drain = sem("act_drain")
        dve_drain = sem("dve_drain")
        stage_full = sem("stage_full")
        stage_hi = sem("stage_hi")
        stage_lo = sem("stage_lo")
        sc_ready = sem("sc_ready")
        col_ready = sem("col_ready")
        diag_ready = sem("diag_ready")
        gelu_done = sem("gelu_done")
        vstat = sem("vstat")
        gm_step = sem("gm_step")
        stat_step = sem("stat_step")
        stat_seen = sem("stat_seen")
        var_ready = sem("var_ready")
        rstd_ready = sem("rstd_ready")
        xn_ready = sem("xn_ready")
        res_mul = sem("res_mul")
        res_base = sem("res_base")
        res_added = sem("res_added")
        lnbc_scaled = sem("lnbc_scaled")
        psum_hi = sem("psum_hi")
        rope_step = sem("rope_step")
        y_step = sem("y_step")
        exp_done = sem("exp_done")
        mask_done = sem("mask_done")
        lgh_ready = sem("lgh_ready")
        lg_dve = sem("lg_dve")
        lg_act = sem("lg_act")
        pool_const = sem("pool_const")

        DRAIN = {"A": act_drain, "D": dve_drain}
        N_CONST = 16 * 2

        def res(t):
            return res_lat[:, t, :] if t < LAT else res_ctx[:, t - LAT, :]

        def gate_of(t):
            return gate_lat if t < LAT else gate_ctx

        def unit_in(phase, i, k):
            u = BASE[phase]["units"] + k
            return u % RAW, 16 * (u // RAW + 1) + i * (16 * PER[phase]["units"] // RAW)

        def slot(phase, k):
            return (BASE[phase]["units"] + k) % SPL

        ADA_AT = {"ada0a": 0, "ada0b": BASE["gmlp"]["units"] + 1, "ada1": BASE["ffn0"]["units"] + 1}

        def ada_slot(phase, a):
            s = (ADA_AT[phase] + a) % RAW
            earlier = 0
            for p in ORDER[:ORDER.index(phase)]:
                earlier += PER[p]["ada"] // RAW
            return s, 16 * (earlier + a // RAW + 1)

        def ada_step(phase, a):
            label = f"ada{a}" if a % 4 < 3 else f"rows{a // 4}"
            return step_of(phase, 0, label)

        BASE_RES = {"start": 0, "ln0a": TILES0, "ln0b": 2 * TILES0, "ln1a": 2 * TILES0 + LAT,
                    "ln1b": 2 * TILES0 + 2 * LAT}
        BASE_STAT = {"v": 0, "ln0a": TILES0, "ln0b": 2 * TILES0, "heads": 3 * TILES0,
                     "ln1a": 3 * TILES0 + 8 * HEADS, "ln1b": 3 * TILES0 + 8 * HEADS + LAT}
        LNS = ["ln0a", "ln0b", "ln1a", "ln1b"]

        FWD_AT = [1024, 1536, 1920, 2176]
        BWD_AT = FWD_AT[::-1]
        XN_V = TILES0
        XN_BASE = {"ln0a": TILES0, "ln0b": 2 * TILES0, "ln1a": 3 * TILES0, "ln1b": 3 * TILES0 + LAT}

        FWD_W = [512, 512, 512, 384, 256, 128]
        BWD_W = [512, 512, 512, 384, 256, 128]
        COL_READY = {"ln0a": 4, "ln0b": 8, "ln1a": 12}
        UNIT_END = {
            "v": ["unit0", "unit1", "unit2", f"v{TILES0 - 1}"],
            "gmlp": [f"u{c}.1" for c in range(CH)] + ["unit4", f"down0.{TILES0 - 1}", "unit6", f"down1.{TILES0 - 1}"],
            "ffn0": [f"up{c}.1" for c in range(CH)] + ["unit4", f"down0.{TILES0 - 1}", "unit6", f"down1.{TILES0 - 1}"],
            "ffn1": [f"up{c}.0" for c in range(CH)] + ["unit4", f"down0.{LAT - 1}", "unit6", f"down1.{LAT - 1}"],
            "heads": ["q0", "q1", "kc0", "kc1", "unit4", "unit5", "unit6", f"v{TILES0 - 1}", "unit8", "unit9",
                      "unit10", f"gf{LAT - 1}", "unit12", "unit13", "unit14", f"gb{LAT - 1}", "unit16",
                      f"down0.{LAT - 1}", "unit18", f"down1.{LAT - 1}"],
        }


        block = keep.enter_context(nc.Block())

        @block.sync
        def _(sp):
            sp.dma_start(cvec[:, :, :], cvec_d).then_inc(cvec_in, 16)
            sp.dma_start(ident[:, :], small_d[:, 0:P]).then_inc(const_in, 16)
            sp.dma_start(cols[:, :], cols_d).then_inc(const_in, 16)

            def load_ada(phase):
                first = BASE[phase]["ada"]
                for a in range(PER[phase]["ada"]):
                    s, _ = ada_slot(phase, a)
                    if a >= RAW:
                        sp.wait_ge(pe_step, ada_step(phase, a - RAW))
                    elif ADA_AT[phase]:
                        sp.wait_ge(lo_done, ADA_AT[phase] + a - RAW + 1)
                    sp.dma_start(raw[:, s, :], ada_units[first + a]).then_inc(ada_in[s], 16)

            def load_weights(u0, u1, ada_phase):
                n_ada = PER[ada_phase]["ada"]
                for u in range(u0, u0 + RAW):
                    sp.wait_ge(pe_step, ada_step(ada_phase, n_ada - RAW + u - u0))
                    sp.dma_start(raw[:, u % RAW, :], w_units[u]).then_inc(w_in[u % RAW], 16)
                trips = (u1 - u0 - RAW) // RAW
                base = u0 + RAW
                with nc.sync.Fori(0, trips) as i:
                    for j in range(RAW):
                        u = base + j
                        sp.wait_ge(lo_done, i * RAW + (u - RAW + 1))
                        sp.dma_start(raw[:, u % RAW, :], w_units[i * RAW + u]).then_inc(w_in[u % RAW], 16)
                for u in range(base + trips * RAW, u1):
                    sp.wait_ge(lo_done, u - RAW + 1)
                    sp.dma_start(raw[:, u % RAW, :], w_units[u]).then_inc(w_in[u % RAW], 16)

            first = BASE["ada0a"]["ada"]
            for a in range(PER["ada0a"]["ada"]):
                s, _ = ada_slot("ada0a", a)
                if a >= RAW:
                    sp.wait_ge(pe_step, ada_step("ada0a", a - RAW))
                sp.dma_start(raw[:, s, :], ada_units[first + a]).then_inc(ada_in[s], 16)
                if a == 7:
                    sp.dma_start(xT[:, :, :], xT_d).then_inc(xT_in, 16)
            load_weights(0, ADA_AT["ada0b"], "ada0a")
            load_ada("ada0b")
            load_weights(ADA_AT["ada0b"], ADA_AT["ada1"], "ada0b")
            load_ada("ada1")
            load_weights(ADA_AT["ada1"], TOTAL["units"], "ada1")
            for t in range(LAT):
                sp.wait_ge(res_base, BASE_RES["ln1b"] + t + 1)
                sp.dma_start(out_d[t * P:(t + 1) * P, :], res_lat[:, t, :]).then_inc(out_done, 16)
            sp.wait_ge(out_done, 16 * LAT)

        @block.tensor
        def _(pe):
            def free(phase, i, label):
                for who, value in occupants(phase, i, label):
                    pe.wait_ge(DRAIN[who], value)

            def mm3(out, s_hi, s_lo, m_hi, m_lo, first, last):
                nc.tensor.matmul(out, s_hi, m_hi, start=first, stop=False)
                nc.tensor.matmul(out, s_hi, m_lo, start=False, stop=False)
                return nc.tensor.matmul(out, s_lo, m_hi, start=False, stop=last)

            def feature_unit(phase, i, k, groups):
                pe.wait_ge(lo_done, before("units", phase, i) + (k + 1))
                s = slot(phase, k)
                for label, a, b in groups:
                    free(phase, i, label)
                    out = bank[dict((x[0], x[1]) for x in STEPS[phase])[label]][:, 0:b - a]
                    for kc in range(KC):
                        c = slice(kc * P, (kc + 1) * P)
                        last = mm3(out, w_hi[:, s, c], w_lo[:, s, c], hT_hi[:, kc, a:b], hT_lo[:, kc, a:b],
                                   kc == 0, kc == KC - 1)
                    last.then_inc(pe_step, 1)

            def token_units(phase, i, k0, name, tiles):
                for q in range(4):
                    k = k0 + q
                    pe.wait_ge(lo_done, before("units", phase, i) + (k + 1))
                    s = slot(phase, k)
                    for t in range(tiles):
                        if q == 0:
                            free(phase, i, f"{name}{t}")
                        for kk in range(2):
                            kc = 2 * q + kk
                            c = slice(kk * 512, (kk + 1) * 512)
                            tt = slice(t * P, (t + 1) * P)
                            last = mm3(bank[t][:, :], hT_hi[:, kc, tt], hT_lo[:, kc, tt], w_hi[:, s, c],
                                       w_lo[:, s, c], kc == 0, kc == KC - 1)
                        if q == 3:
                            last.then_inc(pe_step, 1)
                    if q < 3:
                        last.then_inc(pe_step, 1)

            def down(phase, i, k0, tiles, a_hi, a_lo, ready):
                for half in range(2):
                    for q in range(2):
                        k = k0 + 2 * half + q
                        pe.wait_ge(lo_done, before("units", phase, i) + (k + 1))
                        s = slot(phase, k)

                        def part(t, kks):
                            for kk in kks:
                                c = 2 * q + kk
                                if half == 0:
                                    ready(c, t)
                                if c == 0:
                                    free(phase, i, f"down{half}.{t}")
                                tt = slice(t * P, (t + 1) * P)
                                n = slice(kk * 512, (kk + 1) * 512)
                                last = mm3(bank[t][:, :], a_hi[:, c, tt], a_lo[:, c, tt], w_hi[:, s, n],
                                           w_lo[:, s, n], c == 0, c == CH - 1)
                            return last

                        if half == 0 and q == 1:
                            for t in range(tiles):
                                part(t, [0])
                            for t in range(tiles):
                                part(t, [1]).then_inc(pe_step, 1)
                        else:
                            for t in range(tiles):
                                last = part(t, [0, 1])
                                if q == 1:
                                    last.then_inc(pe_step, 1)
                            if q == 0:
                                last.then_inc(pe_step, 1)

            def ada(phase):
                blocks = PER[phase]["ada"] // 4

                def to_columns(b):
                    pe.wait_ge(*named(drained(phase, 0, f"rows{b}")))
                    free(phase, 0, f"cols{b}")
                    for j in range(4):
                        last = nc.tensor.transpose(bank[4 + b % 2][:, 2 * j:2 * j + 2],
                                                   rbuf[0:2, b % 2, j * P:(j + 1) * P], ident[0:2, 0:2])
                    last.then_inc(pe_step, 1)

                for b in range(blocks):
                    free(phase, 0, f"rows{b}")
                    for q in range(4):
                        s, value = ada_slot(phase, 4 * b + q)
                        pe.wait_ge(ada_in[s], value)
                        for kk in range(2):
                            kc = 2 * q + kk
                            last = nc.tensor.matmul(bank[6 + b % 2][0:2, :], scT[:, kc, :],
                                                    raw[:, s, kk * 512:(kk + 1) * 512], start=kc == 0,
                                                    stop=kc == KC - 1)
                        last.then_inc(pe_step, 1)
                    if b >= 1:
                        to_columns(b - 1)
                to_columns(blocks - 1)

            def named(pair):
                return DRAIN[pair[0]], pair[1]

            diags = [0]

            def gates(phase):
                for j in range(len(STEPS[phase])):
                    free(phase, 0, f"gate{j}")
                    pe.wait_ge(diag_ready, diags[0] + 1)
                    nc.tensor.matmul(bank[j][:, :], ones[:, :], gy[:, diags[0] % 2, :], start=True,
                                     stop=True).then_inc(pe_step, 1)
                    diags[0] += 1

            def ln(phase, tiles):
                for t in range(tiles):
                    pe.wait_ge(xn_ready, XN_BASE[phase] + t + 1)
                    for h in range(2):
                        free(phase, 0, f"ln{t}.{h}")
                        b = bank[[[6, 7], [4, 5]][t % 2][h]]
                        for j in range(4):
                            c = 4 * h + j
                            last = nc.tensor.transpose(b[:, j * P:(j + 1) * P], res(t)[:, c * P:(c + 1) * P],
                                                       ident[:, :])
                        last.then_inc(pe_step, 1)

            pe.wait_ge(const_in, N_CONST)
            pe.wait_ge(pool_const, 2)
            pe.wait_ge(sc_ready, 1)
            ada("ada0a")
            pe.wait_ge(stage_lo, before("stage", "v"))

            def v_trip(i):
                token_units("v", i, 0, "v", TILES0)

            v_trip(0)
            with nc.tensor.Fori(1, 4) as i:
                v_trip(i)
            ada("ada0b")
            gates("gate0a")

            pe.wait_ge(const_in, N_CONST + 16 * 2)
            for h in range(2):
                free("rowsum", 0, f"rs{h}")
                nc.tensor.matmul(bank[4 + h][:, :], ones[:, :], wsT[:, 4 * h:4 * h + 4, :].rearrange("p a b -> p (a b)"),
                                 start=True, stop=True).then_inc(pe_step, 1)
            pe.wait_ge(xn_ready, XN_V)
            for p in range(PIECES_A):
                for c in range(CH):
                    g = (CH * p + c) // 2
                    feature_unit("gmlp", p, c, [(f"u{c}.0", 0, HALF0), (f"u{c}.1", HALF0, TOK0)])
                    col = slice((CH * p + c) * P, (CH * p + c + 1) * P)
                    for h in range(2):
                        free("gmlp", p, f"s{c}.{h}")
                        for j in range(3):
                            last = nc.tensor.matmul(bank[4 + h][:, j * P:(j + 1) * P], vtok[:, 3 * h + j, col],
                                                    wsT[:, g, :], start=True, stop=True)
                        last.then_inc(pe_step, 1)

                def ready(c, t):
                    if t in (0, 3):
                        pe.wait_ge(stage_lo, count("stage", "gmlp", p, 2 * c + t // 3))
                down("gmlp", p, CH, TILES0, act_hi0, act_lo0, ready)
            gates("gate0b")
            ada("ada1")
            ln("ln0a", TILES0)
            pe.wait_ge(stage_lo, before("stage", "ffn0"))

            with nc.tensor.Fori(0, PIECES_F) as p:
                for c in range(CH):
                    feature_unit("ffn0", p, c, [(f"up{c}.0", 0, HALF0), (f"up{c}.1", HALF0, TOK0)])

                def ready(c, t):
                    if t in (0, 3):
                        pe.wait_ge(stage_lo, count("stage", "ffn0", p, 2 * c + t // 3))
                down("ffn0", p, CH, TILES0, act_hi0, act_lo0, ready)
            gates("gate1a")
            ln("ln0b", TILES0)
            pe.wait_ge(stage_lo, before("stage", "heads"))

            with nc.tensor.Fori(0, HEADS) as h:
                feature_unit("heads", h, 0, [("q0", 0, TOKL)])
                feature_unit("heads", h, 1, [("q1", 0, TOKL)])
                feature_unit("heads", h, 2, [("k0", 0, TOKL), ("kc0", TOKL, TOK0)])
                feature_unit("heads", h, 3, [("k1", 0, TOKL), ("kc1", TOKL, TOK0)])
                token_units("heads", h, 4, "v", TILES0)
                pe.wait_ge(stage_lo, count("stage", "heads", h, 5))
                for t in range(TILES0):
                    free("heads", h, f"s{t}")
                    tt = slice(t * P, (t + 1) * P)
                    b = bank[[6, 7, 4, 5, 6, 7][t]]
                    for d in range(2):
                        last = mm3(b[:, :], k_hi[:, d, tt], k_lo[:, d, tt], q_hi[:, d, :], q_lo[:, d, :],
                                   d == 0, d == 1)
                    last.then_inc(pe_step, 1)
                token_units("heads", h, 8, "gf", LAT)
                for t in range(LAT):
                    free("heads", h, f"of{t}")
                    pe.wait_ge(stage_lo, count("stage", "heads", h, 6 + 2 + t))
                    pe.wait_ge(*named(drained("heads", h, "v5")))
                    keys = [(LAT, 0 + t * P), (LAT + 1, 512 + t * P)]
                    keys += [(kt, FWD_AT[kt] + (t - kt) * P) for kt in range(t + 1)]
                    for n, (kt, at) in enumerate(keys):
                        last = mm3(bank[4 + t][:, :], pa_hi[:, at:at + P], pa_lo[:, at:at + P], v_hi[:, kt, :],
                                   v_lo[:, kt, :], n == 0, n == len(keys) - 1)
                    last.then_inc(pe_step, 1)
                token_units("heads", h, 12, "gb", LAT)
                for t in reversed(range(LAT)):
                    free("heads", h, f"ob{t}")
                    pe.wait_ge(stage_lo, count("stage", "heads", h, 12 + 2 + (LAT - 1 - t)))
                    keys = [(LAT, 0 + t * P), (LAT + 1, 512 + t * P)]
                    keys += [(kt, BWD_AT[kt] + t * P) for kt in range(t, LAT)]
                    for n, (kt, at) in enumerate(keys):
                        last = mm3(bank[4 + t][:, :], pa_hi[:, at:at + P], pa_lo[:, at:at + P], v_hi[:, kt, :],
                                   v_lo[:, kt, :], n == 0, n == len(keys) - 1)
                    last.then_inc(pe_step, 1)
                for t in range(LAT):
                    free("heads", h, f"y{t}")
                    pe.wait_ge(y_step, h * 8 + (LAT + LAT - t))
                    for j in range(CH):
                        last = nc.tensor.transpose(bank[4 + t][:, j * P:(j + 1) * P], y[:, t, j * P:(j + 1) * P],
                                                   ident[:, :])
                    last.then_inc(pe_step, 1)

                def ready(c, t):
                    if c == 0:
                        pe.wait_ge(*named(drained("heads", h, f"y{t}")))
                down("heads", h, 16, LAT, act_hi1, act_lo1, ready)
            gates("gate1b")
            ln("ln1a", LAT)
            pe.wait_ge(stage_lo, before("stage", "ffn1"))

            with nc.tensor.Fori(0, PIECES_F) as p:
                for c in range(CH):
                    feature_unit("ffn1", p, c, [(f"up{c}.0", 0, TOKL)])

                def ready(c, t):
                    if t == 0:
                        pe.wait_ge(stage_lo, count("stage", "ffn1", p, c))
                down("ffn1", p, CH, LAT, act_hi1, act_lo1, ready)

        @block.scalar
        def _(act):
            def split_hi(phase, i, k, used):
                if isinstance(i, int) and count("units", phase, i, k) > TOTAL["units"]:
                    return
                s, value = unit_in(phase, i, k)
                act.wait_ge(w_in[s], value)
                if used is not None:
                    act.wait_ge(pe_step, used)
                nc.scalar.activation(w_hi[:, slot(phase, k), :], raw[:, s, :], ACT.Copy).then_inc(hi_done, 1)

            def stage_split(phase, i, j, out, width):
                q = BASE[phase]["stage"] + j
                src = stage[:, q % 2, 0:width]
                if len(out.shape) == 3:
                    src = src.rearrange("p (a b) -> p a b", a=out.shape[1])
                nc.scalar.activation(out, src, ACT.Copy).then_inc(stage_hi, 1)

            def used_unit(phase, i, k):
                return step_of(phase, i, UNIT_END[phase][k])

            def ada(phase):
                for b in range(PER[phase]["ada"] // 4):
                    act.wait_ge(pe_step, step_of(phase, 0, f"rows{b}"))
                    if b >= 2:
                        act.wait_ge(pe_step, step_of(phase, 0, f"cols{b - 2}"))
                    nc.scalar.activation(rbuf[0:2, b % 2, :], bank[6 + b % 2][0:2, :], ACT.Copy)\
                        .then_inc(act_drain, 1)

            def gates(phase):
                n = len(STEPS[phase])
                for j in range(n):
                    act.wait_ge(pe_step, step_of(phase, 0, f"gate{j}"))
                    g = gate_lat if j < 2 else gate_ctx
                    nc.scalar.activation(g[:, (j % 2) * 512:(j % 2 + 1) * 512], bank[j][:, :], ACT.Copy)\
                        .then_inc(act_drain, 1)

            def ln(phase, tiles):
                act.wait_ge(col_ready, COL_READY[phase])
                for t in range(tiles):
                    v = 0 if t < LAT else 1
                    for h in range(2):
                        j = 2 * t + h
                        q = BASE[phase]["stage"] + j
                        b = bank[[[6, 7], [4, 5]][t % 2][h]]
                        act.wait_ge(pe_step, step_of(phase, 0, f"ln{t}.{h}"))
                        act.wait_ge(stage_lo, q - 1)
                        for c in range(4):
                            kc = 4 * h + c
                            last = nc.scalar.activation(stage[:, q % 2, c * P:(c + 1) * P], b[:, c * P:(c + 1) * P],
                                                        ACT.Identity, bias=colB[:, kc, v:v + 1],
                                                        scale=colS[:, kc, v:v + 1])
                        last.then_inc(act_drain, 1)
                        act.wait_ge(act_drain, drained(phase, 0, f"ln{t}.{h}")[1])
                        stage_split(phase, 0, j, hT_hi[:, 4 * h:4 * h + 4, t * P:(t + 1) * P], 512)

            def load_lnbc(n, dst, row):
                act.dma_start(dst[:, 0, :], ln_d[row, :].partition_broadcast(P)).then_inc(lnbc_in, 16)
                act.dma_start(dst[:, 1, :], ln_d[row + 1, :].partition_broadcast(P)).then_inc(lnbc_in, 16)

            act.wait_ge(cvec_in, 16)
            nc.scalar.activation(scT[:, :, :], cvec[:, :, :], ACT.Silu).then_inc(sc_ready, 1)
            act.dma_start(mask[:, :, :], small_d[:, P:3 * P].rearrange("p (a b) -> p a b", a=2)).then_inc(dec_in, 16)
            act.dma_start(lg[:, 0, :], decay_d.partition_broadcast(P)).then_inc(dec_in, 16)
            act.dma_start(bv[:, :], bv_d.partition_broadcast(P)).then_inc(res_in, 16)
            act.wait_ge(const_in, N_CONST)
            act.dma_start(wsT[:, :, :], wsT_d).then_inc(const_in, 16)
            act.dma_start(bs[:, :, :], bs_d.partition_broadcast(P).rearrange("p (a b) -> p a b", a=8))\
               .then_inc(const_in, 16)
            act.dma_start(res_lat[:, :, :], x_d.rearrange("(t p) d -> p t d", p=P)).then_inc(res_in, 16)
            act.dma_start(res_ctx[:, :, :], ctx_d.rearrange("(t p) d -> p t d", p=P)).then_inc(res_in, 16)

            act.wait_ge(dec_in, 32)
            nc.scalar.activation(lg[:, 1, :], lg[:, 0, :], ACT.Exp).then_inc(lg_act, 1)
            act.wait_ge(lg_dve, 1)
            nc.scalar.activation(lg[:, 3, :], lg[:, 2, :], ACT.Ln).then_inc(lg_act, 1)

            ada("ada0a")
            for j in range(2 * KC):
                kc, v = j // 2, j % 2
                a, b = (0, TOKL) if v == 0 else (TOKL, TOK0)
                act.wait_ge(stage_full, count("full", "h0", 0, j))
                stage_split("h0", 0, j, hT_hi[:, kc, a:b], b - a)
            split_hi("v", 0, 0, None)

            def v_trip(i):
                begin = before("step", "v", i)
                for k in range(4):
                    used = None if (k == 0 and isinstance(i, int) and i == 0) else \
                        (begin if k == 0 else used_unit("v", i, k - 1))
                    split_hi("v", i, k + 1, used)
                for t in range(TILES0):
                    act.wait_ge(dve_drain, drained("v", i, f"v{t}")[1])
                    c = vtok[:, t, bass.ts(i, 512)]
                    nc.scalar.activation(c, c, ACT.Gelu).then_inc(gelu_done, 1)

            v_trip(0)
            with nc.scalar.Fori(1, 4) as i:
                v_trip(i)
            ada("ada0b")
            gates("gate0a")
            for h in range(2):
                act.wait_ge(pe_step, step_of("rowsum", 0, f"rs{h}"))
                nc.scalar.activation(rowsum[:, 4 * h:4 * h + 4, :].rearrange("p a b -> p (a b)"), bank[4 + h][:, :],
                                     ACT.Copy).then_inc(act_drain, 1)

            def down_splits(phase, i, k0):
                for k in range(k0, k0 + 4):
                    split_hi(phase, i, k + 1, used_unit(phase, i, k - 1))

            for p in range(PIECES_A):
                begin = before("step", "gmlp", p)
                for c in range(CH):
                    split_hi("gmlp", p, c + 1, begin if c == 0 else used_unit("gmlp", p, c - 1))
                    for g in range(2):
                        j = 2 * c + g
                        q = BASE["gmlp"]["stage"] + 8 * p + j
                        act.wait_ge(pe_step, step_of("gmlp", p, f"u{c}.{g}"))
                        act.wait_ge(stage_full, before("full", "gmlp", p) + j - 1)
                        nc.scalar.activation(rbuf[:, q % 2, 0:HALF0], bank[6 + g][:, 0:HALF0], ACT.Gelu,
                                             bias=cols[:, BU + CH * p + c:BU + CH * p + c + 1]).then_inc(act_drain, 1)
                    for g in range(2):
                        j = 2 * c + g
                        act.wait_ge(stage_full, count("full", "gmlp", p, j))
                        stage_split("gmlp", p, j, act_hi0[:, c, g * HALF0:(g + 1) * HALF0], HALF0)
                down_splits("gmlp", p, CH)
            act.wait_ge(pe_step, before("step", "gate0b"))
            load_lnbc(0, lnbc0, 0)
            gates("gate0b")
            ada("ada1")
            ln("ln0a", TILES0)

            def ffn(phase, i, groups, width, a_hi, last_trip=False):
                begin = before("step", phase, i)
                for c in range(CH):
                    split_hi(phase, i, c + 1, begin if c == 0 else used_unit(phase, i, c - 1))
                    for g in range(groups):
                        j = groups * c + g
                        q = BASE[phase]["stage"] + j
                        act.wait_ge(pe_step, step_of(phase, i, f"up{c}.{g}"))
                        act.wait_ge(stage_full, before("full", phase, i) + (j - 1))
                        b = bank[6 + g] if groups == 2 else bank[4 + c]
                        nc.scalar.activation(rbuf[:, q % 2, 0:width], b[:, 0:width], ACT.Relu).then_inc(act_drain, 1)
                    for g in range(groups):
                        j = groups * c + g
                        act.wait_ge(stage_full, count("full", phase, i, j))
                        stage_split(phase, i, j, a_hi[:, c, g * width:(g + 1) * width], width)
                down_splits(phase, i, CH)

            with nc.scalar.Fori(0, PIECES_F) as p:
                ffn("ffn0", p, 2, HALF0, act_hi0)
            act.wait_ge(res_base, BASE_RES["ln0a"] + TILES0)
            load_lnbc(1, lnbc0, 2)
            gates("gate1a")
            ln("ln0b", TILES0)

            act.wait_ge(res_base, BASE_RES["ln0b"] + LAT)
            act.dma_start(rope[:, :, :], rope_d).then_inc(rope_in, 16)
            with nc.scalar.Fori(0, HEADS) as h:
                begin = before("step", "heads", h)
                act.wait_ge(stage_full, before("full", "heads", h))
                act.dma_start(dec[:, :, :], dist_d).then_inc(dec_in, 16)
                split_hi("heads", h, 1, begin)
                split_hi("heads", h, 2, used_unit("heads", h, 0))
                for d in range(2):
                    act.wait_ge(stage_full, count("full", "heads", h, d))
                    stage_split("heads", h, d, q_hi[:, d, :], TOKL)
                split_hi("heads", h, 3, used_unit("heads", h, 1))
                split_hi("heads", h, 4, used_unit("heads", h, 2))
                for d in range(2):
                    act.wait_ge(stage_full, count("full", "heads", h, 2 + d))
                    stage_split("heads", h, 2 + d, k_hi[:, d, 0:TOKL], TOKL)
                for d in range(2):
                    act.wait_ge(dve_drain, drained("heads", h, f"kc{d}")[1])
                    stage_split("heads", h, 4 + d, k_hi[:, d, TOKL:TOK0], CTX * P)
                for k in range(5, 9):
                    split_hi("heads", h, k, used_unit("heads", h, k - 2))
                act.wait_ge(dec_in, h * 16 + 48)
                act.wait_ge(lgh_ready, h + 1)
                for way in range(2):
                    nc.scalar.activation(dec[:, way, :], dec[:, way, :], ACT.Exp, scale=lgh[:, way:way + 1])\
                        .then_inc(exp_done, 1)
                for t in range(TILES0):
                    act.wait_ge(pe_step, step_of("heads", h, f"v{t}"))
                    nc.scalar.activation(v_hi[:, t, :], bank[t][:, :], ACT.Copy).then_inc(psum_hi, 1)
                split_hi("heads", h, 9, used_unit("heads", h, 7))
                for t in range(TILES0):
                    act.wait_ge(pe_step, step_of("heads", h, f"s{t}"))
                    nc.scalar.activation(scr[:, t, :], bank[[6, 7, 4, 5, 6, 7][t]][:, :], ACT.Copy)\
                        .then_inc(act_drain, 1)
                at = 0
                for n, w in enumerate(FWD_W):
                    act.wait_ge(stage_full, count("full", "heads", h, 4 + n))
                    stage_split("heads", h, 6 + n, pa_hi[:, at:at + w], w)
                    at += w
                    if n in (1, 3, 5):
                        k = 10 + n // 2
                        split_hi("heads", h, k, used_unit("heads", h, k - 2))
                split_hi("heads", h, 13, used_unit("heads", h, 11))
                for t in range(LAT):
                    act.wait_ge(pe_step, step_of("heads", h, f"gf{t}"))
                    nc.scalar.activation(gs[:, t, :], bank[t][:, :], ACT.Silu).then_inc(act_drain, 1)
                split_hi("heads", h, 14, used_unit("heads", h, 12))
                act.wait_ge(pe_step, step_of("heads", h, f"of{LAT - 1}"))
                at = 0
                for n, w in enumerate(BWD_W):
                    act.wait_ge(stage_full, count("full", "heads", h, 10 + n))
                    stage_split("heads", h, 12 + n, pa_hi[:, at:at + w], w)
                    at += w
                    if n in (1, 3):
                        k = 15 + n // 2
                        split_hi("heads", h, k, used_unit("heads", h, k - 2))
                split_hi("heads", h, 17, used_unit("heads", h, 15))
                for t in range(LAT):
                    act.wait_ge(pe_step, step_of("heads", h, f"gb{t}"))
                    act.wait_ge(*[dve_drain, drained("heads", h, f"of{t}")[1]])
                    nc.scalar.activation(gs[:, t, :], bank[t][:, :], ACT.Silu).then_inc(act_drain, 1)
                for t in range(LAT):
                    act.wait_ge(pe_step, step_of("heads", h, f"y{t}"))
                    nc.scalar.activation(act_hi1[:, :, t * P:(t + 1) * P],
                                         bank[4 + t][:, :].rearrange("p (a b) -> p a b", a=CH), ACT.Copy)\
                        .then_inc(psum_hi, 1)
                for k in range(18, 21):
                    split_hi("heads", h, k, used_unit("heads", h, k - 2))
            act.wait_ge(pe_step, before("step", "gate1b"))
            load_lnbc(2, lnbc1, 4)
            gates("gate1b")
            ln("ln1a", LAT)
            with nc.scalar.Fori(0, PIECES_F - 1) as p:
                ffn("ffn1", p, 1, TOKL, act_hi1)
            ffn("ffn1", PIECES_F - 1, 1, TOKL, act_hi1)
            act.wait_ge(res_base, BASE_RES["ln1a"] + LAT)
            load_lnbc(3, lnbc1, 6)

        @block.vector
        def _(dve):
            tt = nc.vector.tensor_tensor
            ts = nc.vector.tensor_scalar
            stt = nc.vector.scalar_tensor_tensor

            def f32(ap):
                return ap.bitcast(F32)

            def split_lo(phase, i, k):
                if isinstance(i, int) and count("units", phase, i, k) > TOTAL["units"]:
                    return
                dve.wait_ge(hi_done, count("units", phase, i, k))
                s, _ = unit_in(phase, i, k)
                w = slot(phase, k)
                tt(w_lo[:, w, :], raw[:, s, :], f32(w_hi[:, w, :]), ALU.subtract).then_inc(lo_done, 1)

            def stage_lo_part(phase, i, j, out, hi, width):
                q = BASE[phase]["stage"] + j
                dve.wait_ge(stage_hi, count("stage", phase, i, j))
                src = stage[:, q % 2, 0:width]
                if len(out.shape) == 3:
                    src = src.rearrange("p (a b) -> p a b", a=out.shape[1])
                tt(out, src, f32(hi), ALU.subtract).then_inc(stage_lo, 1)

            def stage_slot(phase, i, j, width):
                q = BASE[phase]["stage"] + j
                if isinstance(i, int) and count("stage", phase, i, j) < 3:
                    return stage[:, q % 2, 0:width]
                dve.wait_ge(stage_lo, count("stage", phase, i, j) - 2)
                return stage[:, q % 2, 0:width]

            def ada(phase, layer, first):
                for b in range(PER[phase]["ada"] // 4):
                    dve.wait_ge(pe_step, step_of(phase, 0, f"cols{b}"))
                    c = 4 * (first + b)
                    at = ADAB + 48 * layer + c
                    tt(modc[:, layer, c:c + 4, :], bank[4 + b % 2][:, 0:8].rearrange("p (a b) -> p a b", b=2),
                       cols[:, at:at + 4].unsqueeze(2).to_broadcast([P, 4, 2]), ALU.add).then_inc(dve_drain, 1)

            def mod(layer, part):
                return modc[:, layer, 8 * part:8 * part + 8, :]

            cr = [0]

            def columns(phase, layer, shift, scale, ln_row):
                g = cols[:, LNC + 8 * ln_row:LNC + 8 * ln_row + 8].unsqueeze(2).to_broadcast([P, 8, 2])
                b = cols[:, LNC + 8 * ln_row + 8:LNC + 8 * ln_row + 16].unsqueeze(2).to_broadcast([P, 8, 2])
                ts(col1[:, :, :], mod(layer, scale), 1.0, None, ALU.add).then_inc(col_ready, 1)
                dve.wait_ge(col_ready, cr[0] + 1)
                tt(colS[:, :, :], col1[:, :, :], g, ALU.mult).then_inc(col_ready, 1)
                tt(colB[:, :, :], col1[:, :, :], b, ALU.mult).then_inc(col_ready, 1)
                dve.wait_ge(col_ready, cr[0] + 3)
                tt(colB[:, :, :], colB[:, :, :], mod(layer, shift), ALU.add).then_inc(col_ready, 1)
                cr[0] += 4

            dg = [0]

            def diagonals(phase, layer, part):
                n = len(STEPS[phase])
                dve.wait_ge(res_added, before("add", phase))
                for j in range(n):
                    v, half = j // 2, j % 2
                    if j >= 2:
                        dve.wait_ge(pe_step, step_of(phase, 0, f"gate{j - 2}"))
                    c = 8 * part + 4 * half
                    tt(gy[:, dg[0] % 2, :].rearrange("p (a b) -> p a b", a=4),
                       ident[:, :].unsqueeze(1).to_broadcast([P, 4, P]),
                       modc[:, layer, c:c + 4, v:v + 1].to_broadcast([P, 4, P]), ALU.mult).then_inc(diag_ready, 1)
                    dg[0] += 1

            def statistics(sources, s, done):
                for n, src in enumerate(sources):
                    last = nc.vector.bn_stats(out=bst[:, s, n, :], in_=src)
                last.then_inc(stat_step, 1)
                dve.wait_ge(stat_step, 2 * done + 1)
                if not isinstance(done, int):
                    dve.sem_inc(stat_seen, 1)
                nc.vector.bn_aggr(out=mv[:, s, :], in_=bst[:, s, 0:len(sources), :]).then_inc(stat_step, 1)
                dve.wait_ge(stat_step, 2 * done + 2)
                ts(veps[:, s:s + 1], mv[:, s, 1:2], EPS, None, ALU.add).then_inc(var_ready, 1)

            def ln_rows(phase, last_phase, tiles):
                def norm(t):
                    dve.wait_ge(rstd_ready, BASE_STAT[phase] + t + 1)
                    ts(res(t), res(t), mv[:, t, 0:1], rstd[:, t:t + 1], ALU.subtract, ALU.mult).then_inc(xn_ready, 1)

                n = 2 * tiles
                end = before("add", last_phase, TRIPS[last_phase])
                for t in range(tiles):
                    dve.wait_ge(res_added, end - tiles + t + 1)
                    statistics([res(t)[:, 0:512], res(t)[:, 512:1024]], t, BASE_STAT[phase] + t)
                    if t >= 1:
                        norm(t - 1)
                norm(tiles - 1)

            def ln_split(phase, tiles):
                for t in range(tiles):
                    for h in range(2):
                        at = (slice(None), slice(4 * h, 4 * h + 4), slice(t * P, (t + 1) * P))
                        stage_lo_part(phase, 0, 2 * t + h, hT_lo[at], hT_hi[at], 512)

            def drain_half(phase, i, half, tiles):
                for t in range(tiles):
                    e = BASE[phase]["add"] + half * tiles + t
                    dve.wait_ge(pe_step, step_of(phase, i, f"down{half}.{t}"))
                    if not (isinstance(i, int) and e + i * PER[phase]["add"] < 2):
                        dve.wait_ge(res_added, count("add", phase, i, half * tiles + t) - 2)
                    tt(gy[:, e % 2, :], bank[t][:, :], gate_of(t)[:, half * 512:(half + 1) * 512], ALU.mult)\
                        .then_inc(dve_drain, 1)

            def down(phase, i, k0, tiles):
                split_lo(phase, i, k0 + 1)
                split_lo(phase, i, k0 + 2)
                drain_half(phase, i, 0, tiles)
                split_lo(phase, i, k0 + 3)
                split_lo(phase, i, k0 + 4)
                drain_half(phase, i, 1, tiles)

            dve.wait_ge(lg_act, 1)
            ts(lg[:, 2, :], lg[:, 1, :], -1.0, 1.0, ALU.mult, ALU.add).then_inc(lg_dve, 1)
            dve.wait_ge(lg_dve, 1)
            ts(lg[:, 4, :], lg[:, 2, :], -1.0, 1.0, ALU.mult, ALU.add).then_inc(lg_dve, 1)
            dve.wait_ge(lg_dve, 2)
            ts(lg[:, 4, :], lg[:, 4, :], 1e-30, None, ALU.max).then_inc(lg_dve, 1)
            dve.wait_ge(lg_dve, 3)
            nc.vector.reciprocal(lg[:, 4, :], lg[:, 4, :]).then_inc(lg_dve, 1)
            dve.wait_ge(lg_dve, 4)
            tt(lg[:, 5, :], lg[:, 4, :], lg[:, 1, :], ALU.mult).then_inc(lg_dve, 1)
            dve.wait_ge(lg_dve, 5)
            dve.wait_ge(lg_act, 2)
            tt(lg[:, 5, :], lg[:, 5, :], lg[:, 3, :], ALU.mult).then_inc(lg_dve, 1)

            dve.wait_ge(const_in, N_CONST)
            ada("ada0a", 0, 0)
            dve.wait_ge(dve_drain, before("D", "h0"))
            ts(colS[:, :, :], mod(0, 1), 1.0, None, ALU.add).then_inc(vstat, 1)
            dve.wait_ge(vstat, 1)
            dve.wait_ge(xT_in, 16)
            for j in range(2 * KC):
                kc, v = j // 2, j % 2
                a, b = (0, TOKL) if v == 0 else (TOKL, TOK0)
                ts(stage_slot("h0", 0, j, b - a), xT[:, kc, a:b], colS[:, kc, v:v + 1], mod(0, 0)[:, kc, v:v + 1],
                   ALU.mult, ALU.add).then_inc(stage_full, 1)
                if j >= 1:
                    kc, v = (j - 1) // 2, (j - 1) % 2
                    a, b = (0, TOKL) if v == 0 else (TOKL, TOK0)
                    stage_lo_part("h0", 0, j - 1, hT_lo[:, kc, a:b], hT_hi[:, kc, a:b], b - a)
            stage_lo_part("h0", 0, 2 * KC - 1, hT_lo[:, KC - 1, TOKL:TOK0], hT_hi[:, KC - 1, TOKL:TOK0], TOK0 - TOKL)
            split_lo("v", 0, 0)

            dve.wait_ge(res_in, 48)
            def v_trip(i):
                for k in range(1, 5):
                    split_lo("v", i, k)
                for t in range(TILES0):
                    dve.wait_ge(pe_step, step_of("v", i, f"v{t}"))
                    tt(vtok[:, t, bass.ts(i, 512)], bank[t][:, :], bv[:, bass.ts(i, 512)], ALU.add)\
                        .then_inc(dve_drain, 1)

            v_trip(0)
            with nc.vector.Fori(1, 4) as i:
                v_trip(i)
            for t in range(TILES0):
                dve.wait_ge(gelu_done, 3 * TILES0 + t + 1)
                statistics([vtok[:, t, n * 512:(n + 1) * 512] for n in range(4)], t, t)
            for t in range(TILES0):
                dve.wait_ge(rstd_ready, t + 1)
                ts(vtok[:, t, :], vtok[:, t, :], mv[:, t, 0:1], rstd[:, t:t + 1], ALU.subtract, ALU.mult)\
                    .then_inc(xn_ready, 1)
            ada("ada0b", 0, 4)
            dve.wait_ge(dve_drain, before("D", "gate0a"))
            diagonals("gate0a", 0, 2)

            dve.wait_ge(act_drain, before("A", "gmlp"))
            dve.wait_ge(const_in, N_CONST + 32)
            for p in range(PIECES_A):
                for c in range(CH):
                    split_lo("gmlp", p, c + 1)
                    n = CH * p + c
                    g = n // 2
                    if c:
                        dve.wait_ge(dve_drain, drained("gmlp", p, f"s{c - 1}.1")[1])
                    stt(dcol[:, :], rowsum[:, g, :], cols[:, LNB + n:LNB + n + 1], bs[:, g, :], ALU.mult, ALU.add)\
                        .then_inc(gm_step, 1)
                    dve.wait_ge(gm_step, n + 1)
                    for h in range(2):
                        j = 2 * c + h
                        q = BASE["gmlp"]["stage"] + 8 * p + j
                        st = stage_slot("gmlp", p, j, HALF0)
                        dve.wait_ge(pe_step, step_of("gmlp", p, f"s{c}.{h}"))
                        st3 = st.rearrange("p (a b) -> p a b", a=3)
                        stt(st3, bank[4 + h][:, 0:HALF0].rearrange("p (a b) -> p a b", a=3),
                            cols[:, LNG + n:LNG + n + 1], dcol[:, :].unsqueeze(1).to_broadcast([P, 3, P]),
                            ALU.mult, ALU.add).then_inc(dve_drain, 1)
                        dve.wait_ge(dve_drain, drained("gmlp", p, f"s{c}.{h}")[1])
                        dve.wait_ge(act_drain, drained("gmlp", p, f"u{c}.{h}")[1])
                        tt(st, st, rbuf[:, q % 2, 0:HALF0], ALU.mult).then_inc(stage_full, 1)
                    for h in range(2):
                        at = (slice(None), c, slice(h * HALF0, (h + 1) * HALF0))
                        stage_lo_part("gmlp", p, 2 * c + h, act_lo0[at], act_hi0[at], HALF0)
                down("gmlp", p, CH, TILES0)
            diagonals("gate0b", 0, 5)
            ln_rows("ln0a", "gmlp", TILES0)
            ada("ada1", 1, 0)
            columns("ln0a", 0, 3, 4, 0)
            ln_split("ln0a", TILES0)

            def ffn(phase, i, groups, width, a_hi, a_lo, tiles):
                for c in range(CH):
                    split_lo(phase, i, c + 1)
                    for g in range(groups):
                        j = groups * c + g
                        q = BASE[phase]["stage"] + j
                        st = stage_slot(phase, i, j, width)
                        dve.wait_ge(act_drain, drained(phase, i, f"up{c}.{g}")[1])
                        r = rbuf[:, q % 2, 0:width]
                        tt(st, r, r, ALU.mult).then_inc(stage_full, 1)
                    for g in range(groups):
                        at = (slice(None), c, slice(g * width, (g + 1) * width))
                        stage_lo_part(phase, i, groups * c + g, a_lo[at], a_hi[at], width)
                down(phase, i, CH, tiles)

            dve.wait_ge(act_drain, before("A", "ffn0"))
            with nc.vector.Fori(0, PIECES_F) as p:
                ffn("ffn0", p, 2, HALF0, act_hi0, act_lo0, TILES0)
            dve.wait_ge(dve_drain, before("D", "gate1a"))
            diagonals("gate1a", 1, 2)
            dve.wait_ge(act_drain, before("A", "gate1a"))
            columns("ln0b", 1, 0, 1, 2)
            ln_rows("ln0b", "ffn0", TILES0)
            ln_split("ln0b", TILES0)

            dve.wait_ge(res_base, BASE_RES["ln0b"] + LAT)
            dve.wait_ge(act_drain, before("A", "heads"))
            dve.wait_ge(rope_in, 16)
            dve.wait_ge(dec_in, 32)
            dve.wait_ge(lg_dve, 6)
            with nc.vector.Fori(0, HEADS) as h:
                def rotate(r, a, b, scale, j, at_q):
                    t1, t2 = bank[a[1]][:, :], bank[b[1]][:, :]
                    cos, sin = rope[:, 0, :], rope[:, 1, :]
                    dve.wait_ge(pe_step, step_of("heads", h, b[0]))
                    stt(rbuf[:, 0, :], t1, scale, cos, ALU.mult, ALU.mult).then_inc(rope_step, 1)
                    stt(rbuf[:, 1, :], t2, scale, sin, ALU.mult, ALU.mult).then_inc(rope_step, 1)
                    dve.wait_ge(rope_step, h * 4 + (2 * r + 2))
                    st = stage_slot("heads", h, j, TOKL)
                    tt(st, rbuf[:, 0, :], rbuf[:, 1, :], ALU.subtract).then_inc(stage_full, 1)
                    dve.wait_ge(stage_full, count("full", "heads", h, at_q))
                    stt(rbuf[:, 0, :], t1, scale, sin, ALU.mult, ALU.mult).then_inc(dve_drain, 1)
                    stt(rbuf[:, 1, :], t2, scale, cos, ALU.mult, ALU.mult).then_inc(dve_drain, 1)
                    dve.wait_ge(dve_drain, drained("heads", h, b[0])[1])
                    st = stage_slot("heads", h, j + 1, TOKL)
                    tt(st, rbuf[:, 0, :], rbuf[:, 1, :], ALU.add).then_inc(stage_full, 1)

                nc.vector.tensor_copy(lgh[:, :].unsqueeze(2), lg[:, 5, :].rearrange("p (w h) -> p w h", w=2)
                                      [:, :, bass.ds(h, 1)]).then_inc(lgh_ready, 1)
                split_lo("heads", h, 1)
                split_lo("heads", h, 2)
                rotate(0, ("q0", 4), ("q1", 5), 1.0, 0, 0)
                for d in range(2):
                    stage_lo_part("heads", h, d, q_lo[:, d, :], q_hi[:, d, :], TOKL)
                split_lo("heads", h, 3)
                split_lo("heads", h, 4)
                rotate(1, ("k0", 6), ("k1", 7), DK ** -0.5, 2, 2)
                for d in range(2):
                    stage_lo_part("heads", h, 2 + d, k_lo[:, d, 0:TOKL], k_hi[:, d, 0:TOKL], TOKL)
                for d in range(2):
                    dve.wait_ge(pe_step, step_of("heads", h, f"kc{d}"))
                    ts(stage_slot("heads", h, 4 + d, CTX * P), bank[4 + d][:, 0:CTX * P], DK ** -0.5, None, ALU.mult)\
                        .then_inc(dve_drain, 1)
                for d in range(2):
                    stage_lo_part("heads", h, 4 + d, k_lo[:, d, TOKL:TOK0], k_hi[:, d, TOKL:TOK0], CTX * P)
                for k in range(5, 9):
                    split_lo("heads", h, k)
                for way, a in ((0, 0), (1, 768 - P)):
                    dve.wait_ge(exp_done, h * 2 + (way + 1))
                    tt(dec[:, way, a:a + P], dec[:, way, a:a + P], mask[:, way, :], ALU.mult).then_inc(mask_done, 1)
                for t in range(TILES0):
                    dve.wait_ge(psum_hi, h * 10 + (t + 1))
                    tt(v_lo[:, t, :], bank[t][:, :], f32(v_hi[:, t, :]), ALU.subtract).then_inc(dve_drain, 1)
                split_lo("heads", h, 9)

                def decayed(way, j0, full0, keys, splits):
                    at = 0
                    for n, (kt, a, m, w) in enumerate(keys):
                        st = stage_slot("heads", h, j0 + n, w)
                        if way == 0:
                            dve.wait_ge(act_drain, drained("heads", h, f"s{kt}")[1])
                        tt(st, scr[:, kt, a:a + w], dec[:, way, m:m + w], ALU.mult).then_inc(stage_full, 1)
                        stage_lo_part("heads", h, j0 + n, pa_lo[:, at:at + w], pa_hi[:, at:at + w], w)
                        at += w
                        if n in splits:
                            split_lo("heads", h, splits[n])

                dve.wait_ge(mask_done, h * 2 + 2)
                decayed(0, 6, 4, [(LAT, 0, 256, 512), (LAT + 1, 0, 128, 512)]
                        + [(kt, kt * P, 0, 512 - kt * P) for kt in range(LAT)], {1: 10, 3: 11, 5: 12})
                split_lo("heads", h, 13)
                for t in range(LAT):
                    dve.wait_ge(pe_step, step_of("heads", h, f"of{t}"))
                    statistics([bank[4 + t][:, :]], t, h * 8 + (BASE_STAT["heads"] + t))
                    dve.wait_ge(act_drain, drained("heads", h, f"gf{t}")[1])
                    stt(y[:, t, :], bank[4 + t][:, :], mv[:, t, 0:1], gs[:, t, :], ALU.subtract, ALU.mult)\
                        .then_inc(dve_drain, 1)
                    dve.wait_ge(rstd_ready, h * 8 + (BASE_STAT["heads"] + t + 1))
                    dve.wait_ge(dve_drain, drained("heads", h, f"of{t}")[1])
                    ts(y[:, t, :], y[:, t, :], rstd[:, t:t + 1], None, ALU.mult).then_inc(y_step, 1)
                split_lo("heads", h, 14)
                decayed(1, 12, 10, [(LAT, 0, 128, 512), (LAT + 1, 0, 0, 512)]
                        + [(kt, 0, 640 - kt * P, (kt + 1) * P) for kt in reversed(range(LAT))], {1: 15, 3: 16})
                for n, t in enumerate(reversed(range(LAT))):
                    dve.wait_ge(pe_step, step_of("heads", h, f"ob{t}"))
                    statistics([bank[4 + t][:, :]], 4 + t, h * 8 + (BASE_STAT["heads"] + LAT + n))
                    dve.wait_ge(act_drain, drained("heads", h, f"gb{t}")[1])
                    if n >= 2:
                        dve.wait_ge(y_step, h * 8 + (LAT + n - 1))
                    stt(rbuf[:, n % 2, :], bank[4 + t][:, :], mv[:, 4 + t, 0:1], gs[:, t, :], ALU.subtract, ALU.mult)\
                        .then_inc(dve_drain, 1)
                    dve.wait_ge(rstd_ready, h * 8 + (BASE_STAT["heads"] + LAT + n + 1))
                    dve.wait_ge(dve_drain, drained("heads", h, f"ob{t}")[1])
                    stt(y[:, t, :], rbuf[:, n % 2, :], rstd[:, 4 + t:5 + t], y[:, t, :], ALU.mult, ALU.add)\
                        .then_inc(y_step, 1)
                for t in range(LAT):
                    dve.wait_ge(psum_hi, h * 10 + (TILES0 + t + 1))
                    tt(act_lo1[:, :, t * P:(t + 1) * P], bank[4 + t][:, :].rearrange("p (a b) -> p a b", a=CH),
                       f32(act_hi1[:, :, t * P:(t + 1) * P]), ALU.subtract).then_inc(dve_drain, 1)
                down("heads", h, 16, LAT)
            diagonals("gate1b", 1, 5)
            columns("ln1a", 1, 3, 4, 4)
            ln_rows("ln1a", "heads", LAT)
            ln_split("ln1a", LAT)
            dve.wait_ge(act_drain, before("A", "ffn1"))
            with nc.vector.Fori(0, PIECES_F - 1) as p:
                ffn("ffn1", p, 1, TOKL, act_hi1, act_lo1, LAT)
            ffn("ffn1", PIECES_F - 1, 1, TOKL, act_hi1, act_lo1, LAT)
            ln_rows("ln1b", "ffn1", LAT)

        @block.gpsimd
        def _(pool):
            gt = nc.gpsimd.tensor_tensor

            def power(phase, i, n, s):
                done = BASE_STAT[phase] + n + 1
                if not isinstance(i, int) or i:
                    done = i * 8 + done
                pool.wait_ge(var_ready, done)
                gt(rstd[:, s:s + 1], veps[:, s:s + 1], mhalf[:, s:s + 1], ALU.pow).then_inc(rstd_ready, 1)

            def add(phase, i, tiles):
                for half in range(2):
                    for t in range(tiles):
                        j = half * tiles + t
                        e = BASE[phase]["add"] + j
                        pool.wait_ge(dve_drain, drained(phase, i, f"down{half}.{t}")[1])
                        if e >= 2 * tiles or not isinstance(i, int):
                            pool.wait_ge(res_added, count("add", phase, i, j) - 2 * tiles)
                        r = res(t)[:, half * 512:(half + 1) * 512]
                        gt(r, r, gy[:, e % 2, :], ALU.add).then_inc(res_added, 1)

            def ln(phase, k, lnbc, tiles, scale):
                pool.wait_ge(lnbc_in, 32 * (k + 1))
                if scale:
                    nc.gpsimd.tensor_scalar(lnbc[:, :, :], lnbc[:, :, :], ALPHA, None, ALU.mult)\
                        .then_inc(lnbc_scaled, 1)
                    pool.wait_ge(lnbc_scaled, k + 1)
                for t in range(tiles):
                    if scale:
                        pool.wait_ge(pe_step, step_of(phase, 0, f"ln{t}.1"))
                    else:
                        pool.wait_ge(xn_ready, XN_BASE[phase] + t + 1)
                    gt(res(t), res(t), lnbc[:, 0, :], ALU.mult).then_inc(res_mul, 1)
                    pool.wait_ge(res_mul, BASE_RES[phase] - TILES0 + t + 1)
                    gt(res(t), res(t), lnbc[:, 1, :], ALU.add).then_inc(res_base, 1)

            nc.gpsimd.memset(ones[:, :], 1.0).then_inc(pool_const, 1)
            nc.gpsimd.memset(mhalf[:, :], -0.5).then_inc(pool_const, 1)
            pool.wait_ge(res_in, 48)
            for t in range(TILES0):
                nc.gpsimd.tensor_scalar(res(t), res(t), ALPHA, None, ALU.mult).then_inc(res_base, 1)
            pool.wait_ge(pool_const, 2)
            for t in range(TILES0):
                power("v", 0, t, t)
            pool.wait_ge(res_base, BASE_RES["ln0a"])
            for p in range(PIECES_A):
                add("gmlp", p, TILES0)
            for t in range(TILES0):
                power("ln0a", 0, t, t)
            ln("ln0a", 0, lnbc0, TILES0, True)
            pool.wait_ge(res_base, BASE_RES["ln0b"])
            with nc.gpsimd.Fori(0, PIECES_F) as p:
                add("ffn0", p, TILES0)
            for t in range(TILES0):
                power("ln0b", 0, t, t)
            ln("ln0b", 1, lnbc0, LAT, True)
            pool.wait_ge(res_base, BASE_RES["ln1a"])
            with nc.gpsimd.Fori(0, HEADS) as h:
                for t in range(LAT):
                    power("heads", h, t, t)
                for n, t in enumerate(reversed(range(LAT))):
                    power("heads", h, LAT + n, 4 + t)
                add("heads", h, LAT)
            for t in range(LAT):
                power("ln1a", 0, t, t)
            ln("ln1a", 2, lnbc1, LAT, True)
            pool.wait_ge(res_base, BASE_RES["ln1b"])
            with nc.gpsimd.Fori(0, PIECES_F) as p:
                add("ffn1", p, LAT)
            for t in range(LAT):
                power("ln1b", 0, t, t)
            ln("ln1b", 3, lnbc1, LAT, False)


def kernel(**inputs):
    import numpy as _np
    import concourse.bacc as _bacc
    from concourse import mybir as _mybir
    from concourse.bass_utils import run_bass_kernel_spmd as _run

    a = {k: _np.asarray(v) for k, v in inputs.items()}

    def feature_units(w):
        return w.reshape(KC, P, -1, P).transpose(2, 1, 0, 3).reshape(-1, P, UNIT)

    def token_units(w):
        return w.reshape(w.shape[0] // 256, 2, P, -1, 512).transpose(3, 0, 2, 1, 4).reshape(-1, P, UNIT)

    def ffn_units(w1, w2):
        for p in range(PIECES_F):
            yield feature_units(w1[:, p * 512:(p + 1) * 512])
            yield token_units(w2[p * 512:(p + 1) * 512])

    def units():
        w_in, w_out = a["a_w_in"][0], a["a_w_out"][0]
        yield token_units(w_in[:, 2048:])
        for p in range(PIECES_A):
            yield feature_units(w_in[:, p * 512:(p + 1) * 512])
            yield token_units(w_out[p * 512:(p + 1) * 512])
        yield from ffn_units(a["ffn_w1"][0], a["ffn_w2"][0])
        w_in, w_out = a["b_w_in"][0], a["b_w_out"][0]
        for h in range(HEADS):
            yield feature_units(w_in[:, h * DK:(h + 1) * DK])
            yield feature_units(w_in[:, 1024 + h * DK:1024 + (h + 1) * DK])
            for part in range(3):
                at = 2048 * (part + 1) + h * DV
                yield token_units(w_in[:, at:at + DV])
            yield token_units(w_out[h * DV:(h + 1) * DV])
        yield from ffn_units(a["ffn_w1"][1], a["ffn_w2"][1])

    def columns(v):
        return v.reshape(-1, P).T

    lns = [a[f"ln{n}_{x}"][l] for l in range(DEPTH) for n in (1, 2) for x in "gb"]
    t = _np.arange(TOKL)
    inv = (_np.float32(10000.0) ** (-_np.arange(DK // 4, dtype=_np.float32) / _np.float32(DK // 4)))
    ang = _np.concatenate([inv[:, None] * (t // 64).astype(_np.float32), inv[:, None] * (t % 64).astype(_np.float32)])
    rope = _np.stack([_np.cos(ang), _np.sin(ang)], 1).astype(_np.float32)
    j, m = _np.arange(P)[:, None], _np.arange(768)[None]
    dist = _np.stack([_np.maximum(m - j, 0), _np.maximum(640 + j - m, 0)], 1).astype(_np.float32)
    small = _np.concatenate([_np.eye(P), m[:, :P] >= j, j >= m[:, :P]], 1).astype(_np.float32)
    arrays = {
        "w_units": _np.concatenate(list(units())),
        "ada_units": _np.concatenate([token_units(a["ada_w"][l]) for l in range(DEPTH)]),
        "xT": _np.concatenate([a["x"][0], a["ctx"][0]]).T.reshape(KC, P, TOK0).transpose(1, 0, 2),
        "x": a["x"][0],
        "ctx": a["ctx"][0],
        "cols": _np.concatenate([columns(a["ada_b"])] + [columns(v) for v in lns]
                                + [columns(a["a_b_in"][0, :2048]), columns(a["a_ln_g"][0]), columns(a["a_ln_b"][0])], 1),
        "cvec": _np.stack([columns(a["c"][0]), columns(a["c_ctx"])], 2),
        "wsT": a["a_w_s"][0].transpose(2, 0, 1),
        "bs": a["a_b_s"][0].reshape(-1),
        "bv": a["a_b_in"][0, 2048:],
        "ln": _np.stack(lns),
        "decay": a["b_decay"][0].reshape(-1),
        "dist": dist,
        "rope": rope,
        "small": small,
    }
    nc = _bacc.Bacc("TRN2", target_bir_lowering=False, num_devices=1, dynamic_dma_scratch_size=1024)
    args, feeds = [], {}
    for name, v in arrays.items():
        feeds[name + "_d"] = _np.ascontiguousarray(v)
        args.append(nc.dram_tensor(name + "_d", v.shape, _mybir.dt.float32, kind="ExternalInput").ap())
    out = nc.dram_tensor("out_d", (TOKL, D), _mybir.dt.float32, kind="ExternalOutput").ap()
    build(nc, *args, out)
    r = _run(nc, [feeds], core_ids=[0])
    return r.results[0]["out_d"].reshape(1, TOKL, D)
```

```python
import math
from contextlib import ExitStack

import concourse.bass as bass
from concourse import mybir

F32 = mybir.dt.float32
F32R = mybir.dt.float32r
ACT = mybir.ActivationFunctionType
ALU = mybir.AluOpType

P = 128
D = 1024
KC = D // P
LAT, CTX = 4, 2
TILES0 = LAT + CTX
TOK0 = TILES0 * P
TOKL = LAT * P
HALF0 = TOK0 // 2
DEPTH = 2
ALPHA = (2 * DEPTH) ** 0.25
EPS = 1e-5
HEADS, DK, DV = 4, 256, 512
CH = 4
PIECES_A = 2048 // 512
PIECES_F = 4096 // 512
UNIT = 1024
RAW, SPL = 4, 2
SLOTS_M0, SLOTS_M1 = 8, 4
WIDE_M0, WIDE_M1 = 1024, 6 * D // (4096 // 512)



def _down(tiles, unit):
    out = []
    for half in range(2):
        out.append((f"unit{unit + 2 * half}", None, None))
        out += [(f"down{half}.{t}", t, "D") for t in range(tiles)]
    return out


def _mod(group, units, rows=None):
    return [(f"rows{group}", rows, "A") if n == KC - 1 else (f"mod{group}.{n}", None, None) for n in units]


def _tokens(name, tiles, unit):
    return [(f"unit{unit + q}", None, None) for q in range(3)] + [(f"{name}{t}", t, {"v": "D"}.get(name, "A"))
                                                                  for t in range(tiles)]


def _ln(tiles):
    return [(f"ln{t}.{h}", [[6, 7], [4, 5]][t % 2][h], "A") for t in range(tiles) for h in range(2)]


_V0 = _mod(0, range(8), 6) + [("cols0", 7, "D")]
_V0 += _mod(1, range(4)) + [("unit0", None, None)] + _mod(1, range(4, 8), 6) + [("cols1", 7, "D")]
_V0 += [("unit1", None, None), ("unit2", None, None)] + _mod(2, range(4)) + [(f"v{t}", t, "D") for t in range(3)]
_V0 += _mod(2, range(4, 8), 6) + [(f"v{t}", t, "D") for t in range(3, 6)] + [("cols2", 7, "D")]
_V = [("unit0", None, None)] + _mod(0, range(2)) + [("unit1", None, None)] + _mod(0, range(2, 4))
_V += [("unit2", None, None)] + _mod(0, range(4, 8), 6) + [(f"v{t}", t, "D") for t in range(6)] + [("cols0", 7, "D")]
_GMLP = []
for _c in range(CH):
    _GMLP += [(f"u{_c}.0", 6, "A"), (f"u{_c}.1", 7, "A"), (f"s{_c}.0", 4, "D"), (f"s{_c}.1", 5, "D")]
_UP0 = [[(f"up{c}.{g}", 6 + g, "A") for g in range(2)] for c in range(CH)]
_FFN0 = _UP0[0] + _mod(0, range(3)) + _UP0[1] + _mod(0, range(3, 6)) + _UP0[2] + _mod(0, range(6, 8), 4) + _UP0[3]
_FFN0 += [("cols0", 5, "D")]
_FFN1 = [(f"up{c}.0", 4 + c, "A") for c in range(CH)]
_HEAD = [("q0", 4, "D"), ("q1", 5, "D"), ("k0", 6, "D"), ("kc0", 4, "D"), ("k1", 7, "D"), ("kc1", 5, "D")]
_HEAD += _tokens("v", TILES0, 4)
_HEAD += [(f"s{t}", [6, 7, 4, 5, 6, 7][t], "A") for t in range(TILES0)]
_HEAD += _tokens("gf", LAT, 8) + [(f"of{t}", 4 + t, "D") for t in range(LAT)]
_HEAD += _tokens("gb", LAT, 12) + [(f"ob{t}", 4 + t, "D") for t in reversed(range(LAT))]
_HEAD += [(f"y{t}", 4 + t, "D") for t in range(LAT)]

PHASES = [
    ("v0", 1, _V0, dict(units=4, stage=2 * KC, full=2 * KC, mods=3)),
    ("v", 3, _V, dict(units=4, mods=1)),
    ("gate0a", 1, [(f"gate{j}", j, "A") for j in range(4)], {}),
    ("rowsum", 1, [("rs0", 4, "A"), ("rs1", 5, "A")], {}),
    ("gmlp", PIECES_A, _GMLP + _down(TILES0, 4), dict(units=8, stage=2 * CH, full=2 * CH, add=2 * TILES0)),
    ("gate0b", 1, [(f"gate{j}", j, "A") for j in range(4)], {}),
    ("ln0a", 1, _ln(TILES0), dict(stage=2 * TILES0)),
    ("ffn0", PIECES_F, _FFN0 + _down(TILES0, 4), dict(units=8, stage=2 * CH, full=2 * CH, add=2 * TILES0,
                                                     mods=1)),
    ("gate1a", 1, [(f"gate{j}", j, "A") for j in range(2)], {}),
    ("ln0b", 1, _ln(TILES0), dict(stage=2 * TILES0)),
    ("heads", HEADS, _HEAD + _down(LAT, 16), dict(units=20, stage=18, full=16, add=2 * LAT)),
    ("gate1b", 1, [(f"gate{j}", j, "A") for j in range(2)], {}),
    ("ln1a", 1, _ln(LAT), dict(stage=2 * LAT)),
    ("ffn1", PIECES_F, _FFN1 + _down(LAT, 4), dict(units=8, stage=CH, full=CH, add=2 * LAT)),
    ("ln1b", 1, [], {}),
]
ORDER = [p[0] for p in PHASES]
TRIPS = {p[0]: p[1] for p in PHASES}
STEPS = {p[0]: p[2] for p in PHASES}
PER = {}
for _n, _t, _s, _k in PHASES:
    PER[_n] = dict(step=len(_s), A=sum(s[2] == "A" for s in _s), D=sum(s[2] == "D" for s in _s), units=0, mods=0,
                   stage=0, full=0, add=0)
    PER[_n].update(_k)
BASE = {}
_sum = dict.fromkeys(PER["v"], 0)
for _n in ORDER:
    BASE[_n] = dict(_sum)
    for _k in _sum:
        _sum[_k] += TRIPS[_n] * PER[_n][_k]
TOTAL = _sum


LATE = {"k0": 2, "k1": 3, "kc0": 4, "kc1": 5}


def count(kind, phase, i, j):
    return i * PER[phase][kind] + (BASE[phase][kind] + j + 1)


def before(kind, phase, i=0):
    return i * PER[phase][kind] + BASE[phase][kind]


def step_of(phase, i, label):
    return count("step", phase, i, [s[0] for s in STEPS[phase]].index(label))


def drained(phase, i, label):
    steps = STEPS[phase]
    at = [s[0] for s in steps].index(label)
    who = steps[at][2]
    mine = [s[0] for s in steps if s[2] == who]
    if label in LATE:
        return who, count(who, phase, i, LATE[label])
    return who, count(who, phase, i, mine.index(label))


def occupants(phase, i, label):
    steps = STEPS[phase]
    at = [s[0] for s in steps].index(label)
    bank = steps[at][1]
    for s in reversed(steps[:at]):
        if s[1] == bank:
            return [drained(phase, i, s[0])]
    found = []
    if not (isinstance(i, int) and i == 0):
        same = [s for s in steps if s[1] == bank][-1]
        who, value = drained(phase, i, same[0])
        found.append((who, value - PER[phase][who]))
        if isinstance(i, int):
            return found
    for p in reversed(ORDER[:ORDER.index(phase)]):
        same = [s for s in STEPS[p] if s[1] == bank]
        if same:
            found.append(drained(p, TRIPS[p] - 1, same[-1][0]))
            break
    return found


def build(nc, w_units, mod0_units, mod1_units, xT_d, x_d, ctx_d, cols_d, cvec_d, wsT_d, bs_d, bv_d, ln_d, decay_d, dist_d, rope_d,
          small_d, out_d):
    keep = ExitStack()
    with keep:
        def sem(name):
            return keep.enter_context(nc.semaphore(name))

        def sb(name, shape, dt=F32, scope=keep):
            return scope.enter_context(nc.sbuf_tensor(name, shape, dt))

        hT_hi = sb("hT_hi", [P, KC, TOK0], F32R)
        hT_lo = sb("hT_lo", [P, KC, TOK0], F32R)
        raw = sb("raw", [P, RAW, UNIT])
        w_hi = sb("w_hi", [P, SPL, UNIT], F32R)
        w_lo = sb("w_lo", [P, SPL, UNIT], F32R)
        res_lat = sb("res_lat", [P, LAT, D])
        gate_lat = sb("gate_lat", [P, D])
        stage = sb("stage", [P, 2, 512])
        rbuf = sb("rbuf", [P, 2, 512])
        gy = sb("gy", [P, 2, 512])
        ident = sb("ident", [P, P])
        ones = sb("ones", [P, P])
        mask = sb("mask", [P, 2, P])
        NCOL = cols_d.shape[1]
        cols = sb("cols", [P, NCOL])
        scT = sb("scT", [P, KC, 32])
        cvec = sb("cvec", [P, KC, 2])
        modc = sb("modc", [P, DEPTH, 48, 2])
        colS = sb("colS", [P, KC, 2])
        colB = sb("colB", [P, KC, 2])
        col1 = sb("col1", [P, KC, 2])
        dcol = sb("dcol", [P, P])
        bst = sb("bst", [P, 8, 4, 6])
        mv = sb("mv", [P, 8, 2])
        veps = sb("veps", [P, 8])
        rstd = sb("rstd", [P, 8])
        mhalf = sb("mhalf", [P, 8])
        lg = sb("lg", [P, 6, 8])
        lgh = sb("lgh", [P, 2])
        ADAB, LNC, BU, LNG, LNB = 0, 96, 160, 176, 192

        layer0 = ExitStack()
        res_ctx = sb("res_ctx", [P, CTX, D], scope=layer0)
        gate_ctx = sb("gate_ctx", [P, D], scope=layer0)
        in_v = ExitStack()
        mod0 = sb("mod0", [P, SLOTS_M0, WIDE_M0], scope=in_v)
        in_v.close()
        act_hi0 = sb("act_hi0", [P, CH, TOK0], F32R, layer0)
        act_lo0 = sb("act_lo0", [P, CH, TOK0], F32R, layer0)
        in_gmlp = ExitStack()
        wsT = sb("wsT", [P, 8, P], scope=in_gmlp)
        rowsum = sb("rowsum", [P, 8, P], scope=in_gmlp)
        bs = sb("bs", [P, 8, P], scope=in_gmlp)
        bv = sb("bv", [P, 2048], scope=in_gmlp)
        at_start = ExitStack()
        xT = sb("xT", [P, KC, TOK0], scope=at_start)
        at_start.close()
        vtok = sb("vtok", [P, TILES0, 2048], scope=in_gmlp)
        in_gmlp.close()
        in_ffn0 = ExitStack()
        pad0 = sb("pad0", [P, 5120], scope=in_ffn0)
        lnbc0 = sb("lnbc0", [P, 2, D], scope=in_ffn0)
        mod1 = sb("mod1", [P, SLOTS_M1, WIDE_M1], scope=in_ffn0)
        rows1 = sb("rows1", [P, WIDE_M1 // 2], scope=in_ffn0)
        in_ffn0.close()
        layer0.close()

        layer1 = ExitStack()
        PW = 2 * 512 + (512 + 384 + 256 + 128)
        pa_hi = sb("pa_hi", [P, PW], F32R, layer1)
        pa_lo = sb("pa_lo", [P, PW], F32R, layer1)
        act_hi1 = pa_hi[:, 0:CH * 512].rearrange("p (c t) -> p c t", c=CH)
        act_lo1 = pa_lo[:, 0:CH * 512].rearrange("p (c t) -> p c t", c=CH)
        in_heads = ExitStack()
        v_hi = sb("v_hi", [P, TILES0, DV], F32R, in_heads)
        v_lo = sb("v_lo", [P, TILES0, DV], F32R, in_heads)
        q_hi = sb("q_hi", [P, 2, TOKL], F32R, in_heads)
        q_lo = sb("q_lo", [P, 2, TOKL], F32R, in_heads)
        k_hi = sb("k_hi", [P, 2, TOK0], F32R, in_heads)
        k_lo = sb("k_lo", [P, 2, TOK0], F32R, in_heads)
        scr = sb("scr", [P, TILES0, TOKL], scope=in_heads)
        gs = sb("gs", [P, LAT, DV], scope=in_heads)
        y = sb("y", [P, LAT, DV], scope=in_heads)
        dec = sb("dec", [P, 2, 768], scope=in_heads)
        rope = sb("rope", [P, 2, TOKL], scope=in_heads)
        in_heads.close()
        lnbc1 = sb("lnbc1", [P, 2, D], scope=layer1)
        layer1.close()

        bank = [keep.enter_context(nc.psum_tensor(f"bank{b}", [P, 512], F32)) for b in range(8)]

        w_in = [sem(f"w_in{s}") for s in range(RAW)]
        mod0_in = [sem(f"mod0_in{s}") for s in range(SLOTS_M0)]
        mod1_in = [sem(f"mod1_in{s}") for s in range(SLOTS_M1)]
        const_in = sem("const_in")
        cvec_in = sem("cvec_in")
        rope_in = sem("rope_in")
        xT_in = [sem(f"xT_in{s}") for s in range(4)]
        res_in = sem("res_in")
        bv_in = sem("bv_in")
        lnbc_in = sem("lnbc_in")
        dec_in = sem("dec_in")
        out_done = sem("out_done")
        hi_done = sem("hi_done")
        lo_done = sem("lo_done")
        pe_step = sem("pe_step")
        act_drain = sem("act_drain")
        dve_drain = sem("dve_drain")
        stage_full = sem("stage_full")
        stage_hi = sem("stage_hi")
        stage_lo = sem("stage_lo")
        sc_zero = sem("sc_zero")
        sc_ready = sem("sc_ready")
        col_ready = sem("col_ready")
        diag_ready = sem("diag_ready")
        gelu_done = sem("gelu_done")
        vstat = sem("vstat")
        gm_step = sem("gm_step")
        stat_step = sem("stat_step")
        stat_seen = sem("stat_seen")
        var_ready = sem("var_ready")
        rstd_ready = sem("rstd_ready")
        xn_ready = sem("xn_ready")
        res_mul = sem("res_mul")
        res_base = sem("res_base")
        res_added = sem("res_added")
        lnbc_scaled = sem("lnbc_scaled")
        psum_hi = sem("psum_hi")
        rope_step = sem("rope_step")
        y_step = sem("y_step")
        exp_done = sem("exp_done")
        mask_done = sem("mask_done")
        lgh_ready = sem("lgh_ready")
        lg_dve = sem("lg_dve")
        lg_act = sem("lg_act")
        pool_const = sem("pool_const")
        mod_step = sem("mod_step")

        DRAIN = {"A": act_drain, "D": dve_drain}
        N_CONST = 16 * 2

        def res(t):
            return res_lat[:, t, :] if t < LAT else res_ctx[:, t - LAT, :]

        def gate_of(t):
            return gate_lat if t < LAT else gate_ctx

        def unit_in(phase, i, k):
            u = BASE[phase]["units"] + k
            return u % RAW, 16 * (u // RAW + 1) + i * (16 * PER[phase]["units"] // RAW)

        def slot(phase, k):
            return (BASE[phase]["units"] + k) % SPL

        MOD_UNITS = {0: (mod0, mod0_in, SLOTS_M0, WIDE_M0), 1: (mod1, mod1_in, SLOTS_M1, WIDE_M1)}

        def groups_before(phase, i, g):
            return before("mods", phase, i) + (g - (BASE["ffn0"]["mods"] if phase == "ffn0" else 0))

        def mod_done(phase, i, g, n):
            return step_of(phase, i, f"rows{g}" if n == KC - 1 else f"mod{g}.{n}")

        BASE_RES = {"start": 0, "ln0a": TILES0, "ln0b": 2 * TILES0, "ln1a": 2 * TILES0 + LAT,
                    "ln1b": 2 * TILES0 + 2 * LAT}
        BASE_STAT = {"v": 0, "ln0a": TILES0, "ln0b": 2 * TILES0, "heads": 3 * TILES0,
                     "ln1a": 3 * TILES0 + 8 * HEADS, "ln1b": 3 * TILES0 + 8 * HEADS + LAT}
        LNS = ["ln0a", "ln0b", "ln1a", "ln1b"]

        FWD_AT = [1024, 1536, 1920, 2176]
        BWD_AT = FWD_AT[::-1]
        XN_V = PIECES_A * TILES0
        XN_BASE = {"ln0a": XN_V, "ln0b": XN_V + TILES0, "ln1a": XN_V + 2 * TILES0, "ln1b": XN_V + 2 * TILES0 + LAT}

        FWD_W = [512, 512, 512, 384, 256, 128]
        BWD_W = [512, 512, 512, 384, 256, 128]
        COL_READY = {"ln0a": 4, "ln0b": 8, "ln1a": 12}
        UNIT_END = {
            "v0": ["unit0", "unit1", "unit2", f"v{TILES0 - 1}"],
            "v": ["unit0", "unit1", "unit2", f"v{TILES0 - 1}"],
            "gmlp": [f"u{c}.1" for c in range(CH)] + ["unit4", f"down0.{TILES0 - 1}", "unit6", f"down1.{TILES0 - 1}"],
            "ffn0": [f"up{c}.1" for c in range(CH)] + ["unit4", f"down0.{TILES0 - 1}", "unit6", f"down1.{TILES0 - 1}"],
            "ffn1": [f"up{c}.0" for c in range(CH)] + ["unit4", f"down0.{LAT - 1}", "unit6", f"down1.{LAT - 1}"],
            "heads": ["q0", "q1", "kc0", "kc1", "unit4", "unit5", "unit6", f"v{TILES0 - 1}", "unit8", "unit9",
                      "unit10", f"gf{LAT - 1}", "unit12", "unit13", "unit14", f"gb{LAT - 1}", "unit16",
                      f"down0.{LAT - 1}", "unit18", f"down1.{LAT - 1}"],
        }


        block = keep.enter_context(nc.Block())

        @block.sync
        def _(sp):
            def weights(u, i=0, per=0):
                if u >= RAW:
                    sp.wait_ge(lo_done, i * per + (u - RAW + 1))
                sp.dma_start(raw[:, u % RAW, :], w_units[i * per + u]).then_inc(w_in[u % RAW], 16)

            def mods0(n, used=None, i=0):
                if used is not None:
                    sp.wait_ge(pe_step, used)
                s = n % SLOTS_M0
                sp.dma_start(mod0[:, s, :], mod0_units[i * SLOTS_M0 + n]).then_inc(mod0_in[s], 16)

            def mods1(n, used=None, i=0):
                if used is not None:
                    sp.wait_ge(pe_step, used)
                s = n % SLOTS_M1
                sp.dma_start(mod1[:, s, :], mod1_units[i * KC + n]).then_inc(mod1_in[s], 16)

            def load_xT(q):
                sp.dma_start(xT[:, 2 * q:2 * q + 2, :], xT_d[:, 2 * q:2 * q + 2, :]).then_inc(xT_in[q], 16)

            sp.dma_start(cvec[:, :, :], cvec_d).then_inc(cvec_in, 16)
            for n in range(KC):
                mods0(n)
                if n == 1:
                    sp.dma_start(ident[:, :], small_d[:, 0:P]).then_inc(const_in, 16)
                    sp.dma_start(cols[:, :], cols_d).then_inc(const_in, 16)
                if n == 5:
                    load_xT(0)
            weights(0)
            for n in range(4):
                mods0(KC + n, mod_done("v0", 0, 0, n))
            load_xT(1)
            weights(1)
            for n in range(4, KC):
                mods0(KC + n, mod_done("v0", 0, 0, n))
            load_xT(2)
            weights(2)
            load_xT(3)
            weights(3)
            sp.dma_start(bv[:, :], bv_d.partition_broadcast(P)).then_inc(bv_in, 16)
            for n in range(KC):
                mods0(2 * KC + n, mod_done("v0", 0, 1, n))
            for k in range(4):
                weights(4 + k)
                for n in (2 * k, 2 * k + 1):
                    mods0(3 * KC + n, mod_done("v0", 0, 2, n))
            sp.dma_start(res_lat[:, :, :], x_d.rearrange("(t p) d -> p t d", p=P)).then_inc(res_in, 16)
            sp.dma_start(res_ctx[:, :, :], ctx_d.rearrange("(t p) d -> p t d", p=P)).then_inc(res_in, 16)
            with nc.sync.Fori(0, 2) as i:
                for k in range(4):
                    weights(8 + k, i, 4)
                    for n in (2 * k, 2 * k + 1):
                        mods0(4 * KC + n, mod_done("v", i, 0, n), i)
            at = BASE["gmlp"]["units"]
            for k in range(4):
                weights(at + k)
            sp.wait_ge(pe_step, step_of("v", 2, "rows0"))
            sp.dma_start(wsT[:, :, :], wsT_d).then_inc(const_in, 16)
            sp.dma_start(bs[:, :, :], bs_d.partition_broadcast(P).rearrange("p (a b) -> p a b", a=8))\
               .then_inc(const_in, 16)
            with nc.sync.Fori(0, PIECES_A) as i:
                for k in range(8):
                    weights(at + RAW + k, i, 8)
            at = BASE["ffn0"]["units"] + RAW
            sp.wait_ge(pe_step, step_of("gmlp", PIECES_A - 1, "s3.1"))
            for n in range(SLOTS_M1):
                mods1(n)

            def piece(i, units):
                for k in range(8):
                    weights(at + k, i, 8)
                    for n in {1: (0, 1, 2), 2: (3, 4, 5), 3: (6, 7)}.get(k, ()):
                        if n < units:
                            mods1(SLOTS_M1 + n, mod_done("ffn0", i, 0, n), i)

            with nc.sync.Fori(0, PIECES_F - 1) as i:
                piece(i, KC)
            piece(PIECES_F - 1, KC - SLOTS_M1)
            at = BASE["heads"]["units"] + RAW
            with nc.sync.Fori(0, (TOTAL["units"] - at) // RAW) as i:
                for k in range(RAW):
                    weights(at + k, i, RAW)
            for t in range(LAT):
                sp.wait_ge(res_base, BASE_RES["ln1b"] + t + 1)
                sp.dma_start(out_d[t * P:(t + 1) * P, :], res_lat[:, t, :]).then_inc(out_done, 16)
            sp.wait_ge(out_done, 16 * LAT)

        @block.tensor
        def _(pe):
            def free(phase, i, label):
                for who, value in occupants(phase, i, label):
                    pe.wait_ge(DRAIN[who], value)

            def mm3(out, s_hi, s_lo, m_hi, m_lo, first, last):
                nc.tensor.matmul(out, s_hi, m_hi, start=first, stop=False)
                nc.tensor.matmul(out, s_hi, m_lo, start=False, stop=False)
                return nc.tensor.matmul(out, s_lo, m_hi, start=False, stop=last)

            def feature_unit(phase, i, k, groups):
                pe.wait_ge(lo_done, before("units", phase, i) + (k + 1))
                s = slot(phase, k)
                for label, a, b in groups:
                    free(phase, i, label)
                    out = bank[dict((x[0], x[1]) for x in STEPS[phase])[label]][:, 0:b - a]
                    for kc in range(KC):
                        c = slice(kc * P, (kc + 1) * P)
                        last = mm3(out, w_hi[:, s, c], w_lo[:, s, c], hT_hi[:, kc, a:b], hT_lo[:, kc, a:b],
                                   kc == 0, kc == KC - 1)
                    last.then_inc(pe_step, 1)

            def token_units(phase, i, k0, name, tiles, ready=None, between=()):
                between = dict(between)
                for q in range(4):
                    k = k0 + q
                    pe.wait_ge(lo_done, before("units", phase, i) + (k + 1))
                    s = slot(phase, k)
                    for t in range(tiles):
                        if q == 0:
                            free(phase, i, f"{name}{t}")
                        for kk in range(2):
                            kc = 2 * q + kk
                            if ready:
                                ready(kc, t)
                            c = slice(kk * 512, (kk + 1) * 512)
                            tt = slice(t * P, (t + 1) * P)
                            last = mm3(bank[t][:, :], hT_hi[:, kc, tt], hT_lo[:, kc, tt], w_hi[:, s, c],
                                       w_lo[:, s, c], kc == 0, kc == KC - 1)
                        if q == 3 or t == tiles - 1:
                            last.then_inc(pe_step, 1)
                        if (q, t) in between:
                            between[q, t]()

            def down(phase, i, k0, tiles, a_hi, a_lo, ready):
                for half in range(2):
                    for q in range(2):
                        k = k0 + 2 * half + q
                        pe.wait_ge(lo_done, before("units", phase, i) + (k + 1))
                        s = slot(phase, k)

                        def part(t, kks):
                            for kk in kks:
                                c = 2 * q + kk
                                if half == 0:
                                    ready(c, t)
                                if c == 0:
                                    free(phase, i, f"down{half}.{t}")
                                tt = slice(t * P, (t + 1) * P)
                                n = slice(kk * 512, (kk + 1) * 512)
                                last = mm3(bank[t][:, :], a_hi[:, c, tt], a_lo[:, c, tt], w_hi[:, s, n],
                                           w_lo[:, s, n], c == 0, c == CH - 1)
                            return last

                        if half == 0 and q == 1:
                            for t in range(tiles):
                                part(t, [0])
                            for t in range(tiles):
                                part(t, [1]).then_inc(pe_step, 1)
                        else:
                            for t in range(tiles):
                                last = part(t, [0, 1])
                                if q == 1:
                                    last.then_inc(pe_step, 1)
                            if q == 0:
                                last.then_inc(pe_step, 1)

            def mods(phase, i, g, units, rows):
                buf, landed, slots, wide = MOD_UNITS[phase == "ffn0"]
                w = wide // 2
                for n in units:
                    if n == 0:
                        free(phase, i, f"rows{g}")
                    s = n % slots
                    trips = KC // slots
                    pe.wait_ge(landed[s], 16 * (n // slots + 1) + 16 * trips * groups_before(phase, i, g))
                    for block in range(2):
                        tile = 32 * (2 * (n % 2) + block)
                        last = nc.tensor.matmul(bank[rows][tile:tile + 32, 0:w], scT[:, n, :],
                                                buf[:, s, block * w:(block + 1) * w], start=n < 2, stop=n >= KC - 2,
                                                tile_position=(0, tile))
                    last.then_inc(pe_step, 1)

            def mod_columns(phase, i, g, src, b):
                pe.wait_ge(*named(drained(phase, i, f"rows{g}")))
                free(phase, i, f"cols{g}")
                for j in range(src.shape[1] // P):
                    last = nc.tensor.transpose(bank[b][:, j * P:(j + 1) * P], src[:, j * P:(j + 1) * P], ident[:, :])
                last.then_inc(pe_step, 1)

            def named(pair):
                return DRAIN[pair[0]], pair[1]

            diags = [0]

            def gates(phase):
                for j in range(len(STEPS[phase])):
                    free(phase, 0, f"gate{j}")
                    pe.wait_ge(diag_ready, diags[0] + 1)
                    nc.tensor.matmul(bank[j][:, :], ones[:, :], gy[:, diags[0] % 2, :], start=True,
                                     stop=True).then_inc(pe_step, 1)
                    diags[0] += 1

            def ln(phase, tiles):
                for t in range(tiles):
                    pe.wait_ge(xn_ready, XN_BASE[phase] + t + 1)
                    for h in range(2):
                        free(phase, 0, f"ln{t}.{h}")
                        b = bank[[[6, 7], [4, 5]][t % 2][h]]
                        for j in range(4):
                            c = 4 * h + j
                            last = nc.tensor.transpose(b[:, j * P:(j + 1) * P], res(t)[:, c * P:(c + 1) * P],
                                                       ident[:, :])
                        last.then_inc(pe_step, 1)

            pe.wait_ge(const_in, N_CONST)
            pe.wait_ge(pool_const, 2)
            pe.wait_ge(sc_ready, 1)
            mods("v0", 0, 0, range(KC), 6)
            mod_columns("v0", 0, 0, rbuf[:, 0, :], 7)

            def hT_ready(kc, t):
                if t in (0, LAT):
                    pe.wait_ge(stage_lo, 2 * kc + t // LAT + 1)

            def part(g, units):
                return lambda: mods("v0", 0, g, units, 6)

            def columns_of(g):
                return lambda: mod_columns("v0", 0, g, rbuf[:, 0, :], 7)

            token_units("v0", 0, 0, "v", TILES0, hT_ready,
                        {(0, 2): part(1, range(4)), (0, 5): part(1, range(4, KC)), (1, 2): columns_of(1),
                         (2, 5): part(2, range(4)), (3, 2): part(2, range(4, KC)), (3, 5): columns_of(2)})
            with nc.tensor.Fori(0, 3) as i:
                def part(units):
                    return lambda: mods("v", i, 0, units, 6)

                token_units("v", i, 0, "v", TILES0, None,
                            {(0, 5): part(range(2)), (1, 5): part(range(2, 4)), (2, 5): part(range(4, KC)),
                             (3, 5): lambda: mod_columns("v", i, 0, rbuf[:, 0, :], 7)})
            gates("gate0a")

            pe.wait_ge(const_in, N_CONST + 16 * 2)
            for h in range(2):
                free("rowsum", 0, f"rs{h}")
                nc.tensor.matmul(bank[4 + h][:, :], ones[:, :], wsT[:, 4 * h:4 * h + 4, :].rearrange("p a b -> p (a b)"),
                                 start=True, stop=True).then_inc(pe_step, 1)
            for p in range(PIECES_A):
                for c in range(CH):
                    g = (CH * p + c) // 2
                    feature_unit("gmlp", p, c, [(f"u{c}.0", 0, HALF0), (f"u{c}.1", HALF0, TOK0)])
                    col = slice((CH * p + c) * P, (CH * p + c + 1) * P)
                    if c == 0:
                        pe.wait_ge(xn_ready, (p + 1) * TILES0)
                    for h in range(2):
                        free("gmlp", p, f"s{c}.{h}")
                        for j in range(3):
                            last = nc.tensor.matmul(bank[4 + h][:, j * P:(j + 1) * P], vtok[:, 3 * h + j, col],
                                                    wsT[:, g, :], start=True, stop=True)
                        last.then_inc(pe_step, 1)

                def ready(c, t):
                    if t in (0, 3):
                        pe.wait_ge(stage_lo, count("stage", "gmlp", p, 2 * c + t // 3))
                down("gmlp", p, CH, TILES0, act_hi0, act_lo0, ready)
            gates("gate0b")
            ln("ln0a", TILES0)
            pe.wait_ge(stage_lo, before("stage", "ffn0"))

            with nc.tensor.Fori(0, PIECES_F) as p:
                for c in range(CH):
                    feature_unit("ffn0", p, c, [(f"up{c}.0", 0, HALF0), (f"up{c}.1", HALF0, TOK0)])
                    if c < 3:
                        mods("ffn0", p, 0, [(0, 1, 2), (3, 4, 5), (6, 7)][c], 4)
                mod_columns("ffn0", p, 0, rows1, 5)

                def ready(c, t):
                    if t in (0, 3):
                        pe.wait_ge(stage_lo, count("stage", "ffn0", p, 2 * c + t // 3))
                down("ffn0", p, CH, TILES0, act_hi0, act_lo0, ready)
            gates("gate1a")
            ln("ln0b", TILES0)
            pe.wait_ge(stage_lo, before("stage", "heads"))

            with nc.tensor.Fori(0, HEADS) as h:
                feature_unit("heads", h, 0, [("q0", 0, TOKL)])
                feature_unit("heads", h, 1, [("q1", 0, TOKL)])
                feature_unit("heads", h, 2, [("k0", 0, TOKL), ("kc0", TOKL, TOK0)])
                feature_unit("heads", h, 3, [("k1", 0, TOKL), ("kc1", TOKL, TOK0)])
                token_units("heads", h, 4, "v", TILES0)
                pe.wait_ge(stage_lo, count("stage", "heads", h, 5))
                for t in range(TILES0):
                    free("heads", h, f"s{t}")
                    tt = slice(t * P, (t + 1) * P)
                    b = bank[[6, 7, 4, 5, 6, 7][t]]
                    for d in range(2):
                        last = mm3(b[:, :], k_hi[:, d, tt], k_lo[:, d, tt], q_hi[:, d, :], q_lo[:, d, :],
                                   d == 0, d == 1)
                    last.then_inc(pe_step, 1)
                token_units("heads", h, 8, "gf", LAT)
                for t in range(LAT):
                    free("heads", h, f"of{t}")
                    pe.wait_ge(stage_lo, count("stage", "heads", h, 6 + 2 + t))
                    pe.wait_ge(*named(drained("heads", h, "v5")))
                    keys = [(LAT, 0 + t * P), (LAT + 1, 512 + t * P)]
                    keys += [(kt, FWD_AT[kt] + (t - kt) * P) for kt in range(t + 1)]
                    for n, (kt, at) in enumerate(keys):
                        last = mm3(bank[4 + t][:, :], pa_hi[:, at:at + P], pa_lo[:, at:at + P], v_hi[:, kt, :],
                                   v_lo[:, kt, :], n == 0, n == len(keys) - 1)
                    last.then_inc(pe_step, 1)
                token_units("heads", h, 12, "gb", LAT)
                for t in reversed(range(LAT)):
                    free("heads", h, f"ob{t}")
                    pe.wait_ge(stage_lo, count("stage", "heads", h, 12 + 2 + (LAT - 1 - t)))
                    keys = [(LAT, 0 + t * P), (LAT + 1, 512 + t * P)]
                    keys += [(kt, BWD_AT[kt] + t * P) for kt in range(t, LAT)]
                    for n, (kt, at) in enumerate(keys):
                        last = mm3(bank[4 + t][:, :], pa_hi[:, at:at + P], pa_lo[:, at:at + P], v_hi[:, kt, :],
                                   v_lo[:, kt, :], n == 0, n == len(keys) - 1)
                    last.then_inc(pe_step, 1)
                for t in range(LAT):
                    free("heads", h, f"y{t}")
                    pe.wait_ge(y_step, h * 8 + (LAT + LAT - t))
                    for j in range(CH):
                        last = nc.tensor.transpose(bank[4 + t][:, j * P:(j + 1) * P], y[:, t, j * P:(j + 1) * P],
                                                   ident[:, :])
                    last.then_inc(pe_step, 1)

                def ready(c, t):
                    if c == 0:
                        pe.wait_ge(*named(drained("heads", h, f"y{t}")))
                down("heads", h, 16, LAT, act_hi1, act_lo1, ready)
            gates("gate1b")
            ln("ln1a", LAT)
            pe.wait_ge(stage_lo, before("stage", "ffn1"))

            with nc.tensor.Fori(0, PIECES_F) as p:
                for c in range(CH):
                    feature_unit("ffn1", p, c, [(f"up{c}.0", 0, TOKL)])

                def ready(c, t):
                    if t == 0:
                        pe.wait_ge(stage_lo, count("stage", "ffn1", p, c))
                down("ffn1", p, CH, LAT, act_hi1, act_lo1, ready)

        @block.scalar
        def _(act):
            def split_hi(phase, i, k, used):
                if isinstance(i, int) and count("units", phase, i, k) > TOTAL["units"]:
                    return
                s, value = unit_in(phase, i, k)
                act.wait_ge(w_in[s], value)
                if used is not None:
                    act.wait_ge(pe_step, used)
                nc.scalar.activation(w_hi[:, slot(phase, k), :], raw[:, s, :], ACT.Copy).then_inc(hi_done, 1)

            def stage_split(phase, i, j, out, width):
                q = BASE[phase]["stage"] + j
                src = stage[:, q % 2, 0:width]
                if len(out.shape) == 3:
                    src = src.rearrange("p (a b) -> p a b", a=out.shape[1])
                nc.scalar.activation(out, src, ACT.Copy).then_inc(stage_hi, 1)

            def used_unit(phase, i, k):
                return step_of(phase, i, UNIT_END[phase][k])

            def mod_rows(phase, i, g, out, b, used):
                act.wait_ge(pe_step, step_of(phase, i, f"rows{g}"))
                if used is not None:
                    act.wait_ge(pe_step, used)
                nc.scalar.activation(out, bank[b][:, 0:out.shape[1]], ACT.Copy).then_inc(act_drain, 1)

            def gates(phase):
                n = len(STEPS[phase])
                for j in range(n):
                    act.wait_ge(pe_step, step_of(phase, 0, f"gate{j}"))
                    g = gate_lat if j < 2 else gate_ctx
                    nc.scalar.activation(g[:, (j % 2) * 512:(j % 2 + 1) * 512], bank[j][:, :], ACT.Copy)\
                        .then_inc(act_drain, 1)

            def ln(phase, tiles):
                act.wait_ge(col_ready, COL_READY[phase])
                for t in range(tiles):
                    v = 0 if t < LAT else 1
                    for h in range(2):
                        j = 2 * t + h
                        q = BASE[phase]["stage"] + j
                        b = bank[[[6, 7], [4, 5]][t % 2][h]]
                        act.wait_ge(pe_step, step_of(phase, 0, f"ln{t}.{h}"))
                        act.wait_ge(stage_lo, q - 1)
                        for c in range(4):
                            kc = 4 * h + c
                            last = nc.scalar.activation(stage[:, q % 2, c * P:(c + 1) * P], b[:, c * P:(c + 1) * P],
                                                        ACT.Identity, bias=colB[:, kc, v:v + 1],
                                                        scale=colS[:, kc, v:v + 1])
                        last.then_inc(act_drain, 1)
                        act.wait_ge(act_drain, drained(phase, 0, f"ln{t}.{h}")[1])
                        stage_split(phase, 0, j, hT_hi[:, 4 * h:4 * h + 4, t * P:(t + 1) * P], 512)

            def load_lnbc(n, dst, row):
                act.dma_start(dst[:, 0, :], ln_d[row, :].partition_broadcast(P)).then_inc(lnbc_in, 16)
                act.dma_start(dst[:, 1, :], ln_d[row + 1, :].partition_broadcast(P)).then_inc(lnbc_in, 16)

            act.wait_ge(cvec_in, 16)
            act.wait_ge(sc_zero, 1)
            nc.scalar.activation(scT[:, :, 0:2], cvec[:, :, :], ACT.Silu).then_inc(sc_ready, 1)
            act.dma_start(mask[:, :, :], small_d[:, P:3 * P].rearrange("p (a b) -> p a b", a=2)).then_inc(dec_in, 16)
            act.dma_start(lg[:, 0, :], decay_d.partition_broadcast(P)).then_inc(dec_in, 16)
            act.wait_ge(dec_in, 32)
            nc.scalar.activation(lg[:, 1, :], lg[:, 0, :], ACT.Exp).then_inc(lg_act, 1)
            act.wait_ge(lg_dve, 1)
            nc.scalar.activation(lg[:, 3, :], lg[:, 2, :], ACT.Ln).then_inc(lg_act, 1)

            def h0_split(kcs):
                for j in [2 * kc + v for kc in kcs for v in range(2)]:
                    kc, v = j // 2, j % 2
                    a, b = (0, TOKL) if v == 0 else (TOKL, TOK0)
                    act.wait_ge(stage_full, count("full", "v0", 0, j))
                    stage_split("v0", 0, j, hT_hi[:, kc, a:b], b - a)

            mod_rows("v0", 0, 0, rbuf[:, 0, :], 6, None)
            h0_split(range(2))
            split_hi("v0", 0, 0, None)
            h0_split(range(2, 4))
            split_hi("v0", 0, 1, None)
            mod_rows("v0", 0, 1, rbuf[:, 0, :], 6, step_of("v0", 0, "cols0"))
            split_hi("v0", 0, 2, used_unit("v0", 0, 0))
            h0_split(range(4, 6))
            split_hi("v0", 0, 3, used_unit("v0", 0, 1))
            h0_split(range(6, 8))
            split_hi("v0", 0, 4, used_unit("v0", 0, 2))

            def gelus(phase, i, at):
                for t in range(TILES0):
                    act.wait_ge(dve_drain, drained(phase, i, f"v{t}")[1])
                    c = vtok[:, t, bass.ds(at, 512)]
                    nc.scalar.activation(c, c, ACT.Gelu).then_inc(gelu_done, 1)

            mod_rows("v0", 0, 2, rbuf[:, 0, :], 6, step_of("v0", 0, "cols1"))
            gelus("v0", 0, 0)
            with nc.scalar.Fori(0, 3) as i:
                begin = before("step", "v", i)
                split_hi("v", i, 1, begin - 1)
                for k in range(1, 4):
                    split_hi("v", i, k + 1, used_unit("v", i, k - 1))
                mod_rows("v", i, 0, rbuf[:, 0, :], 6, begin)
                gelus("v", i, i * 512 + 512)
            gates("gate0a")
            for h in range(2):
                act.wait_ge(pe_step, step_of("rowsum", 0, f"rs{h}"))
                nc.scalar.activation(rowsum[:, 4 * h:4 * h + 4, :].rearrange("p a b -> p (a b)"), bank[4 + h][:, :],
                                     ACT.Copy).then_inc(act_drain, 1)

            def down_splits(phase, i, k0):
                for k in range(k0, k0 + 4):
                    split_hi(phase, i, k + 1, used_unit(phase, i, k - 1))

            for p in range(PIECES_A):
                begin = before("step", "gmlp", p)
                for c in range(CH):
                    split_hi("gmlp", p, c + 1, begin if c == 0 else used_unit("gmlp", p, c - 1))
                    for g in range(2):
                        j = 2 * c + g
                        q = BASE["gmlp"]["stage"] + 8 * p + j
                        act.wait_ge(pe_step, step_of("gmlp", p, f"u{c}.{g}"))
                        act.wait_ge(stage_full, before("full", "gmlp", p) + j - 1)
                        nc.scalar.activation(rbuf[:, q % 2, 0:HALF0], bank[6 + g][:, 0:HALF0], ACT.Gelu,
                                             bias=cols[:, BU + CH * p + c:BU + CH * p + c + 1]).then_inc(act_drain, 1)
                    for g in range(2):
                        j = 2 * c + g
                        act.wait_ge(stage_full, count("full", "gmlp", p, j))
                        stage_split("gmlp", p, j, act_hi0[:, c, g * HALF0:(g + 1) * HALF0], HALF0)
                down_splits("gmlp", p, CH)
            act.wait_ge(pe_step, before("step", "gate0b"))
            load_lnbc(0, lnbc0, 0)
            gates("gate0b")
            ln("ln0a", TILES0)

            def ffn(phase, i, groups, width, a_hi, last_trip=False):
                begin = before("step", phase, i)
                for c in range(CH):
                    split_hi(phase, i, c + 1, begin if c == 0 else used_unit(phase, i, c - 1))
                    for g in range(groups):
                        j = groups * c + g
                        q = BASE[phase]["stage"] + j
                        act.wait_ge(pe_step, step_of(phase, i, f"up{c}.{g}"))
                        act.wait_ge(stage_full, before("full", phase, i) + (j - 1))
                        b = bank[6 + g] if groups == 2 else bank[4 + c]
                        nc.scalar.activation(rbuf[:, q % 2, 0:width], b[:, 0:width], ACT.Relu).then_inc(act_drain, 1)
                    for g in range(groups):
                        j = groups * c + g
                        act.wait_ge(stage_full, count("full", phase, i, j))
                        stage_split(phase, i, j, a_hi[:, c, g * width:(g + 1) * width], width)
                    if phase == "ffn0" and c == 2:
                        mod_rows(phase, i, 0, rows1[:, :], 4, begin)
                down_splits(phase, i, CH)

            with nc.scalar.Fori(0, PIECES_F) as p:
                ffn("ffn0", p, 2, HALF0, act_hi0)
            act.wait_ge(res_base, BASE_RES["ln0a"] + TILES0)
            load_lnbc(1, lnbc0, 2)
            gates("gate1a")
            ln("ln0b", TILES0)

            act.wait_ge(res_base, BASE_RES["ln0b"] + LAT)
            act.dma_start(rope[:, :, :], rope_d).then_inc(rope_in, 16)
            with nc.scalar.Fori(0, HEADS) as h:
                begin = before("step", "heads", h)
                act.wait_ge(stage_full, before("full", "heads", h))
                act.dma_start(dec[:, :, :], dist_d).then_inc(dec_in, 16)
                split_hi("heads", h, 1, begin)
                split_hi("heads", h, 2, used_unit("heads", h, 0))
                for d in range(2):
                    act.wait_ge(stage_full, count("full", "heads", h, d))
                    stage_split("heads", h, d, q_hi[:, d, :], TOKL)
                split_hi("heads", h, 3, used_unit("heads", h, 1))
                split_hi("heads", h, 4, used_unit("heads", h, 2))
                for d in range(2):
                    act.wait_ge(stage_full, count("full", "heads", h, 2 + d))
                    stage_split("heads", h, 2 + d, k_hi[:, d, 0:TOKL], TOKL)
                for d in range(2):
                    act.wait_ge(dve_drain, drained("heads", h, f"kc{d}")[1])
                    stage_split("heads", h, 4 + d, k_hi[:, d, TOKL:TOK0], CTX * P)
                for k in range(5, 9):
                    split_hi("heads", h, k, used_unit("heads", h, k - 2))
                act.wait_ge(dec_in, h * 16 + 48)
                act.wait_ge(lgh_ready, h + 1)
                for way in range(2):
                    nc.scalar.activation(dec[:, way, :], dec[:, way, :], ACT.Exp, scale=lgh[:, way:way + 1])\
                        .then_inc(exp_done, 1)
                for t in range(TILES0):
                    act.wait_ge(pe_step, step_of("heads", h, f"v{t}"))
                    nc.scalar.activation(v_hi[:, t, :], bank[t][:, :], ACT.Copy).then_inc(psum_hi, 1)
                split_hi("heads", h, 9, used_unit("heads", h, 7))
                for t in range(TILES0):
                    act.wait_ge(pe_step, step_of("heads", h, f"s{t}"))
                    nc.scalar.activation(scr[:, t, :], bank[[6, 7, 4, 5, 6, 7][t]][:, :], ACT.Copy)\
                        .then_inc(act_drain, 1)
                at = 0
                for n, w in enumerate(FWD_W):
                    act.wait_ge(stage_full, count("full", "heads", h, 4 + n))
                    stage_split("heads", h, 6 + n, pa_hi[:, at:at + w], w)
                    at += w
                    if n in (1, 3, 5):
                        k = 10 + n // 2
                        split_hi("heads", h, k, used_unit("heads", h, k - 2))
                split_hi("heads", h, 13, used_unit("heads", h, 11))
                for t in range(LAT):
                    act.wait_ge(pe_step, step_of("heads", h, f"gf{t}"))
                    nc.scalar.activation(gs[:, t, :], bank[t][:, :], ACT.Silu).then_inc(act_drain, 1)
                split_hi("heads", h, 14, used_unit("heads", h, 12))
                act.wait_ge(pe_step, step_of("heads", h, f"of{LAT - 1}"))
                at = 0
                for n, w in enumerate(BWD_W):
                    act.wait_ge(stage_full, count("full", "heads", h, 10 + n))
                    stage_split("heads", h, 12 + n, pa_hi[:, at:at + w], w)
                    at += w
                    if n in (1, 3):
                        k = 15 + n // 2
                        split_hi("heads", h, k, used_unit("heads", h, k - 2))
                split_hi("heads", h, 17, used_unit("heads", h, 15))
                for t in range(LAT):
                    act.wait_ge(pe_step, step_of("heads", h, f"gb{t}"))
                    act.wait_ge(*[dve_drain, drained("heads", h, f"of{t}")[1]])
                    nc.scalar.activation(gs[:, t, :], bank[t][:, :], ACT.Silu).then_inc(act_drain, 1)
                for t in range(LAT):
                    act.wait_ge(pe_step, step_of("heads", h, f"y{t}"))
                    nc.scalar.activation(act_hi1[:, :, t * P:(t + 1) * P],
                                         bank[4 + t][:, :].rearrange("p (a b) -> p a b", a=CH), ACT.Copy)\
                        .then_inc(psum_hi, 1)
                for k in range(18, 21):
                    split_hi("heads", h, k, used_unit("heads", h, k - 2))
            act.wait_ge(pe_step, before("step", "gate1b"))
            load_lnbc(2, lnbc1, 4)
            gates("gate1b")
            ln("ln1a", LAT)
            with nc.scalar.Fori(0, PIECES_F - 1) as p:
                ffn("ffn1", p, 1, TOKL, act_hi1)
            ffn("ffn1", PIECES_F - 1, 1, TOKL, act_hi1)
            act.wait_ge(res_base, BASE_RES["ln1a"] + LAT)
            load_lnbc(3, lnbc1, 6)

        @block.vector
        def _(dve):
            tt = nc.vector.tensor_tensor
            ts = nc.vector.tensor_scalar
            stt = nc.vector.scalar_tensor_tensor

            def f32(ap):
                return ap.bitcast(F32)

            def split_lo(phase, i, k):
                if isinstance(i, int) and count("units", phase, i, k) > TOTAL["units"]:
                    return
                dve.wait_ge(hi_done, count("units", phase, i, k))
                s, _ = unit_in(phase, i, k)
                w = slot(phase, k)
                tt(w_lo[:, w, :], raw[:, s, :], f32(w_hi[:, w, :]), ALU.subtract).then_inc(lo_done, 1)

            def stage_lo_part(phase, i, j, out, hi, width):
                q = BASE[phase]["stage"] + j
                dve.wait_ge(stage_hi, count("stage", phase, i, j))
                src = stage[:, q % 2, 0:width]
                if len(out.shape) == 3:
                    src = src.rearrange("p (a b) -> p a b", a=out.shape[1])
                tt(out, src, f32(hi), ALU.subtract).then_inc(stage_lo, 1)

            def stage_slot(phase, i, j, width):
                q = BASE[phase]["stage"] + j
                if isinstance(i, int) and count("stage", phase, i, j) < 3:
                    return stage[:, q % 2, 0:width]
                dve.wait_ge(stage_lo, count("stage", phase, i, j) - 2)
                return stage[:, q % 2, 0:width]

            def mod_columns(phase, i, g, b, n, out, bias):
                dve.wait_ge(pe_step, step_of(phase, i, f"cols{g}"))
                src = bank[b][:, 0:n * P].rearrange("p (j par b r) -> p par b j r", j=n, par=2, b=2)
                tt(out, src[:, 0, :, :, 0:2], bias.unsqueeze(3).to_broadcast([P, 2, n, 2]), ALU.add)\
                    .then_inc(mod_step, 1)
                dve.wait_ge(mod_step, before("mods", phase, i) + (g + 1))
                tt(out, out, src[:, 1, :, :, 0:2], ALU.add).then_inc(dve_drain, 1)

            def mod(layer, part):
                return modc[:, layer, 8 * part:8 * part + 8, :]

            cr = [0]

            def columns(phase, layer, shift, scale, ln_row):
                g = cols[:, LNC + 8 * ln_row:LNC + 8 * ln_row + 8].unsqueeze(2).to_broadcast([P, 8, 2])
                b = cols[:, LNC + 8 * ln_row + 8:LNC + 8 * ln_row + 16].unsqueeze(2).to_broadcast([P, 8, 2])
                ts(col1[:, :, :], mod(layer, scale), 1.0, None, ALU.add).then_inc(col_ready, 1)
                dve.wait_ge(col_ready, cr[0] + 1)
                tt(colS[:, :, :], col1[:, :, :], g, ALU.mult).then_inc(col_ready, 1)
                tt(colB[:, :, :], col1[:, :, :], b, ALU.mult).then_inc(col_ready, 1)
                dve.wait_ge(col_ready, cr[0] + 3)
                tt(colB[:, :, :], colB[:, :, :], mod(layer, shift), ALU.add).then_inc(col_ready, 1)
                cr[0] += 4

            dg = [0]

            def diagonals(phase, layer, part):
                n = len(STEPS[phase])
                dve.wait_ge(res_added, before("add", phase))
                for j in range(n):
                    v, half = j // 2, j % 2
                    if j >= 2:
                        dve.wait_ge(pe_step, step_of(phase, 0, f"gate{j - 2}"))
                    c = 8 * part + 4 * half
                    tt(gy[:, dg[0] % 2, :].rearrange("p (a b) -> p a b", a=4),
                       ident[:, :].unsqueeze(1).to_broadcast([P, 4, P]),
                       modc[:, layer, c:c + 4, v:v + 1].to_broadcast([P, 4, P]), ALU.mult).then_inc(diag_ready, 1)
                    dg[0] += 1

            def statistics(sources, s, done, at=0):
                for n, src in enumerate(sources):
                    last = nc.vector.bn_stats(out=bst[:, s, at + n, :], in_=src)
                last.then_inc(stat_step, 1)
                dve.wait_ge(stat_step, 2 * done + 1)
                if not isinstance(done, int):
                    dve.sem_inc(stat_seen, 1)
                nc.vector.bn_aggr(out=mv[:, s, :], in_=bst[:, s, 0:at + len(sources), :]).then_inc(stat_step, 1)
                dve.wait_ge(stat_step, 2 * done + 2)
                ts(veps[:, s:s + 1], mv[:, s, 1:2], EPS, None, ALU.add).then_inc(var_ready, 1)

            def ln_rows(phase, last_phase, tiles):
                def norm(t):
                    dve.wait_ge(rstd_ready, BASE_STAT[phase] + t + 1)
                    ts(res(t), res(t), mv[:, t, 0:1], rstd[:, t:t + 1], ALU.subtract, ALU.mult).then_inc(xn_ready, 1)

                n = 2 * tiles
                end = before("add", last_phase, TRIPS[last_phase])
                for t in range(tiles):
                    dve.wait_ge(res_added, end - tiles + t + 1)
                    statistics([res(t)[:, 0:512], res(t)[:, 512:1024]], t, BASE_STAT[phase] + t)
                    if t >= 1:
                        norm(t - 1)
                norm(tiles - 1)

            def ln_split(phase, tiles):
                for t in range(tiles):
                    for h in range(2):
                        at = (slice(None), slice(4 * h, 4 * h + 4), slice(t * P, (t + 1) * P))
                        stage_lo_part(phase, 0, 2 * t + h, hT_lo[at], hT_hi[at], 512)

            def drain_half(phase, i, half, tiles):
                for t in range(tiles):
                    e = BASE[phase]["add"] + half * tiles + t
                    dve.wait_ge(pe_step, step_of(phase, i, f"down{half}.{t}"))
                    if not (isinstance(i, int) and e + i * PER[phase]["add"] < 2):
                        dve.wait_ge(res_added, count("add", phase, i, half * tiles + t) - 2)
                    tt(gy[:, e % 2, :], bank[t][:, :], gate_of(t)[:, half * 512:(half + 1) * 512], ALU.mult)\
                        .then_inc(dve_drain, 1)

            def down(phase, i, k0, tiles, then=None):
                split_lo(phase, i, k0 + 1)
                split_lo(phase, i, k0 + 2)
                if then:
                    then()
                drain_half(phase, i, 0, tiles)
                split_lo(phase, i, k0 + 3)
                split_lo(phase, i, k0 + 4)
                drain_half(phase, i, 1, tiles)

            dve.wait_ge(lg_act, 1)
            ts(lg[:, 2, :], lg[:, 1, :], -1.0, 1.0, ALU.mult, ALU.add).then_inc(lg_dve, 1)
            dve.wait_ge(lg_dve, 1)
            ts(lg[:, 4, :], lg[:, 2, :], -1.0, 1.0, ALU.mult, ALU.add).then_inc(lg_dve, 1)
            dve.wait_ge(lg_dve, 2)
            ts(lg[:, 4, :], lg[:, 4, :], 1e-30, None, ALU.max).then_inc(lg_dve, 1)
            dve.wait_ge(lg_dve, 3)
            nc.vector.reciprocal(lg[:, 4, :], lg[:, 4, :]).then_inc(lg_dve, 1)
            dve.wait_ge(lg_dve, 4)
            tt(lg[:, 5, :], lg[:, 4, :], lg[:, 1, :], ALU.mult).then_inc(lg_dve, 1)
            dve.wait_ge(lg_dve, 5)
            dve.wait_ge(lg_act, 2)
            tt(lg[:, 5, :], lg[:, 5, :], lg[:, 3, :], ALU.mult).then_inc(lg_dve, 1)

            dve.wait_ge(const_in, N_CONST)
            def split_mods(g):
                m = modc[:, 0, 0:16, :].rearrange("p (b g j) v -> p g b j v", b=2, g=2)[:, g]
                bias = cols[:, ADAB:ADAB + 16].rearrange("p (b g j) -> p g b j", b=2, g=2)[:, g]
                mod_columns("v0", 0, g, 7, 4, m, bias)
                dve.wait_ge(dve_drain, drained("v0", 0, f"cols{g}")[1])
                ts(colS[:, 4 * g:4 * g + 4, :], mod(0, 1)[:, 4 * g:4 * g + 4, :], 1.0, None, ALU.add)\
                    .then_inc(vstat, 1)
                dve.wait_ge(vstat, g + 1)

            def h0(kcs):
                def low(j):
                    kc, v = j // 2, j % 2
                    a, b = (0, TOKL) if v == 0 else (TOKL, TOK0)
                    stage_lo_part("v0", 0, j, hT_lo[:, kc, a:b], hT_hi[:, kc, a:b], b - a)

                js = [2 * kc + v for kc in kcs for v in range(2)]
                for j in js:
                    kc, v = j // 2, j % 2
                    a, b = (0, TOKL) if v == 0 else (TOKL, TOK0)
                    dve.wait_ge(xT_in[kc // 2], 16)
                    ts(stage_slot("v0", 0, j, b - a), xT[:, kc, a:b], colS[:, kc, v:v + 1],
                       mod(0, 0)[:, kc, v:v + 1], ALU.mult, ALU.add).then_inc(stage_full, 1)
                    if j > js[0]:
                        low(j - 1)
                low(js[-1])

            split_mods(0)
            h0(range(2))
            split_lo("v0", 0, 0)
            h0(range(2, 4))
            split_lo("v0", 0, 1)
            split_mods(1)
            split_lo("v0", 0, 2)
            h0(range(4, 6))
            split_lo("v0", 0, 3)
            h0(range(6, 8))
            split_lo("v0", 0, 4)

            def mods_of(i, layer, c, n):
                return (modc[:, layer, bass.ds(c, n), :].rearrange("p (b j) v -> p b j v", b=2),
                        cols[:, bass.ds(c + (ADAB + 48 * layer), n)].rearrange("p (b j) -> p b j", b=2))

            def add_bias(phase, i, at):
                for t in range(TILES0):
                    dve.wait_ge(pe_step, step_of(phase, i, f"v{t}"))
                    tt(vtok[:, t, bass.ds(at, 512)], bank[t][:, :], bv[:, bass.ds(at, 512)], ALU.add)\
                        .then_inc(dve_drain, 1)

            dve.wait_ge(bv_in, 16)
            add_bias("v0", 0, 0)
            mod_columns("v0", 0, 2, 7, 4, *mods_of(0, 0, 16, 8))
            with nc.vector.Fori(0, 3) as i:
                split_lo("v", i, 1)
                split_lo("v", i, 2)
                for t in range(TILES0):
                    dve.wait_ge(gelu_done, i * TILES0 + (t + 1))
                    nc.vector.bn_stats(out=bst[:, t, bass.ds(i, 1), :].rearrange("p a b -> p (a b)"),
                                       in_=vtok[:, t, bass.ds(i * 512, 512)])
                split_lo("v", i, 3)
                split_lo("v", i, 4)
                add_bias("v", i, i * 512 + 512)
                mod_columns("v", i, 0, 7, 4, *mods_of(i, 0, i * 8 + 24, 8))
            dve.wait_ge(dve_drain, before("D", "gate0a"))
            diagonals("gate0a", 0, 2)
            for t in range(TILES0):
                dve.wait_ge(gelu_done, 3 * TILES0 + t + 1)
                statistics([vtok[:, t, 3 * 512:4 * 512]], t, t, 3)

            def normalise_v(p):
                for t in range(TILES0):
                    if p == 0:
                        dve.wait_ge(rstd_ready, t + 1)
                    c = vtok[:, t, p * 512:(p + 1) * 512]
                    ts(c, c, mv[:, t, 0:1], rstd[:, t:t + 1], ALU.subtract, ALU.mult).then_inc(xn_ready, 1)

            normalise_v(0)

            dve.wait_ge(act_drain, before("A", "gmlp"))
            dve.wait_ge(const_in, N_CONST + 32)
            for p in range(PIECES_A):
                for c in range(CH):
                    split_lo("gmlp", p, c + 1)
                    n = CH * p + c
                    g = n // 2
                    if c:
                        dve.wait_ge(dve_drain, drained("gmlp", p, f"s{c - 1}.1")[1])
                    stt(dcol[:, :], rowsum[:, g, :], cols[:, LNB + n:LNB + n + 1], bs[:, g, :], ALU.mult, ALU.add)\
                        .then_inc(gm_step, 1)
                    dve.wait_ge(gm_step, n + 1)
                    for h in range(2):
                        j = 2 * c + h
                        q = BASE["gmlp"]["stage"] + 8 * p + j
                        st = stage_slot("gmlp", p, j, HALF0)
                        dve.wait_ge(pe_step, step_of("gmlp", p, f"s{c}.{h}"))
                        st3 = st.rearrange("p (a b) -> p a b", a=3)
                        stt(st3, bank[4 + h][:, 0:HALF0].rearrange("p (a b) -> p a b", a=3),
                            cols[:, LNG + n:LNG + n + 1], dcol[:, :].unsqueeze(1).to_broadcast([P, 3, P]),
                            ALU.mult, ALU.add).then_inc(dve_drain, 1)
                        dve.wait_ge(dve_drain, drained("gmlp", p, f"s{c}.{h}")[1])
                        dve.wait_ge(act_drain, drained("gmlp", p, f"u{c}.{h}")[1])
                        tt(st, st, rbuf[:, q % 2, 0:HALF0], ALU.mult).then_inc(stage_full, 1)
                    for h in range(2):
                        at = (slice(None), c, slice(h * HALF0, (h + 1) * HALF0))
                        stage_lo_part("gmlp", p, 2 * c + h, act_lo0[at], act_hi0[at], HALF0)
                if p < PIECES_A - 1:
                    down("gmlp", p, CH, TILES0, lambda: normalise_v(p + 1))
                else:
                    down("gmlp", p, CH, TILES0)
            diagonals("gate0b", 0, 5)
            ln_rows("ln0a", "gmlp", TILES0)
            columns("ln0a", 0, 3, 4, 0)
            ln_split("ln0a", TILES0)

            def ffn(phase, i, groups, width, a_hi, a_lo, tiles):
                for c in range(CH):
                    split_lo(phase, i, c + 1)
                    for g in range(groups):
                        j = groups * c + g
                        q = BASE[phase]["stage"] + j
                        st = stage_slot(phase, i, j, width)
                        dve.wait_ge(act_drain, drained(phase, i, f"up{c}.{g}")[1])
                        r = rbuf[:, q % 2, 0:width]
                        tt(st, r, r, ALU.mult).then_inc(stage_full, 1)
                    for g in range(groups):
                        at = (slice(None), c, slice(g * width, (g + 1) * width))
                        stage_lo_part(phase, i, groups * c + g, a_lo[at], a_hi[at], width)
                if phase == "ffn0":
                    mod_columns(phase, i, 0, 5, 3, *mods_of(i, 1, i * 6, 6))
                down(phase, i, CH, tiles)

            dve.wait_ge(act_drain, before("A", "ffn0"))
            with nc.vector.Fori(0, PIECES_F) as p:
                ffn("ffn0", p, 2, HALF0, act_hi0, act_lo0, TILES0)
            dve.wait_ge(dve_drain, before("D", "gate1a"))
            diagonals("gate1a", 1, 2)
            dve.wait_ge(act_drain, before("A", "gate1a"))
            columns("ln0b", 1, 0, 1, 2)
            ln_rows("ln0b", "ffn0", TILES0)
            ln_split("ln0b", TILES0)

            dve.wait_ge(res_base, BASE_RES["ln0b"] + LAT)
            dve.wait_ge(act_drain, before("A", "heads"))
            dve.wait_ge(rope_in, 16)
            dve.wait_ge(dec_in, 32)
            dve.wait_ge(lg_dve, 6)
            with nc.vector.Fori(0, HEADS) as h:
                def rotate(r, a, b, scale, j, at_q):
                    t1, t2 = bank[a[1]][:, :], bank[b[1]][:, :]
                    cos, sin = rope[:, 0, :], rope[:, 1, :]
                    dve.wait_ge(pe_step, step_of("heads", h, b[0]))
                    stt(rbuf[:, 0, :], t1, scale, cos, ALU.mult, ALU.mult).then_inc(rope_step, 1)
                    stt(rbuf[:, 1, :], t2, scale, sin, ALU.mult, ALU.mult).then_inc(rope_step, 1)
                    dve.wait_ge(rope_step, h * 4 + (2 * r + 2))
                    st = stage_slot("heads", h, j, TOKL)
                    tt(st, rbuf[:, 0, :], rbuf[:, 1, :], ALU.subtract).then_inc(stage_full, 1)
                    dve.wait_ge(stage_full, count("full", "heads", h, at_q))
                    stt(rbuf[:, 0, :], t1, scale, sin, ALU.mult, ALU.mult).then_inc(dve_drain, 1)
                    stt(rbuf[:, 1, :], t2, scale, cos, ALU.mult, ALU.mult).then_inc(dve_drain, 1)
                    dve.wait_ge(dve_drain, drained("heads", h, b[0])[1])
                    st = stage_slot("heads", h, j + 1, TOKL)
                    tt(st, rbuf[:, 0, :], rbuf[:, 1, :], ALU.add).then_inc(stage_full, 1)

                nc.vector.tensor_copy(lgh[:, :].unsqueeze(2), lg[:, 5, :].rearrange("p (w h) -> p w h", w=2)
                                      [:, :, bass.ds(h, 1)]).then_inc(lgh_ready, 1)
                split_lo("heads", h, 1)
                split_lo("heads", h, 2)
                rotate(0, ("q0", 4), ("q1", 5), 1.0, 0, 0)
                for d in range(2):
                    stage_lo_part("heads", h, d, q_lo[:, d, :], q_hi[:, d, :], TOKL)
                split_lo("heads", h, 3)
                split_lo("heads", h, 4)
                rotate(1, ("k0", 6), ("k1", 7), DK ** -0.5, 2, 2)
                for d in range(2):
                    stage_lo_part("heads", h, 2 + d, k_lo[:, d, 0:TOKL], k_hi[:, d, 0:TOKL], TOKL)
                for d in range(2):
                    dve.wait_ge(pe_step, step_of("heads", h, f"kc{d}"))
                    ts(stage_slot("heads", h, 4 + d, CTX * P), bank[4 + d][:, 0:CTX * P], DK ** -0.5, None, ALU.mult)\
                        .then_inc(dve_drain, 1)
                for d in range(2):
                    stage_lo_part("heads", h, 4 + d, k_lo[:, d, TOKL:TOK0], k_hi[:, d, TOKL:TOK0], CTX * P)
                for k in range(5, 9):
                    split_lo("heads", h, k)
                for way, a in ((0, 0), (1, 768 - P)):
                    dve.wait_ge(exp_done, h * 2 + (way + 1))
                    tt(dec[:, way, a:a + P], dec[:, way, a:a + P], mask[:, way, :], ALU.mult).then_inc(mask_done, 1)
                for t in range(TILES0):
                    dve.wait_ge(psum_hi, h * 10 + (t + 1))
                    tt(v_lo[:, t, :], bank[t][:, :], f32(v_hi[:, t, :]), ALU.subtract).then_inc(dve_drain, 1)
                split_lo("heads", h, 9)

                def decayed(way, j0, full0, keys, splits):
                    at = 0
                    for n, (kt, a, m, w) in enumerate(keys):
                        st = stage_slot("heads", h, j0 + n, w)
                        if way == 0:
                            dve.wait_ge(act_drain, drained("heads", h, f"s{kt}")[1])
                        tt(st, scr[:, kt, a:a + w], dec[:, way, m:m + w], ALU.mult).then_inc(stage_full, 1)
                        stage_lo_part("heads", h, j0 + n, pa_lo[:, at:at + w], pa_hi[:, at:at + w], w)
                        at += w
                        if n in splits:
                            split_lo("heads", h, splits[n])

                dve.wait_ge(mask_done, h * 2 + 2)
                decayed(0, 6, 4, [(LAT, 0, 256, 512), (LAT + 1, 0, 128, 512)]
                        + [(kt, kt * P, 0, 512 - kt * P) for kt in range(LAT)], {1: 10, 3: 11, 5: 12})
                split_lo("heads", h, 13)
                for t in range(LAT):
                    dve.wait_ge(pe_step, step_of("heads", h, f"of{t}"))
                    statistics([bank[4 + t][:, :]], t, h * 8 + (BASE_STAT["heads"] + t))
                    dve.wait_ge(act_drain, drained("heads", h, f"gf{t}")[1])
                    stt(y[:, t, :], bank[4 + t][:, :], mv[:, t, 0:1], gs[:, t, :], ALU.subtract, ALU.mult)\
                        .then_inc(dve_drain, 1)
                    dve.wait_ge(rstd_ready, h * 8 + (BASE_STAT["heads"] + t + 1))
                    dve.wait_ge(dve_drain, drained("heads", h, f"of{t}")[1])
                    ts(y[:, t, :], y[:, t, :], rstd[:, t:t + 1], None, ALU.mult).then_inc(y_step, 1)
                split_lo("heads", h, 14)
                decayed(1, 12, 10, [(LAT, 0, 128, 512), (LAT + 1, 0, 0, 512)]
                        + [(kt, 0, 640 - kt * P, (kt + 1) * P) for kt in reversed(range(LAT))], {1: 15, 3: 16})
                for n, t in enumerate(reversed(range(LAT))):
                    dve.wait_ge(pe_step, step_of("heads", h, f"ob{t}"))
                    statistics([bank[4 + t][:, :]], 4 + t, h * 8 + (BASE_STAT["heads"] + LAT + n))
                    dve.wait_ge(act_drain, drained("heads", h, f"gb{t}")[1])
                    if n >= 2:
                        dve.wait_ge(y_step, h * 8 + (LAT + n - 1))
                    stt(rbuf[:, n % 2, :], bank[4 + t][:, :], mv[:, 4 + t, 0:1], gs[:, t, :], ALU.subtract, ALU.mult)\
                        .then_inc(dve_drain, 1)
                    dve.wait_ge(rstd_ready, h * 8 + (BASE_STAT["heads"] + LAT + n + 1))
                    dve.wait_ge(dve_drain, drained("heads", h, f"ob{t}")[1])
                    stt(y[:, t, :], rbuf[:, n % 2, :], rstd[:, 4 + t:5 + t], y[:, t, :], ALU.mult, ALU.add)\
                        .then_inc(y_step, 1)
                for t in range(LAT):
                    dve.wait_ge(psum_hi, h * 10 + (TILES0 + t + 1))
                    tt(act_lo1[:, :, t * P:(t + 1) * P], bank[4 + t][:, :].rearrange("p (a b) -> p a b", a=CH),
                       f32(act_hi1[:, :, t * P:(t + 1) * P]), ALU.subtract).then_inc(dve_drain, 1)
                down("heads", h, 16, LAT)
            diagonals("gate1b", 1, 5)
            columns("ln1a", 1, 3, 4, 4)
            ln_rows("ln1a", "heads", LAT)
            ln_split("ln1a", LAT)
            dve.wait_ge(act_drain, before("A", "ffn1"))
            with nc.vector.Fori(0, PIECES_F - 1) as p:
                ffn("ffn1", p, 1, TOKL, act_hi1, act_lo1, LAT)
            ffn("ffn1", PIECES_F - 1, 1, TOKL, act_hi1, act_lo1, LAT)
            ln_rows("ln1b", "ffn1", LAT)

        @block.gpsimd
        def _(pool):
            gt = nc.gpsimd.tensor_tensor

            def power(phase, i, n, s):
                done = BASE_STAT[phase] + n + 1
                if not isinstance(i, int) or i:
                    done = i * 8 + done
                pool.wait_ge(var_ready, done)
                gt(rstd[:, s:s + 1], veps[:, s:s + 1], mhalf[:, s:s + 1], ALU.pow).then_inc(rstd_ready, 1)

            def add(phase, i, tiles):
                for half in range(2):
                    for t in range(tiles):
                        j = half * tiles + t
                        e = BASE[phase]["add"] + j
                        pool.wait_ge(dve_drain, drained(phase, i, f"down{half}.{t}")[1])
                        if e >= 2 * tiles or not isinstance(i, int):
                            pool.wait_ge(res_added, count("add", phase, i, j) - 2 * tiles)
                        r = res(t)[:, half * 512:(half + 1) * 512]
                        gt(r, r, gy[:, e % 2, :], ALU.add).then_inc(res_added, 1)

            def ln(phase, k, lnbc, tiles, scale):
                pool.wait_ge(lnbc_in, 32 * (k + 1))
                if scale:
                    nc.gpsimd.tensor_scalar(lnbc[:, :, :], lnbc[:, :, :], ALPHA, None, ALU.mult)\
                        .then_inc(lnbc_scaled, 1)
                    pool.wait_ge(lnbc_scaled, k + 1)
                for t in range(tiles):
                    if scale:
                        pool.wait_ge(pe_step, step_of(phase, 0, f"ln{t}.1"))
                    else:
                        pool.wait_ge(xn_ready, XN_BASE[phase] + t + 1)
                    gt(res(t), res(t), lnbc[:, 0, :], ALU.mult).then_inc(res_mul, 1)
                    pool.wait_ge(res_mul, BASE_RES[phase] - TILES0 + t + 1)
                    gt(res(t), res(t), lnbc[:, 1, :], ALU.add).then_inc(res_base, 1)

            nc.gpsimd.memset(scT[:, :, :], 0.0).then_inc(sc_zero, 1)
            nc.gpsimd.memset(ones[:, :], 1.0).then_inc(pool_const, 1)
            nc.gpsimd.memset(mhalf[:, :], -0.5).then_inc(pool_const, 1)
            pool.wait_ge(res_in, 32)
            for t in range(TILES0):
                nc.gpsimd.tensor_scalar(res(t), res(t), ALPHA, None, ALU.mult).then_inc(res_base, 1)
            pool.wait_ge(pool_const, 2)
            for t in range(TILES0):
                power("v", 0, t, t)
            pool.wait_ge(res_base, BASE_RES["ln0a"])
            for p in range(PIECES_A):
                add("gmlp", p, TILES0)
            for t in range(TILES0):
                power("ln0a", 0, t, t)
            ln("ln0a", 0, lnbc0, TILES0, True)
            pool.wait_ge(res_base, BASE_RES["ln0b"])
            with nc.gpsimd.Fori(0, PIECES_F) as p:
                add("ffn0", p, TILES0)
            for t in range(TILES0):
                power("ln0b", 0, t, t)
            ln("ln0b", 1, lnbc0, LAT, True)
            pool.wait_ge(res_base, BASE_RES["ln1a"])
            with nc.gpsimd.Fori(0, HEADS) as h:
                for t in range(LAT):
                    power("heads", h, t, t)
                for n, t in enumerate(reversed(range(LAT))):
                    power("heads", h, LAT + n, 4 + t)
                add("heads", h, LAT)
            for t in range(LAT):
                power("ln1a", 0, t, t)
            ln("ln1a", 2, lnbc1, LAT, True)
            pool.wait_ge(res_base, BASE_RES["ln1b"])
            with nc.gpsimd.Fori(0, PIECES_F) as p:
                add("ffn1", p, LAT)
            for t in range(LAT):
                power("ln1b", 0, t, t)
            ln("ln1b", 3, lnbc1, LAT, False)


def kernel(**inputs):
    import numpy as _np
    import concourse.bacc as _bacc
    from concourse import mybir as _mybir
    from concourse.bass_utils import run_bass_kernel_spmd as _run

    a = {k: _np.asarray(v) for k, v in inputs.items()}

    def feature_units(w):
        return w.reshape(KC, P, -1, P).transpose(2, 1, 0, 3).reshape(-1, P, UNIT)

    def token_units(w):
        return w.reshape(w.shape[0] // 256, 2, P, -1, 512).transpose(3, 0, 2, 1, 4).reshape(-1, P, UNIT)

    def mod_units(w, wide):
        return w.reshape(KC, P, -1, wide).transpose(2, 0, 1, 3).reshape(-1, P, wide)

    def ffn_units(w1, w2):
        for p in range(PIECES_F):
            yield feature_units(w1[:, p * 512:(p + 1) * 512])
            yield token_units(w2[p * 512:(p + 1) * 512])

    def units():
        w_in, w_out = a["a_w_in"][0], a["a_w_out"][0]
        yield token_units(w_in[:, 2048:])
        for p in range(PIECES_A):
            yield feature_units(w_in[:, p * 512:(p + 1) * 512])
            yield token_units(w_out[p * 512:(p + 1) * 512])
        yield from ffn_units(a["ffn_w1"][0], a["ffn_w2"][0])
        w_in, w_out = a["b_w_in"][0], a["b_w_out"][0]
        for h in range(HEADS):
            yield feature_units(w_in[:, h * DK:(h + 1) * DK])
            yield feature_units(w_in[:, 1024 + h * DK:1024 + (h + 1) * DK])
            for part in range(3):
                at = 2048 * (part + 1) + h * DV
                yield token_units(w_in[:, at:at + DV])
            yield token_units(w_out[h * DV:(h + 1) * DV])
        yield from ffn_units(a["ffn_w1"][1], a["ffn_w2"][1])

    def columns(v):
        return v.reshape(-1, P).T

    lns = [a[f"ln{n}_{x}"][l] for l in range(DEPTH) for n in (1, 2) for x in "gb"]
    t = _np.arange(TOKL)
    inv = (_np.float32(10000.0) ** (-_np.arange(DK // 4, dtype=_np.float32) / _np.float32(DK // 4)))
    ang = _np.concatenate([inv[:, None] * (t // 64).astype(_np.float32), inv[:, None] * (t % 64).astype(_np.float32)])
    rope = _np.stack([_np.cos(ang), _np.sin(ang)], 1).astype(_np.float32)
    j, m = _np.arange(P)[:, None], _np.arange(768)[None]
    dist = _np.stack([_np.maximum(m - j, 0), _np.maximum(640 + j - m, 0)], 1).astype(_np.float32)
    small = _np.concatenate([_np.eye(P), m[:, :P] >= j, j >= m[:, :P]], 1).astype(_np.float32)
    arrays = {
        "w_units": _np.concatenate(list(units())),
        "mod0_units": _np.concatenate([mod_units(a["ada_w"][0][:, :2048].reshape(D, 2, 2, 512)
                                                 .transpose(0, 2, 1, 3).reshape(D, 2048), WIDE_M0),
                                       mod_units(a["ada_w"][0][:, 2048:], WIDE_M0)]),
        "mod1_units": mod_units(a["ada_w"][1], WIDE_M1),
        "xT": _np.concatenate([a["x"][0], a["ctx"][0]]).T.reshape(KC, P, TOK0).transpose(1, 0, 2),
        "x": a["x"][0],
        "ctx": a["ctx"][0],
        "cols": _np.concatenate([columns(a["ada_b"])] + [columns(v) for v in lns]
                                + [columns(a["a_b_in"][0, :2048]), columns(a["a_ln_g"][0]), columns(a["a_ln_b"][0])], 1),
        "cvec": _np.stack([columns(a["c"][0]), columns(a["c_ctx"])], 2),
        "wsT": a["a_w_s"][0].transpose(2, 0, 1),
        "bs": a["a_b_s"][0].reshape(-1),
        "bv": a["a_b_in"][0, 2048:],
        "ln": _np.stack(lns),
        "decay": a["b_decay"][0].reshape(-1),
        "dist": dist,
        "rope": rope,
        "small": small,
    }
    nc = _bacc.Bacc("TRN2", target_bir_lowering=False, num_devices=1, dynamic_dma_scratch_size=1024)
    args, feeds = [], {}
    for name, v in arrays.items():
        feeds[name + "_d"] = _np.ascontiguousarray(v)
        args.append(nc.dram_tensor(name + "_d", v.shape, _mybir.dt.float32, kind="ExternalInput").ap())
    out = nc.dram_tensor("out_d", (TOKL, D), _mybir.dt.float32, kind="ExternalOutput").ap()
    build(nc, *args, out)
    r = _run(nc, [feeds], core_ids=[0])
    return r.results[0]["out_d"].reshape(1, TOKL, D)
```

```python
import math
from contextlib import ExitStack

import concourse.bass as bass
from concourse import mybir

F32 = mybir.dt.float32
F32R = mybir.dt.float32r
ACT = mybir.ActivationFunctionType
ALU = mybir.AluOpType

P = 128
D = 1024
KC = D // P
LAT, CTX = 4, 2
TILES0 = LAT + CTX
TOK0 = TILES0 * P
TOKL = LAT * P
HALF0 = TOK0 // 2
DEPTH = 2
ALPHA = (2 * DEPTH) ** 0.25
EPS = 1e-5
HEADS, DK, DV = 4, 256, 512
CH = 4
PIECES_A = 2048 // 512
PIECES_F = 4096 // 512
UNIT = 1024
RAW, SPL = 4, 2
SLOTS_M0, SLOTS_M1 = 8, 4
WIDE_M0, WIDE_M1 = 1024, 6 * D // (4096 // 512)



def _down(tiles, unit):
    out = []
    for half in range(2):
        out.append((f"unit{unit + 2 * half}", None, None))
        out += [(f"down{half}.{t}", t, "D") for t in range(tiles)]
    return out


def _mod(group, units, rows=None):
    return [(f"rows{group}", rows, "A") if n == KC - 1 else (f"mod{group}.{n}", None, None) for n in units]


def _tokens(name, tiles, unit):
    return [(f"unit{unit + q}", None, None) for q in range(3)] + [(f"{name}{t}", t, {"v": "D"}.get(name, "A"))
                                                                  for t in range(tiles)]


LN_GROUPS = {TILES0: [(0, LAT), (LAT, TILES0)], LAT: [(0, 2), (2, LAT)]}


GATE_BANKS = [6, 7, 0, 1]


def ln_at(tiles, g, kc):
    t0, t1 = LN_GROUPS[tiles][g]
    if t1 - t0 == 4:
        return 2 + kc % 4, 0
    return ([2, 3, 4, 5], [6, 7, 0, 1])[g][kc // 2], kc % 2 * 2 * P


def _ln(tiles, gates):
    out = [(f"gate{j}", GATE_BANKS[j], "A") for j in range(gates)]
    return out + [(f"ln{g}.{kc}", ln_at(tiles, g, kc)[0], "AD"[kc % 2]) for g in range(2) for kc in range(KC)]


_V0 = _mod(0, range(8), 6) + [("cols0", 7, "D")]
_V0 += _mod(1, range(4)) + [("unit0", None, None)] + _mod(1, range(4, 8), 6) + [("cols1", 7, "D")]
_V0 += [("unit1", None, None), ("unit2", None, None)] + _mod(2, range(4)) + [(f"v{t}", t, "D") for t in range(3)]
_V0 += _mod(2, range(4, 8), 6) + [(f"v{t}", t, "D") for t in range(3, 6)] + [("cols2", 7, "D")]
_V = [("unit0", None, None)] + _mod(0, range(2)) + [("unit1", None, None)] + _mod(0, range(2, 4))
_V += [("unit2", None, None)] + _mod(0, range(4, 8), 6) + [(f"v{t}", t, "D") for t in range(6)] + [("cols0", 7, "D")]
_GMLP = []
for _c in range(CH):
    _GMLP += [(f"u{_c}.0", 6, "A"), (f"u{_c}.1", 7, "A"), (f"s{_c}.0", 4, "D"), (f"s{_c}.1", 5, "D")]
_UP0 = [[(f"up{c}.{g}", 6 + g, "A") for g in range(2)] for c in range(CH)]
_FFN0 = _UP0[0] + _mod(0, range(3)) + _UP0[1] + _mod(0, range(3, 6)) + _UP0[2] + _mod(0, range(6, 8), 4) + _UP0[3]
_FFN0 += [("cols0", 5, "D")]
_FFN1 = [(f"up{c}.0", 4 + c, "A") for c in range(CH)]
_HEAD = [("q0", 4, "D"), ("q1", 5, "D"), ("k0", 6, "D"), ("kc0", 2, "D"), ("k1", 7, "D"), ("kc1", 3, "D")]
_HEAD += _tokens("v", TILES0, 4)
_HEAD += [(f"s{t}", [6, 7, 4, 5, 6, 7][t], "A") for t in range(TILES0)]
_HEAD += _tokens("gf", LAT, 8) + [(f"of{t}", 4 + t, "D") for t in range(LAT)]
_HEAD += _tokens("gb", LAT, 12) + [("ob3", 7, "D"), ("ob2", 6, "D"), ("ob1", 5, "D"), ("y3", 7, "D"), ("ob0", 4, "D")]
_HEAD += [(f"y{t}", 4 + t, "D") for t in (2, 1, 0)]

PHASES = [
    ("v0", 1, _V0, dict(units=4, stage=2 * KC, full=2 * KC, mods=3)),
    ("v", 3, _V, dict(units=4, mods=1)),
    ("gate0a", 1, [(f"gate{j}", j, "A") for j in range(4)], {}),
    ("rowsum", 1, [("rs0", 4, "A"), ("rs1", 5, "A")], {}),
    ("gmlp", PIECES_A, _GMLP + _down(TILES0, 4), dict(units=8, stage=2 * CH, full=2 * CH, add=2 * TILES0)),
    ("ln0a", 1, _ln(TILES0, 4), dict(stage=2 * KC)),
    ("ffn0", PIECES_F, _FFN0 + _down(TILES0, 4), dict(units=8, stage=2 * CH, full=2 * CH, add=2 * TILES0,
                                                     mods=1)),
    ("ln0b", 1, _ln(TILES0, 2), dict(stage=2 * KC)),
    ("heads", HEADS, _HEAD + _down(LAT, 16), dict(units=20, stage=18, full=16, add=2 * LAT)),
    ("ln1a", 1, _ln(LAT, 2), dict(stage=2 * KC)),
    ("ffn1", PIECES_F, _FFN1 + _down(LAT, 4), dict(units=8, stage=CH, full=CH, add=2 * LAT)),
    ("ln1b", 1, [], {}),
]
ORDER = [p[0] for p in PHASES]
TRIPS = {p[0]: p[1] for p in PHASES}
STEPS = {p[0]: p[2] for p in PHASES}
PER = {}
for _n, _t, _s, _k in PHASES:
    PER[_n] = dict(step=len(_s), A=sum(s[2] == "A" for s in _s), D=sum(s[2] == "D" for s in _s), units=0, mods=0,
                   stage=0, full=0, add=0)
    PER[_n].update(_k)
BASE = {}
_sum = dict.fromkeys(PER["v"], 0)
for _n in ORDER:
    BASE[_n] = dict(_sum)
    for _k in _sum:
        _sum[_k] += TRIPS[_n] * PER[_n][_k]
TOTAL = _sum


def count(kind, phase, i, j):
    return i * PER[phase][kind] + (BASE[phase][kind] + j + 1)


def before(kind, phase, i=0):
    return i * PER[phase][kind] + BASE[phase][kind]


def step_of(phase, i, label):
    return count("step", phase, i, [s[0] for s in STEPS[phase]].index(label))


def drained(phase, i, label):
    steps = STEPS[phase]
    at = [s[0] for s in steps].index(label)
    who = steps[at][2]
    mine = [s[0] for s in steps if s[2] == who]
    if label in ("k0", "k1", "kc0", "kc1"):
        return who, count(who, phase, i, 2 + ("kc0", "kc1", "k0", "k1").index(label))
    return who, count(who, phase, i, mine.index(label))


def occupants(phase, i, label):
    steps = STEPS[phase]
    at = [s[0] for s in steps].index(label)
    bank = steps[at][1]
    for s in reversed(steps[:at]):
        if s[1] == bank and not (label[:2] == s[0][:2] == "ln" and s is steps[at - 1]):
            return [drained(phase, i, s[0])]
    found = []
    if not (isinstance(i, int) and i == 0):
        same = [s for s in steps if s[1] == bank][-1]
        who, value = drained(phase, i, same[0])
        found.append((who, value - PER[phase][who]))
        if isinstance(i, int):
            return found
    for p in reversed(ORDER[:ORDER.index(phase)]):
        same = [s for s in STEPS[p] if s[1] == bank]
        if same:
            found.append(drained(p, TRIPS[p] - 1, same[-1][0]))
            break
    return found


def build(nc, w_units, mod0_units, mod1_units, xT_d, x_d, ctx_d, cols_d, cvec_d, wsT_d, bs_d, bv_d, ln_d, decay_d, dist_d, rope_d,
          small_d, out_d):
    keep = ExitStack()
    with keep:
        def sem(name):
            return keep.enter_context(nc.semaphore(name))

        def sb(name, shape, dt=F32, scope=keep):
            return scope.enter_context(nc.sbuf_tensor(name, shape, dt))

        hT_hi = sb("hT_hi", [P, KC, TOK0], F32R)
        hT_lo = sb("hT_lo", [P, KC, TOK0], F32R)
        raw = sb("raw", [P, RAW, UNIT])
        w_hi = sb("w_hi", [P, SPL, UNIT], F32R)
        w_lo = sb("w_lo", [P, SPL, UNIT], F32R)
        res_lat = sb("res_lat", [P, LAT, D])
        gate_lat = sb("gate_lat", [P, D])
        stage = sb("stage", [P, 2, 512])
        rbuf = sb("rbuf", [P, 2, 512])
        gy = sb("gy", [P, 2, 512])
        ident = sb("ident", [P, P])
        ones = sb("ones", [P, P])
        mask = sb("mask", [P, 2, P])
        NCOL = cols_d.shape[1]
        cols = sb("cols", [P, NCOL])
        scT = sb("scT", [P, KC, 32])
        cvec = sb("cvec", [P, KC, 2])
        modc = sb("modc", [P, DEPTH, 48, 2])
        colS = sb("colS", [P, KC, 2])
        colB = sb("colB", [P, KC, 2])
        colS1 = sb("colS1", [P, KC, 2])
        colB1 = sb("colB1", [P, KC, 2])
        col1 = sb("col1", [P, KC, 2])
        dcol = sb("dcol", [P, P])
        bst = sb("bst", [P, 8, 4, 6])
        mv = sb("mv", [P, 8, 2])
        veps = sb("veps", [P, 8])
        rstd = sb("rstd", [P, 8])
        nbias = sb("nbias", [P, 8])
        mhalf = sb("mhalf", [P, 8])
        lg = sb("lg", [P, 6, 8])
        lgh = sb("lgh", [P, 2])
        ADAB, LNC, BU, LNG, LNB = 0, 96, 160, 176, 192

        layer0 = ExitStack()
        res_ctx = sb("res_ctx", [P, CTX, D], scope=layer0)
        gate_ctx = sb("gate_ctx", [P, D], scope=layer0)
        in_v = ExitStack()
        mod0 = sb("mod0", [P, SLOTS_M0, WIDE_M0], scope=in_v)
        in_v.close()
        act_hi0 = sb("act_hi0", [P, CH, TOK0], F32R, layer0)
        act_lo0 = sb("act_lo0", [P, CH, TOK0], F32R, layer0)
        in_gmlp = ExitStack()
        wsT = sb("wsT", [P, 8, P], scope=in_gmlp)
        rowsum = sb("rowsum", [P, 8, P], scope=in_gmlp)
        bs = sb("bs", [P, 8, P], scope=in_gmlp)
        bv = sb("bv", [P, 2048], scope=in_gmlp)
        at_start = ExitStack()
        xT = sb("xT", [P, KC, TOK0], scope=at_start)
        at_start.close()
        vtok = sb("vtok", [P, TILES0, 2048], scope=in_gmlp)
        in_gmlp.close()
        in_ffn0 = ExitStack()
        pad0 = sb("pad0", [P, 5120], scope=in_ffn0)
        mod1 = sb("mod1", [P, SLOTS_M1, WIDE_M1], scope=in_ffn0)
        rows1 = sb("rows1", [P, WIDE_M1 // 2], scope=in_ffn0)
        pad1 = sb("pad1", [P, 1440], scope=in_ffn0)
        lnbc0 = sb("lnbc0", [P, 2, D], scope=in_ffn0)
        in_ffn0.close()
        layer0.close()

        layer1 = ExitStack()
        PW = 2 * 512 + (512 + 384 + 256 + 128)
        pa_hi = sb("pa_hi", [P, PW], F32R, layer1)
        pa_lo = sb("pa_lo", [P, PW], F32R, layer1)
        act_hi1 = pa_hi[:, 0:CH * 512].rearrange("p (c t) -> p c t", c=CH)
        act_lo1 = pa_lo[:, 0:CH * 512].rearrange("p (c t) -> p c t", c=CH)
        in_heads = ExitStack()
        v_hi = sb("v_hi", [P, TILES0, DV], F32R, in_heads)
        v_lo = sb("v_lo", [P, TILES0, DV], F32R, in_heads)
        q_hi = sb("q_hi", [P, 2, TOKL], F32R, in_heads)
        q_lo = sb("q_lo", [P, 2, TOKL], F32R, in_heads)
        k_hi = sb("k_hi", [P, 2, TOK0], F32R, in_heads)
        k_lo = sb("k_lo", [P, 2, TOK0], F32R, in_heads)
        scr = sb("scr", [P, TILES0, TOKL], scope=in_heads)
        gs = sb("gs", [P, LAT, DV], scope=in_heads)
        y = sb("y", [P, LAT, DV], scope=in_heads)
        dec = sb("dec", [P, 2, 768], scope=in_heads)
        rope = sb("rope", [P, 2, TOKL], scope=in_heads)
        in_heads.close()
        lnbc1 = sb("lnbc1", [P, 2, D], scope=layer1)
        layer1.close()

        bank = [keep.enter_context(nc.psum_tensor(f"bank{b}", [P, 512], F32)) for b in range(8)]

        w_in = [sem(f"w_in{s}") for s in range(RAW)]
        mod0_in = [sem(f"mod0_in{s}") for s in range(SLOTS_M0)]
        mod1_in = [sem(f"mod1_in{s}") for s in range(SLOTS_M1)]
        const_in = sem("const_in")
        cvec_in = sem("cvec_in")
        rope_in = sem("rope_in")
        xT_in = [sem(f"xT_in{s}") for s in range(4)]
        res_in = sem("res_in")
        bv_in = sem("bv_in")
        lnbc_in = sem("lnbc_in")
        dec_in = sem("dec_in")
        out_done = sem("out_done")
        hi_done = sem("hi_done")
        lo_done = sem("lo_done")
        pe_step = sem("pe_step")
        act_drain = sem("act_drain")
        dve_drain = sem("dve_drain")
        stage_full = sem("stage_full")
        stage_hi = sem("stage_hi")
        stage_lo = sem("stage_lo")
        sc_zero = sem("sc_zero")
        sc_ready = sem("sc_ready")
        col_ready = sem("col_ready")
        diag_ready = sem("diag_ready")
        gelu_done = sem("gelu_done")
        vstat = sem("vstat")
        gm_step = sem("gm_step")
        stat_step = sem("stat_step")
        stat_seen = sem("stat_seen")
        var_ready = sem("var_ready")
        rstd_ready = sem("rstd_ready")
        xn_ready = sem("xn_ready")
        xn_last = sem("xn_last")
        nbias_ready = sem("nbias_ready")
        res_mul = sem("res_mul")
        res_base = sem("res_base")
        res_added = sem("res_added")
        lnbc_scaled = sem("lnbc_scaled")
        psum_hi = sem("psum_hi")
        rope_step = sem("rope_step")
        y_step = sem("y_step")
        exp_done = sem("exp_done")
        mask_done = sem("mask_done")
        lgh_ready = sem("lgh_ready")
        lg_dve = sem("lg_dve")
        lg_act = sem("lg_act")
        pool_const = sem("pool_const")
        end_step = sem("end_step")
        out_ready = sem("out_ready")
        mod_step = sem("mod_step")

        COLS = {"ln0a": (colS, colB), "ln0b": (colS, colB), "ln1a": (colS1, colB1)}
        DIAG = [stage[:, 0, :], stage[:, 1, :], rbuf[:, 0, :], rbuf[:, 1, :]]
        DRAIN = {"A": act_drain, "D": dve_drain}
        N_CONST = 16 * 2

        def res(t):
            return res_lat[:, t, :] if t < LAT else res_ctx[:, t - LAT, :]

        def gate_of(t):
            return gate_lat if t < LAT else gate_ctx

        def unit_in(phase, i, k):
            u = BASE[phase]["units"] + k
            return u % RAW, 16 * (u // RAW + 1) + i * (16 * PER[phase]["units"] // RAW)

        def slot(phase, k):
            return (BASE[phase]["units"] + k) % SPL

        MOD_UNITS = {0: (mod0, mod0_in, SLOTS_M0, WIDE_M0), 1: (mod1, mod1_in, SLOTS_M1, WIDE_M1)}

        def groups_before(phase, i, g):
            return before("mods", phase, i) + (g - (BASE["ffn0"]["mods"] if phase == "ffn0" else 0))

        def mod_done(phase, i, g, n):
            return step_of(phase, i, f"rows{g}" if n == KC - 1 else f"mod{g}.{n}")

        BASE_RES = {"start": 0, "ln0a": TILES0, "ln0b": 2 * TILES0, "ln1a": 2 * TILES0 + LAT,
                    "ln1b": 2 * TILES0 + 2 * LAT}
        BASE_STAT = {"v": 0, "ln0a": TILES0, "ln0b": 2 * TILES0, "heads": 3 * TILES0,
                     "ln1a": 3 * TILES0 + 8 * HEADS, "ln1b": 3 * TILES0 + 8 * HEADS + LAT}

        FWD_AT = [1024, 1536, 1920, 2176]
        BWD_AT = [1536, 2048, 1664, 1024]
        XN_V = PIECES_A * TILES0
        XN_BASE = {"ln0a": XN_V, "ln0b": XN_V + 4, "ln1a": XN_V + 8, "ln1b": XN_V + 10}
        NB_BASE = {"ln0a": 0, "ln0b": 4, "ln1a": 8}
        XL_BASE = {"ln0a": 0, "ln0b": 2, "ln1a": 4}

        FWD_W = [512, 512, 512, 384, 256, 128]
        BWD_W = [512, 512, 512, 384, 256, 128]
        COL_READY = {"ln0a": 4, "ln0b": 8, "ln1a": 12}
        UNIT_END = {
            "v0": ["unit0", "unit1", "unit2", f"v{TILES0 - 1}"],
            "v": ["unit0", "unit1", "unit2", f"v{TILES0 - 1}"],
            "gmlp": [f"u{c}.1" for c in range(CH)] + ["unit4", f"down0.{TILES0 - 1}", "unit6", f"down1.{TILES0 - 1}"],
            "ffn0": [f"up{c}.1" for c in range(CH)] + ["unit4", f"down0.{TILES0 - 1}", "unit6", f"down1.{TILES0 - 1}"],
            "ffn1": [f"up{c}.0" for c in range(CH)] + ["unit4", f"down0.{LAT - 1}", "unit6", f"down1.{LAT - 1}"],
            "heads": ["q0", "q1", "kc0", "kc1", "unit4", "unit5", "unit6", f"v{TILES0 - 1}", "unit8", "unit9",
                      "unit10", f"gf{LAT - 1}", "unit12", "unit13", "unit14", f"gb{LAT - 1}", "unit16",
                      f"down0.{LAT - 1}", "unit18", f"down1.{LAT - 1}"],
        }


        block = keep.enter_context(nc.Block())

        @block.sync
        def _(sp):
            def weights(u, i=0, per=0):
                if u >= RAW:
                    sp.wait_ge(lo_done, i * per + (u - RAW + 1))
                sp.dma_start(raw[:, u % RAW, :], w_units[i * per + u]).then_inc(w_in[u % RAW], 16)

            def mods0(n, used=None, i=0):
                if used is not None:
                    sp.wait_ge(pe_step, used)
                s = n % SLOTS_M0
                sp.dma_start(mod0[:, s, :], mod0_units[i * SLOTS_M0 + n]).then_inc(mod0_in[s], 16)

            def mods1(n, used=None, i=0):
                if used is not None:
                    sp.wait_ge(pe_step, used)
                s = n % SLOTS_M1
                sp.dma_start(mod1[:, s, :], mod1_units[i * KC + n]).then_inc(mod1_in[s], 16)

            def load_lnbc(dst, row):
                sp.dma_start(dst[:, 0, :], ln_d[row, :].partition_broadcast(P)).then_inc(lnbc_in, 16)
                sp.dma_start(dst[:, 1, :], ln_d[row + 1, :].partition_broadcast(P)).then_inc(lnbc_in, 16)

            def load_xT(q):
                sp.dma_start(xT[:, 2 * q:2 * q + 2, :], xT_d[:, 2 * q:2 * q + 2, :]).then_inc(xT_in[q], 16)

            sp.dma_start(cvec[:, :, :], cvec_d).then_inc(cvec_in, 16)
            for n in range(KC):
                mods0(n)
                if n == 1:
                    sp.dma_start(ident[:, :], small_d[:, 0:P]).then_inc(const_in, 16)
                    sp.dma_start(cols[:, :], cols_d).then_inc(const_in, 16)
                if n == 5:
                    load_xT(0)
            weights(0)
            for n in range(4):
                mods0(KC + n, mod_done("v0", 0, 0, n))
            load_xT(1)
            weights(1)
            for n in range(4, KC):
                mods0(KC + n, mod_done("v0", 0, 0, n))
            load_xT(2)
            weights(2)
            load_xT(3)
            weights(3)
            sp.dma_start(bv[:, :], bv_d.partition_broadcast(P)).then_inc(bv_in, 16)
            for n in range(KC):
                mods0(2 * KC + n, mod_done("v0", 0, 1, n))
            for k in range(4):
                weights(4 + k)
                for n in (2 * k, 2 * k + 1):
                    mods0(3 * KC + n, mod_done("v0", 0, 2, n))
            sp.dma_start(res_lat[:, :, :], x_d.rearrange("(t p) d -> p t d", p=P)).then_inc(res_in, 16)
            sp.dma_start(res_ctx[:, :, :], ctx_d.rearrange("(t p) d -> p t d", p=P)).then_inc(res_in, 16)
            with nc.sync.Fori(0, 2) as i:
                for k in range(4):
                    weights(8 + k, i, 4)
                    for n in (2 * k, 2 * k + 1):
                        mods0(4 * KC + n, mod_done("v", i, 0, n), i)
            at = BASE["gmlp"]["units"]
            for k in range(4):
                weights(at + k)
            sp.wait_ge(pe_step, step_of("v", 2, "rows0"))
            sp.dma_start(wsT[:, :, :], wsT_d).then_inc(const_in, 16)
            sp.dma_start(bs[:, :, :], bs_d.partition_broadcast(P).rearrange("p (a b) -> p a b", a=8))\
               .then_inc(const_in, 16)
            with nc.sync.Fori(0, PIECES_A - 1) as i:
                for k in range(8):
                    weights(at + RAW + k, i, 8)
            at = BASE["ffn0"]["units"]
            for u in range(at - RAW, at):
                weights(u)
            sp.wait_ge(pe_step, step_of("gmlp", PIECES_A - 1, "s3.1"))
            load_lnbc(lnbc0, 0)
            for n in range(SLOTS_M1):
                mods1(n)
                weights(at + n)
            at += RAW

            def piece(i, units):
                for k in range(8):
                    weights(at + k, i, 8)
                    for n in {1: (0, 1, 2), 2: (3, 4, 5), 3: (6, 7)}.get(k, ()):
                        if n < units:
                            mods1(SLOTS_M1 + n, mod_done("ffn0", i, 0, n), i)

            with nc.sync.Fori(0, PIECES_F - 1) as i:
                piece(i, KC)
            sp.wait_ge(res_base, BASE_RES["ln0a"] + TILES0)
            load_lnbc(lnbc0, 2)
            sp.dma_start(rope[:, :, :], rope_d).then_inc(rope_in, 16)
            piece(PIECES_F - 1, KC - SLOTS_M1)

            def weights_from(first, n):
                with nc.sync.Fori(0, n // RAW) as i:
                    for k in range(RAW):
                        weights(first + k, i, RAW)
                for k in range(n // RAW * RAW, n):
                    weights(first + k)

            at = BASE["ffn1"]["units"] + 2
            weights_from(BASE["heads"]["units"] + RAW, at - BASE["heads"]["units"] - RAW)
            sp.wait_ge(pe_step, step_of("heads", HEADS - 1, "ob0"))
            load_lnbc(lnbc1, 4)
            weights_from(at, TOTAL["units"] - 16 - at)
            sp.wait_ge(res_base, BASE_RES["ln1a"] + LAT)
            load_lnbc(lnbc1, 6)
            weights_from(TOTAL["units"] - 16, 16)
            for t in (1, 2, 0, 3):
                if t:
                    sp.wait_ge(out_ready, t)
                else:
                    sp.wait_ge(res_base, BASE_RES["ln1b"] + 1)
                sp.dma_start(out_d[t * P:(t + 1) * P, :], res_lat[:, t, :]).then_inc(out_done, 16)
            sp.wait_ge(out_done, 16 * LAT)

        @block.tensor
        def _(pe):
            def free(phase, i, label):
                for who, value in occupants(phase, i, label):
                    pe.wait_ge(DRAIN[who], value)

            def mm3(out, s_hi, s_lo, m_hi, m_lo, first, last):
                nc.tensor.matmul(out, s_hi, m_hi, start=first, stop=False)
                nc.tensor.matmul(out, s_hi, m_lo, start=False, stop=False)
                return nc.tensor.matmul(out, s_lo, m_hi, start=False, stop=last)

            def feature_unit(phase, i, k, groups, fresh=None):
                pe.wait_ge(lo_done, before("units", phase, i) + (k + 1))
                s = slot(phase, k)
                for label, a, b in groups:
                    free(phase, i, label)
                    out = bank[dict((x[0], x[1]) for x in STEPS[phase])[label]][:, 0:b - a]
                    for kc in range(KC):
                        if fresh:
                            pe.wait_ge(stage_lo, before("stage", fresh[0]) + (KC if b > fresh[1] else 0) + kc + 1)
                        c = slice(kc * P, (kc + 1) * P)
                        last = mm3(out, w_hi[:, s, c], w_lo[:, s, c], hT_hi[:, kc, a:b], hT_lo[:, kc, a:b],
                                   kc == 0, kc == KC - 1)
                    last.then_inc(pe_step, 1)

            def token_units(phase, i, k0, name, tiles, ready=None, between=()):
                between = dict(between)
                for q in range(4):
                    k = k0 + q
                    pe.wait_ge(lo_done, before("units", phase, i) + (k + 1))
                    s = slot(phase, k)
                    for t in range(tiles):
                        if q == 0:
                            free(phase, i, f"{name}{t}")
                        for kk in range(2):
                            kc = 2 * q + kk
                            if ready:
                                ready(kc, t)
                            c = slice(kk * 512, (kk + 1) * 512)
                            tt = slice(t * P, (t + 1) * P)
                            last = mm3(bank[t][:, :], hT_hi[:, kc, tt], hT_lo[:, kc, tt], w_hi[:, s, c],
                                       w_lo[:, s, c], kc == 0, kc == KC - 1)
                        if q == 3 or t == tiles - 1:
                            last.then_inc(pe_step, 1)
                        if (q, t) in between:
                            between[q, t]()

            def down(phase, i, k0, tiles, a_hi, a_lo, ready, order=None):
                for half in range(2):
                    for q in range(2):
                        k = k0 + 2 * half + q
                        pe.wait_ge(lo_done, before("units", phase, i) + (k + 1))
                        s = slot(phase, k)

                        def part(t, kks):
                            for kk in kks:
                                c = 2 * q + kk
                                if half == 0:
                                    ready(c, t)
                                if c == 0:
                                    free(phase, i, f"down{half}.{t}")
                                tt = slice(t * P, (t + 1) * P)
                                n = slice(kk * 512, (kk + 1) * 512)
                                last = mm3(bank[t][:, :], a_hi[:, c, tt], a_lo[:, c, tt], w_hi[:, s, n],
                                           w_lo[:, s, n], c == 0, c == CH - 1)
                            return last

                        if half == 0 and q == 1:
                            for t in range(tiles):
                                part(t, [0])
                            for t in range(tiles):
                                part(t, [1]).then_inc(pe_step, 1)
                        else:
                            for t in order if order and half == 0 else range(tiles):
                                last = part(t, [0, 1])
                                if q == 1:
                                    last.then_inc(pe_step, 1)
                            if q == 0:
                                last.then_inc(pe_step, 1)

            def mods(phase, i, g, units, rows):
                buf, landed, slots, wide = MOD_UNITS[phase == "ffn0"]
                w = wide // 2
                for n in units:
                    if n == 0:
                        free(phase, i, f"rows{g}")
                    s = n % slots
                    trips = KC // slots
                    pe.wait_ge(landed[s], 16 * (n // slots + 1) + 16 * trips * groups_before(phase, i, g))
                    for block in range(2):
                        tile = 32 * (2 * (n % 2) + block)
                        last = nc.tensor.matmul(bank[rows][tile:tile + 32, 0:w], scT[:, n, :],
                                                buf[:, s, block * w:(block + 1) * w], start=n < 2, stop=n >= KC - 2,
                                                tile_position=(0, tile))
                    last.then_inc(pe_step, 1)

            def mod_columns(phase, i, g, src, b):
                pe.wait_ge(*named(drained(phase, i, f"rows{g}")))
                free(phase, i, f"cols{g}")
                for j in range(src.shape[1] // P):
                    last = nc.tensor.transpose(bank[b][:, j * P:(j + 1) * P], src[:, j * P:(j + 1) * P], ident[:, :])
                last.then_inc(pe_step, 1)

            def named(pair):
                return DRAIN[pair[0]], pair[1]

            diags = [0]

            def gates(phase, n):
                for j in range(n):
                    free(phase, 0, f"gate{j}")
                    pe.wait_ge(diag_ready, diags[0] + 1)
                    b = dict((x[0], x[1]) for x in STEPS[phase])[f"gate{j}"]
                    nc.tensor.matmul(bank[b][:, :], ones[:, :], DIAG[j], start=True, stop=True).then_inc(pe_step, 1)
                    diags[0] += 1

            def ln(phase, tiles, n_gates):
                gates(phase, n_gates)
                for g, (t0, t1) in enumerate(LN_GROUPS[tiles]):
                    if g == 0:
                        pe.wait_ge(xn_ready, XN_BASE[phase] + t1)
                    else:
                        pe.wait_ge(xn_last, XL_BASE[phase] + 2)
                    for kc in range(KC):
                        free(phase, 0, f"ln{g}.{kc}")
                        b, at = ln_at(tiles, g, kc)
                        for t in range(t0, t1):
                            last = nc.tensor.transpose(bank[b][:, at + (t - t0) * P:at + (t - t0 + 1) * P],
                                                       res(t)[:, kc * P:(kc + 1) * P], ident[:, :])
                        last.then_inc(pe_step, 1)

            pe.wait_ge(const_in, N_CONST)
            pe.wait_ge(pool_const, 2)
            pe.wait_ge(sc_ready, 1)
            mods("v0", 0, 0, range(KC), 6)
            mod_columns("v0", 0, 0, rbuf[:, 0, :], 7)

            def hT_ready(kc, t):
                if t in (0, LAT):
                    pe.wait_ge(stage_lo, 2 * kc + t // LAT + 1)

            def part(g, units):
                return lambda: mods("v0", 0, g, units, 6)

            def columns_of(g):
                return lambda: mod_columns("v0", 0, g, rbuf[:, 0, :], 7)

            token_units("v0", 0, 0, "v", TILES0, hT_ready,
                        {(0, 2): part(1, range(4)), (0, 5): part(1, range(4, KC)), (1, 0): columns_of(1),
                         (2, 5): part(2, range(4)), (3, 2): part(2, range(4, KC)), (3, 5): columns_of(2)})
            with nc.tensor.Fori(0, 3) as i:
                def part(units):
                    return lambda: mods("v", i, 0, units, 6)

                token_units("v", i, 0, "v", TILES0, None,
                            {(0, 5): part(range(2)), (1, 5): part(range(2, 4)), (2, 5): part(range(4, KC)),
                             (3, 5): lambda: mod_columns("v", i, 0, rbuf[:, 0, :], 7)})
            gates("gate0a", 4)

            pe.wait_ge(const_in, N_CONST + 16 * 2)
            for h in range(2):
                free("rowsum", 0, f"rs{h}")
                nc.tensor.matmul(bank[4 + h][:, :], ones[:, :], wsT[:, 4 * h:4 * h + 4, :].rearrange("p a b -> p (a b)"),
                                 start=True, stop=True).then_inc(pe_step, 1)
            for p in range(PIECES_A):
                for c in range(CH):
                    g = (CH * p + c) // 2
                    feature_unit("gmlp", p, c, [(f"u{c}.0", 0, HALF0), (f"u{c}.1", HALF0, TOK0)])
                    col = slice((CH * p + c) * P, (CH * p + c + 1) * P)
                    if c == 0:
                        pe.wait_ge(xn_ready, (p + 1) * TILES0)
                    for h in range(2):
                        free("gmlp", p, f"s{c}.{h}")
                        for j in range(3):
                            last = nc.tensor.matmul(bank[4 + h][:, j * P:(j + 1) * P], vtok[:, 3 * h + j, col],
                                                    wsT[:, g, :], start=True, stop=True)
                        last.then_inc(pe_step, 1)

                def ready(c, t):
                    if t in (0, 3):
                        pe.wait_ge(stage_lo, count("stage", "gmlp", p, 2 * c + t // 3))
                down("gmlp", p, CH, TILES0, act_hi0, act_lo0, ready)
            ln("ln0a", TILES0, 4)

            with nc.tensor.Fori(0, PIECES_F) as p:
                for c in range(CH):
                    feature_unit("ffn0", p, c, [(f"up{c}.0", 0, HALF0), (f"up{c}.1", HALF0, TOK0)],
                                 ("ln0a", TOKL) if c == 0 else None)
                    if c < 3:
                        mods("ffn0", p, 0, [(0, 1, 2), (3, 4, 5), (6, 7)][c], 4)
                mod_columns("ffn0", p, 0, rows1, 5)

                def ready(c, t):
                    if t in (0, 3):
                        pe.wait_ge(stage_lo, count("stage", "ffn0", p, 2 * c + t // 3))
                down("ffn0", p, CH, TILES0, act_hi0, act_lo0, ready)
            ln("ln0b", TILES0, 2)

            with nc.tensor.Fori(0, HEADS) as h:
                feature_unit("heads", h, 0, [("q0", 0, TOKL)], ("ln0b", TOKL))
                feature_unit("heads", h, 1, [("q1", 0, TOKL)])
                feature_unit("heads", h, 2, [("k0", 0, TOKL), ("kc0", TOKL, TOK0)], ("ln0b", TOKL))
                feature_unit("heads", h, 3, [("k1", 0, TOKL), ("kc1", TOKL, TOK0)])
                token_units("heads", h, 4, "v", TILES0)
                pe.wait_ge(stage_lo, count("stage", "heads", h, 5))
                for t in range(TILES0):
                    free("heads", h, f"s{t}")
                    tt = slice(t * P, (t + 1) * P)
                    b = bank[[6, 7, 4, 5, 6, 7][t]]
                    for d in range(2):
                        last = mm3(b[:, :], k_hi[:, d, tt], k_lo[:, d, tt], q_hi[:, d, :], q_lo[:, d, :],
                                   d == 0, d == 1)
                    last.then_inc(pe_step, 1)
                token_units("heads", h, 8, "gf", LAT)
                for t in range(LAT):
                    free("heads", h, f"of{t}")
                    pe.wait_ge(stage_lo, count("stage", "heads", h, 6 + 2 + t))
                    pe.wait_ge(*named(drained("heads", h, "v5")))
                    keys = [(LAT, 0 + t * P), (LAT + 1, 512 + t * P)]
                    keys += [(kt, FWD_AT[kt] + (t - kt) * P) for kt in range(t + 1)]
                    for n, (kt, at) in enumerate(keys):
                        last = mm3(bank[4 + t][:, :], pa_hi[:, at:at + P], pa_lo[:, at:at + P], v_hi[:, kt, :],
                                   v_lo[:, kt, :], n == 0, n == len(keys) - 1)
                    last.then_inc(pe_step, 1)
                token_units("heads", h, 12, "gb", LAT)
                def transpose_y(t):
                    free("heads", h, f"y{t}")
                    pe.wait_ge(y_step, h * 8 + (LAT + LAT - t))
                    for j in range(CH):
                        last = nc.tensor.transpose(bank[4 + t][:, j * P:(j + 1) * P], y[:, t, j * P:(j + 1) * P],
                                                   ident[:, :])
                    last.then_inc(pe_step, 1)

                for t in reversed(range(LAT)):
                    if t == 0:
                        transpose_y(3)
                    free("heads", h, f"ob{t}")
                    pe.wait_ge(stage_lo, count("stage", "heads", h, 12 + 2 + (LAT - 1 - t)))
                    keys = [(LAT, 0 + t * P), (LAT + 1, 512 + t * P)]
                    keys += [(kt, BWD_AT[kt] + t * P) for kt in range(t, LAT)]
                    for n, (kt, at) in enumerate(keys):
                        last = mm3(bank[4 + t][:, :], pa_hi[:, at:at + P], pa_lo[:, at:at + P], v_hi[:, kt, :],
                                   v_lo[:, kt, :], n == 0, n == len(keys) - 1)
                    last.then_inc(pe_step, 1)
                transpose_y(2)
                transpose_y(1)

                def ready(c, t):
                    if c == 0:
                        if t == 1:
                            transpose_y(0)
                        pe.wait_ge(*named(drained("heads", h, f"y{t}")))

                down("heads", h, 16, LAT, act_hi1, act_lo1, ready, (3, 2, 1, 0))
            ln("ln1a", LAT, 2)

            with nc.tensor.Fori(0, PIECES_F) as p:
                for c in range(CH):
                    feature_unit("ffn1", p, c, [(f"up{c}.0", 0, TOKL)], ("ln1a", 2 * P) if c == 0 else None)

                def ready(c, t):
                    if t == 0:
                        pe.wait_ge(stage_lo, count("stage", "ffn1", p, c))
                down("ffn1", p, CH, LAT, act_hi1, act_lo1, ready)

        @block.scalar
        def _(act):
            def split_hi(phase, i, k, used):
                if isinstance(i, int) and count("units", phase, i, k) > TOTAL["units"]:
                    return
                s, value = unit_in(phase, i, k)
                act.wait_ge(w_in[s], value)
                if used is not None:
                    act.wait_ge(pe_step, used)
                nc.scalar.activation(w_hi[:, slot(phase, k), :], raw[:, s, :], ACT.Copy).then_inc(hi_done, 1)

            def stage_split(phase, i, j, out, width):
                q = BASE[phase]["stage"] + j
                src = stage[:, q % 2, 0:width]
                if len(out.shape) == 3:
                    src = src.rearrange("p (a b) -> p a b", a=out.shape[1])
                nc.scalar.activation(out, src, ACT.Copy).then_inc(stage_hi, 1)

            def used_unit(phase, i, k):
                return step_of(phase, i, UNIT_END[phase][k])

            def mod_rows(phase, i, g, out, b, used):
                act.wait_ge(pe_step, step_of(phase, i, f"rows{g}"))
                if used is not None:
                    act.wait_ge(pe_step, used)
                nc.scalar.activation(out, bank[b][:, 0:out.shape[1]], ACT.Copy).then_inc(act_drain, 1)

            def gates(phase, n):
                act.wait_ge(dve_drain, before("D", phase))
                for j in range(n):
                    act.wait_ge(pe_step, step_of(phase, 0, f"gate{j}"))
                    g = gate_lat if j < 2 else gate_ctx
                    b = dict((x[0], x[1]) for x in STEPS[phase])[f"gate{j}"]
                    nc.scalar.activation(g[:, (j % 2) * 512:(j % 2 + 1) * 512], bank[b][:, :], ACT.Copy)\
                        .then_inc(act_drain, 1)

            def ln(phase, tiles, n_gates, next_phase, split_after=1):
                for t in range(LN_GROUPS[tiles][0][1]):
                    act.wait_ge(nbias_ready, NB_BASE[phase] + t + 1)
                    nc.scalar.activation(res(t), res(t), ACT.Identity, bias=nbias[:, t:t + 1], scale=rstd[:, t:t + 1])\
                        .then_inc(xn_ready, 1)
                gates(phase, n_gates)
                act.wait_ge(col_ready, COL_READY[phase])
                scale, shift = COLS[phase]
                for g, (t0, t1) in enumerate(LN_GROUPS[tiles]):
                    v, w = (0 if t0 < LAT else 1), (t1 - t0) * P
                    for kc in range(0, KC, 2):
                        m = (KC * g + kc) // 2
                        q = BASE[phase]["stage"] + 2 * m
                        odd = kc + 1
                        act.wait_ge(pe_step, step_of(phase, 0, f"ln{g}.{odd}"))
                        act.wait_ge(stage_lo, q - 3 if m >= 2 else BASE[phase]["stage"])
                        b, at = ln_at(tiles, g, kc)
                        nc.scalar.activation(stage[:, m % 2, 0:w], bank[b][:, at:at + w], ACT.Identity,
                                             bias=shift[:, kc, v:v + 1], scale=scale[:, kc, v:v + 1])\
                            .then_inc(act_drain, 1)
                        b, at = ln_at(tiles, g, odd)
                        nc.scalar.activation(hT_hi[:, odd, t0 * P:t1 * P], bank[b][:, at:at + w], ACT.Identity,
                                             bias=shift[:, odd, v:v + 1], scale=scale[:, odd, v:v + 1])\
                            .then_inc(stage_hi, 1)
                        act.wait_ge(act_drain, drained(phase, 0, f"ln{g}.{kc}")[1])
                        nc.scalar.activation(hT_hi[:, kc, t0 * P:t1 * P], stage[:, m % 2, 0:w], ACT.Copy)\
                            .then_inc(stage_hi, 1)
                    if g == split_after:
                        split_hi(next_phase, 0, 1, before("step", phase))
                act.wait_ge(stage_lo, BASE[phase]["stage"] + 2 * KC)

            act.wait_ge(cvec_in, 16)
            act.wait_ge(sc_zero, 1)
            nc.scalar.activation(scT[:, :, 0:2], cvec[:, :, :], ACT.Silu).then_inc(sc_ready, 1)
            act.dma_start(mask[:, :, :], small_d[:, P:3 * P].rearrange("p (a b) -> p a b", a=2)).then_inc(dec_in, 16)
            act.dma_start(lg[:, 0, :], decay_d.partition_broadcast(P)).then_inc(dec_in, 16)
            act.wait_ge(dec_in, 32)
            nc.scalar.activation(lg[:, 1, :], lg[:, 0, :], ACT.Exp).then_inc(lg_act, 1)
            act.wait_ge(lg_dve, 1)
            nc.scalar.activation(lg[:, 3, :], lg[:, 2, :], ACT.Ln).then_inc(lg_act, 1)

            def h0_split(kcs):
                for j in [2 * kc + v for kc in kcs for v in range(2)]:
                    kc, v = j // 2, j % 2
                    a, b = (0, TOKL) if v == 0 else (TOKL, TOK0)
                    act.wait_ge(stage_full, count("full", "v0", 0, j))
                    stage_split("v0", 0, j, hT_hi[:, kc, a:b], b - a)

            mod_rows("v0", 0, 0, rbuf[:, 0, :], 6, None)
            split_hi("v0", 0, 0, None)
            h0_split(range(4))
            split_hi("v0", 0, 1, None)
            mod_rows("v0", 0, 1, rbuf[:, 0, :], 6, step_of("v0", 0, "cols0"))
            split_hi("v0", 0, 2, used_unit("v0", 0, 0))
            h0_split(range(4, 6))
            split_hi("v0", 0, 3, used_unit("v0", 0, 1))
            h0_split(range(6, 8))
            split_hi("v0", 0, 4, used_unit("v0", 0, 2))

            def gelus(phase, i, at):
                for t in range(TILES0):
                    act.wait_ge(dve_drain, drained(phase, i, f"v{t}")[1])
                    c = vtok[:, t, bass.ds(at, 512)]
                    nc.scalar.activation(c, c, ACT.Gelu).then_inc(gelu_done, 1)

            mod_rows("v0", 0, 2, rbuf[:, 0, :], 6, step_of("v0", 0, "cols1"))
            gelus("v0", 0, 0)
            with nc.scalar.Fori(0, 3) as i:
                begin = before("step", "v", i)
                split_hi("v", i, 1, begin - 1)
                for k in range(1, 4):
                    split_hi("v", i, k + 1, used_unit("v", i, k - 1))
                mod_rows("v", i, 0, rbuf[:, 0, :], 6, begin)
                gelus("v", i, i * 512 + 512)
            gates("gate0a", 4)
            for h in range(2):
                act.wait_ge(pe_step, step_of("rowsum", 0, f"rs{h}"))
                nc.scalar.activation(rowsum[:, 4 * h:4 * h + 4, :].rearrange("p a b -> p (a b)"), bank[4 + h][:, :],
                                     ACT.Copy).then_inc(act_drain, 1)

            def down_splits(phase, i, k0):
                for k in range(k0, k0 + 4):
                    split_hi(phase, i, k + 1, used_unit(phase, i, k - 1))

            for p in range(PIECES_A):
                begin = before("step", "gmlp", p)
                for c in range(CH):
                    split_hi("gmlp", p, c + 1, begin if c == 0 else used_unit("gmlp", p, c - 1))
                    for g in range(2):
                        j = 2 * c + g
                        q = BASE["gmlp"]["stage"] + 8 * p + j
                        act.wait_ge(pe_step, step_of("gmlp", p, f"u{c}.{g}"))
                        act.wait_ge(stage_full, before("full", "gmlp", p) + j - 1)
                        nc.scalar.activation(rbuf[:, q % 2, 0:HALF0], bank[6 + g][:, 0:HALF0], ACT.Gelu,
                                             bias=cols[:, BU + CH * p + c:BU + CH * p + c + 1]).then_inc(act_drain, 1)
                    for g in range(2):
                        j = 2 * c + g
                        act.wait_ge(stage_full, count("full", "gmlp", p, j))
                        stage_split("gmlp", p, j, act_hi0[:, c, g * HALF0:(g + 1) * HALF0], HALF0)
                down_splits("gmlp", p, CH)
            ln("ln0a", TILES0, 4, "ffn0")

            def ffn(phase, i, groups, width, a_hi):
                begin = before("step", phase, i)
                for c in range(CH):
                    if c:
                        split_hi(phase, i, c + 1, used_unit(phase, i, c - 1))
                    for g in range(groups):
                        j = groups * c + g
                        q = BASE[phase]["stage"] + j
                        act.wait_ge(pe_step, step_of(phase, i, f"up{c}.{g}"))
                        act.wait_ge(stage_full, before("full", phase, i) + (j - 1))
                        b = bank[6 + g] if groups == 2 else bank[4 + c]
                        nc.scalar.activation(rbuf[:, q % 2, 0:width], b[:, 0:width], ACT.Relu).then_inc(act_drain, 1)
                    for g in range(groups):
                        j = groups * c + g
                        act.wait_ge(stage_full, count("full", phase, i, j))
                        stage_split(phase, i, j, a_hi[:, c, g * width:(g + 1) * width], width)
                    if phase == "ffn0" and c == 2:
                        mod_rows(phase, i, 0, rows1[:, :], 4, begin)
                down_splits(phase, i, CH)
                if not isinstance(i, int):
                    split_hi(phase, i, 2 * CH + 1, used_unit(phase, i, 2 * CH - 1))

            with nc.scalar.Fori(0, PIECES_F - 1) as p:
                ffn("ffn0", p, 2, HALF0, act_hi0)
            ffn("ffn0", PIECES_F - 1, 2, HALF0, act_hi0)
            ln("ln0b", TILES0, 2, "heads", 0)

            def head(h):
                split_hi("heads", h, 2, used_unit("heads", h, 0))
                act.wait_ge(stage_full, before("full", "heads", h))
                act.dma_start(dec[:, :, :], dist_d).then_inc(dec_in, 16)
                split_hi("heads", h, 3, used_unit("heads", h, 1))
                for d in range(2):
                    act.wait_ge(stage_full, count("full", "heads", h, d))
                    stage_split("heads", h, d, q_hi[:, d, :], TOKL)
                split_hi("heads", h, 4, used_unit("heads", h, 2))
                for d in range(2):
                    act.wait_ge(dve_drain, drained("heads", h, f"kc{d}")[1])
                    stage_split("heads", h, 2 + d, k_hi[:, d, TOKL:TOK0], CTX * P)
                split_hi("heads", h, 5, used_unit("heads", h, 3))
                for d in range(2):
                    act.wait_ge(stage_full, count("full", "heads", h, 2 + d))
                    stage_split("heads", h, 4 + d, k_hi[:, d, 0:TOKL], TOKL)
                for k in range(6, 9):
                    split_hi("heads", h, k, used_unit("heads", h, k - 2))
                act.wait_ge(dec_in, h * 16 + 48)
                act.wait_ge(lgh_ready, h + 1)
                for way in range(2):
                    nc.scalar.activation(dec[:, way, :], dec[:, way, :], ACT.Exp, scale=lgh[:, way:way + 1])\
                        .then_inc(exp_done, 1)
                for t in range(TILES0):
                    act.wait_ge(pe_step, step_of("heads", h, f"v{t}"))
                    nc.scalar.activation(v_hi[:, t, :], bank[t][:, :], ACT.Copy).then_inc(psum_hi, 1)
                split_hi("heads", h, 9, used_unit("heads", h, 7))
                for t in range(TILES0):
                    act.wait_ge(pe_step, step_of("heads", h, f"s{t}"))
                    nc.scalar.activation(scr[:, t, :], bank[[6, 7, 4, 5, 6, 7][t]][:, :], ACT.Copy)\
                        .then_inc(act_drain, 1)
                for n, (at, w) in enumerate(zip([0, 512] + FWD_AT, FWD_W)):
                    act.wait_ge(stage_full, count("full", "heads", h, 4 + n))
                    stage_split("heads", h, 6 + n, pa_hi[:, at:at + w], w)
                    if n in (1, 3, 5):
                        k = 10 + n // 2
                        split_hi("heads", h, k, used_unit("heads", h, k - 2))
                split_hi("heads", h, 13, used_unit("heads", h, 11))
                for t in range(LAT):
                    act.wait_ge(pe_step, step_of("heads", h, f"gf{t}"))
                    if t == 0:
                        act.wait_ge(res_base, BASE_RES["ln0b"] + LAT)
                    nc.scalar.activation(gs[:, t, :], bank[t][:, :], ACT.Silu).then_inc(act_drain, 1)
                split_hi("heads", h, 14, used_unit("heads", h, 12))
                act.wait_ge(pe_step, step_of("heads", h, f"of{LAT - 1}"))
                for n, (at, w) in enumerate(zip([0, 512] + BWD_AT[::-1], BWD_W)):
                    act.wait_ge(stage_full, count("full", "heads", h, 10 + n))
                    stage_split("heads", h, 12 + n, pa_hi[:, at:at + w], w)
                    if n in (1, 3):
                        k = 15 + n // 2
                        split_hi("heads", h, k, used_unit("heads", h, k - 2))
                split_hi("heads", h, 17, used_unit("heads", h, 15))
                for t in range(LAT):
                    act.wait_ge(pe_step, step_of("heads", h, f"gb{t}"))
                    act.wait_ge(*[dve_drain, drained("heads", h, f"of{t}")[1]])
                    nc.scalar.activation(gs[:, t, :], bank[t][:, :], ACT.Silu).then_inc(act_drain, 1)
                for t in reversed(range(LAT)):
                    act.wait_ge(pe_step, step_of("heads", h, f"y{t}"))
                    nc.scalar.activation(act_hi1[:, :, t * P:(t + 1) * P],
                                         bank[4 + t][:, :].rearrange("p (a b) -> p a b", a=CH), ACT.Copy)\
                        .then_inc(psum_hi, 1)
                for k in range(18, 21 if isinstance(h, int) else 22):
                    split_hi("heads", h, k, used_unit("heads", h, k - 2))

            with nc.scalar.Fori(0, HEADS - 1) as h:
                head(h)
            head(HEADS - 1)
            ln("ln1a", LAT, 2, "ffn1")
            with nc.scalar.Fori(0, PIECES_F - 1) as p:
                ffn("ffn1", p, 1, TOKL, act_hi1)
            ffn("ffn1", PIECES_F - 1, 1, TOKL, act_hi1)

        @block.vector
        def _(dve):
            tt = nc.vector.tensor_tensor
            ts = nc.vector.tensor_scalar
            stt = nc.vector.scalar_tensor_tensor

            def f32(ap):
                return ap.bitcast(F32)

            def split_lo(phase, i, k):
                if isinstance(i, int) and count("units", phase, i, k) > TOTAL["units"]:
                    return
                dve.wait_ge(hi_done, count("units", phase, i, k))
                s, _ = unit_in(phase, i, k)
                w = slot(phase, k)
                tt(w_lo[:, w, :], raw[:, s, :], f32(w_hi[:, w, :]), ALU.subtract).then_inc(lo_done, 1)

            def stage_lo_part(phase, i, j, out, hi, width):
                q = BASE[phase]["stage"] + j
                dve.wait_ge(stage_hi, count("stage", phase, i, j))
                src = stage[:, q % 2, 0:width]
                if len(out.shape) == 3:
                    src = src.rearrange("p (a b) -> p a b", a=out.shape[1])
                tt(out, src, f32(hi), ALU.subtract).then_inc(stage_lo, 1)

            def stage_slot(phase, i, j, width):
                q = BASE[phase]["stage"] + j
                if isinstance(i, int) and count("stage", phase, i, j) < 3:
                    return stage[:, q % 2, 0:width]
                dve.wait_ge(stage_lo, count("stage", phase, i, j) - 2)
                return stage[:, q % 2, 0:width]

            def mod_columns(phase, i, g, b, n, out, bias):
                dve.wait_ge(pe_step, step_of(phase, i, f"cols{g}"))
                src = bank[b][:, 0:n * P].rearrange("p (j par b r) -> p par b j r", j=n, par=2, b=2)
                tt(out, src[:, 0, :, :, 0:2], bias.unsqueeze(3).to_broadcast([P, 2, n, 2]), ALU.add)\
                    .then_inc(mod_step, 1)
                dve.wait_ge(mod_step, before("mods", phase, i) + (g + 1))
                tt(out, out, src[:, 1, :, :, 0:2], ALU.add).then_inc(dve_drain, 1)

            def mod(layer, part):
                return modc[:, layer, 8 * part:8 * part + 8, :]

            cr = [0]

            def columns(phase, layer, shift, scale, ln_row):
                g = cols[:, LNC + 8 * ln_row:LNC + 8 * ln_row + 8].unsqueeze(2).to_broadcast([P, 8, 2])
                b = cols[:, LNC + 8 * ln_row + 8:LNC + 8 * ln_row + 16].unsqueeze(2).to_broadcast([P, 8, 2])
                col_scale, col_shift = COLS[phase]
                ts(col1[:, :, :], mod(layer, scale), 1.0, None, ALU.add).then_inc(col_ready, 1)
                dve.wait_ge(col_ready, cr[0] + 1)
                tt(col_scale[:, :, :], col1[:, :, :], g, ALU.mult).then_inc(col_ready, 1)
                tt(col_shift[:, :, :], col1[:, :, :], b, ALU.mult).then_inc(col_ready, 1)
                dve.wait_ge(col_ready, cr[0] + 3)
                tt(col_shift[:, :, :], col_shift[:, :, :], mod(layer, shift), ALU.add).then_inc(col_ready, 1)
                cr[0] += 4

            def statistics(sources, s, done, at=0, between=None):
                for n, src in enumerate(sources):
                    last = nc.vector.bn_stats(out=bst[:, s, at + n, :], in_=src)
                last.then_inc(stat_step, 1)
                if between:
                    between()
                dve.wait_ge(stat_step, 2 * done + 1)
                if not isinstance(done, int):
                    dve.sem_inc(stat_seen, 1)
                nc.vector.bn_aggr(out=mv[:, s, :], in_=bst[:, s, 0:at + len(sources), :]).then_inc(stat_step, 1)
                dve.wait_ge(stat_step, 2 * done + 2)
                ts(veps[:, s:s + 1], mv[:, s, 1:2], EPS, None, ALU.add).then_inc(var_ready, 1)

            def normalise(phase, t, ready):
                dve.wait_ge(rstd_ready, BASE_STAT[phase] + t + 1)
                ts(res(t), res(t), mv[:, t, 0:1], rstd[:, t:t + 1], ALU.subtract, ALU.mult).then_inc(ready, 1)

            def negative_bias(phase, t, tiles):
                if t < LN_GROUPS[tiles][0][1]:
                    dve.wait_ge(rstd_ready, BASE_STAT[phase] + t + 1)
                    ts(nbias[:, t:t + 1], mv[:, t, 0:1], rstd[:, t:t + 1], -1.0, ALU.mult, ALU.mult)\
                        .then_inc(nbias_ready, 1)

            def ln_split(phase, tiles, next_phase, split_after=1):
                scale, shift = COLS[phase]
                for g, (t0, t1) in enumerate(LN_GROUPS[tiles]):
                    v, w = (0 if t0 < LAT else 1), (t1 - t0) * P
                    for kc in range(0, KC, 2):
                        j, odd = KC * g + kc, kc + 1
                        q = BASE[phase]["stage"] + j
                        m = j // 2
                        part = rbuf[:, m % 2, 0:w]
                        hi = f32(hT_hi[:, odd, t0 * P:t1 * P])
                        dve.wait_ge(stage_hi, count("stage", phase, 0, j))
                        dve.wait_ge(stage_lo, q - 2 if m >= 2 else BASE[phase]["stage"])
                        b, at = ln_at(tiles, g, odd)
                        stt(part, bank[b][:, at:at + w], scale[:, odd, v:v + 1], hi, ALU.mult, ALU.subtract)\
                            .then_inc(dve_drain, 1)
                        dve.wait_ge(stage_hi, count("stage", phase, 0, j + 1))
                        src = stage[:, m % 2, 0:w]
                        tt(hT_lo[:, kc, t0 * P:t1 * P], src, f32(hT_hi[:, kc, t0 * P:t1 * P]), ALU.subtract)\
                            .then_inc(stage_lo, 1)
                        dve.wait_ge(dve_drain, drained(phase, 0, f"ln{g}.{odd}")[1])
                        ts(hT_lo[:, odd, t0 * P:t1 * P], part, shift[:, odd, v:v + 1], None, ALU.add)\
                            .then_inc(stage_lo, 1)
                    if g == split_after:
                        split_lo(next_phase, 0, 1)

            def drain(phase, i, half, t, tiles):
                e = BASE[phase]["add"] + half * tiles + t
                dve.wait_ge(pe_step, step_of(phase, i, f"down{half}.{t}"))
                if not (isinstance(i, int) and e + i * PER[phase]["add"] < 2):
                    dve.wait_ge(res_added, count("add", phase, i, half * tiles + t) - 2)
                tt(gy[:, e % 2, :], bank[t][:, :], gate_of(t)[:, half * 512:(half + 1) * 512], ALU.mult)\
                    .then_inc(dve_drain, 1)

            def down(phase, i, k0, tiles, then=None):
                split_lo(phase, i, k0 + 1)
                split_lo(phase, i, k0 + 2)
                if then:
                    then()
                for t in range(tiles):
                    drain(phase, i, 0, t, tiles)
                split_lo(phase, i, k0 + 3)
                split_lo(phase, i, k0 + 4)
                for t in range(tiles):
                    drain(phase, i, 1, t, tiles)

            def down_and_rows(phase, i, k0, tiles, ln_phase):
                split_lo(phase, i, k0 + 1)
                split_lo(phase, i, k0 + 2)
                for t in range(tiles):
                    drain(phase, i, 0, t, tiles)
                split_lo(phase, i, k0 + 3)
                first = before("add", phase, i)
                for t in range(tiles):
                    dve.wait_ge(res_added, first + t + 1)
                    nc.vector.bn_stats(out=bst[:, t, 0, :], in_=res(t)[:, 0:512])
                final = ln_phase == "ln1b"

                def rows(t):
                    between = None
                    if t >= 1 and not final:
                        between = lambda: negative_bias(ln_phase, t - 1, tiles)
                    if t == 2 and final:
                        between = lambda: normalise(ln_phase, 0, xn_ready)
                    dve.wait_ge(res_added, first + tiles + t + 1)
                    statistics([res(t)[:, 512:1024]], t, BASE_STAT[ln_phase] + t, 1, between)

                for t in range(tiles):
                    drain(phase, i, 1, t, tiles)
                    if t >= 1:
                        rows(t - 1)
                rows(tiles - 1)
                if not final:
                    for t in range(tiles - 2, tiles):
                        normalise(ln_phase, t, xn_last)
                    split_lo(phase, i, k0 + 4)
                    return

                dve.wait_ge(lnbc_in, 128)
                g, b = lnbc1[:, 0, :], lnbc1[:, 1, :]

                def gain(t):
                    stt(res(t), res(t), mv[:, t, 0:1], g, ALU.subtract, ALU.mult).then_inc(end_step, 1)

                def shift(t):
                    dve.wait_ge(end_step, t)
                    dve.wait_ge(rstd_ready, BASE_STAT[ln_phase] + t + 1)
                    stt(res(t), res(t), rstd[:, t:t + 1], b, ALU.mult, ALU.add).then_inc(out_ready, 1)

                gain(1)
                for t in range(2, tiles):
                    gain(t)
                    shift(t - 1)
                shift(tiles - 1)

            dve.wait_ge(lg_act, 1)
            ts(lg[:, 2, :], lg[:, 1, :], -1.0, 1.0, ALU.mult, ALU.add).then_inc(lg_dve, 1)
            dve.wait_ge(lg_dve, 1)
            ts(lg[:, 4, :], lg[:, 2, :], -1.0, 1.0, ALU.mult, ALU.add).then_inc(lg_dve, 1)
            dve.wait_ge(lg_dve, 2)
            ts(lg[:, 4, :], lg[:, 4, :], 1e-30, None, ALU.max).then_inc(lg_dve, 1)
            dve.wait_ge(lg_dve, 3)
            nc.vector.reciprocal(lg[:, 4, :], lg[:, 4, :]).then_inc(lg_dve, 1)
            dve.wait_ge(lg_dve, 4)
            tt(lg[:, 5, :], lg[:, 4, :], lg[:, 1, :], ALU.mult).then_inc(lg_dve, 1)
            dve.wait_ge(lg_dve, 5)
            dve.wait_ge(lg_act, 2)
            tt(lg[:, 5, :], lg[:, 5, :], lg[:, 3, :], ALU.mult).then_inc(lg_dve, 1)

            dve.wait_ge(const_in, N_CONST)
            def split_mods(g):
                m = modc[:, 0, 0:16, :].rearrange("p (b g j) v -> p g b j v", b=2, g=2)[:, g]
                bias = cols[:, ADAB:ADAB + 16].rearrange("p (b g j) -> p g b j", b=2, g=2)[:, g]
                mod_columns("v0", 0, g, 7, 4, m, bias)
                dve.wait_ge(dve_drain, drained("v0", 0, f"cols{g}")[1])
                ts(colS[:, 4 * g:4 * g + 4, :], mod(0, 1)[:, 4 * g:4 * g + 4, :], 1.0, None, ALU.add)\
                    .then_inc(vstat, 1)
                dve.wait_ge(vstat, g + 1)

            def h0(kcs):
                def low(j):
                    kc, v = j // 2, j % 2
                    a, b = (0, TOKL) if v == 0 else (TOKL, TOK0)
                    stage_lo_part("v0", 0, j, hT_lo[:, kc, a:b], hT_hi[:, kc, a:b], b - a)

                js = [2 * kc + v for kc in kcs for v in range(2)]
                for j in js:
                    kc, v = j // 2, j % 2
                    a, b = (0, TOKL) if v == 0 else (TOKL, TOK0)
                    dve.wait_ge(xT_in[kc // 2], 16)
                    ts(stage_slot("v0", 0, j, b - a), xT[:, kc, a:b], colS[:, kc, v:v + 1],
                       mod(0, 0)[:, kc, v:v + 1], ALU.mult, ALU.add).then_inc(stage_full, 1)
                    if j > js[0]:
                        low(j - 1)
                low(js[-1])

            split_lo("v0", 0, 0)
            split_mods(0)
            h0(range(4))
            split_lo("v0", 0, 1)
            split_mods(1)
            split_lo("v0", 0, 2)
            h0(range(4, 6))
            split_lo("v0", 0, 3)
            h0(range(6, 8))
            split_lo("v0", 0, 4)

            def mods_of(i, layer, c, n):
                return (modc[:, layer, bass.ds(c, n), :].rearrange("p (b j) v -> p b j v", b=2),
                        cols[:, bass.ds(c + (ADAB + 48 * layer), n)].rearrange("p (b j) -> p b j", b=2))

            def add_bias(phase, i, at):
                for t in range(TILES0):
                    dve.wait_ge(pe_step, step_of(phase, i, f"v{t}"))
                    tt(vtok[:, t, bass.ds(at, 512)], bank[t][:, :], bv[:, bass.ds(at, 512)], ALU.add)\
                        .then_inc(dve_drain, 1)

            dve.wait_ge(bv_in, 16)
            add_bias("v0", 0, 0)
            mod_columns("v0", 0, 2, 7, 4, *mods_of(0, 0, 16, 8))
            with nc.vector.Fori(0, 3) as i:
                split_lo("v", i, 1)
                split_lo("v", i, 2)
                for t in range(TILES0):
                    dve.wait_ge(gelu_done, i * TILES0 + (t + 1))
                    nc.vector.bn_stats(out=bst[:, t, bass.ds(i, 1), :].rearrange("p a b -> p (a b)"),
                                       in_=vtok[:, t, bass.ds(i * 512, 512)])
                split_lo("v", i, 3)
                split_lo("v", i, 4)
                add_bias("v", i, i * 512 + 512)
                mod_columns("v", i, 0, 7, 4, *mods_of(i, 0, i * 8 + 24, 8))
            dve.wait_ge(dve_drain, before("D", "gate0a"))
            columns("ln0a", 0, 3, 4, 0)
            for t in range(TILES0):
                dve.wait_ge(gelu_done, 3 * TILES0 + t + 1)
                statistics([vtok[:, t, 3 * 512:4 * 512]], t, t, 3)

            def normalise_v(p):
                for t in range(TILES0):
                    if p == 0:
                        dve.wait_ge(rstd_ready, t + 1)
                    c = vtok[:, t, p * 512:(p + 1) * 512]
                    ts(c, c, mv[:, t, 0:1], rstd[:, t:t + 1], ALU.subtract, ALU.mult).then_inc(xn_ready, 1)

            normalise_v(0)

            dve.wait_ge(act_drain, before("A", "gmlp"))
            dve.wait_ge(const_in, N_CONST + 32)
            for p in range(PIECES_A):
                for c in range(CH):
                    split_lo("gmlp", p, c + 1)
                    n = CH * p + c
                    g = n // 2
                    if c:
                        dve.wait_ge(dve_drain, drained("gmlp", p, f"s{c - 1}.1")[1])
                    stt(dcol[:, :], rowsum[:, g, :], cols[:, LNB + n:LNB + n + 1], bs[:, g, :], ALU.mult, ALU.add)\
                        .then_inc(gm_step, 1)
                    dve.wait_ge(gm_step, n + 1)
                    for h in range(2):
                        j = 2 * c + h
                        q = BASE["gmlp"]["stage"] + 8 * p + j
                        st = stage_slot("gmlp", p, j, HALF0)
                        dve.wait_ge(pe_step, step_of("gmlp", p, f"s{c}.{h}"))
                        st3 = st.rearrange("p (a b) -> p a b", a=3)
                        stt(st3, bank[4 + h][:, 0:HALF0].rearrange("p (a b) -> p a b", a=3),
                            cols[:, LNG + n:LNG + n + 1], dcol[:, :].unsqueeze(1).to_broadcast([P, 3, P]),
                            ALU.mult, ALU.add).then_inc(dve_drain, 1)
                        dve.wait_ge(dve_drain, drained("gmlp", p, f"s{c}.{h}")[1])
                        dve.wait_ge(act_drain, drained("gmlp", p, f"u{c}.{h}")[1])
                        tt(st, st, rbuf[:, q % 2, 0:HALF0], ALU.mult).then_inc(stage_full, 1)
                    for h in range(2):
                        at = (slice(None), c, slice(h * HALF0, (h + 1) * HALF0))
                        stage_lo_part("gmlp", p, 2 * c + h, act_lo0[at], act_hi0[at], HALF0)
                if p < PIECES_A - 1:
                    down("gmlp", p, CH, TILES0, lambda: normalise_v(p + 1))
                else:
                    down_and_rows("gmlp", p, CH, TILES0, "ln0a")
            ln_split("ln0a", TILES0, "ffn0")

            def ffn(phase, i, groups, width, a_hi, a_lo, tiles, ln_phase=None):
                for c in range(CH):
                    if c:
                        split_lo(phase, i, c + 1)
                    for g in range(groups):
                        j = groups * c + g
                        q = BASE[phase]["stage"] + j
                        st = stage_slot(phase, i, j, width)
                        dve.wait_ge(act_drain, drained(phase, i, f"up{c}.{g}")[1])
                        r = rbuf[:, q % 2, 0:width]
                        tt(st, r, r, ALU.mult).then_inc(stage_full, 1)
                    for g in range(groups):
                        at = (slice(None), c, slice(g * width, (g + 1) * width))
                        stage_lo_part(phase, i, groups * c + g, a_lo[at], a_hi[at], width)
                if phase == "ffn0":
                    mod_columns(phase, i, 0, 5, 3, *mods_of(i, 1, i * 6, 6))
                if ln_phase:
                    down_and_rows(phase, i, CH, tiles, ln_phase)
                else:
                    down(phase, i, CH, tiles)
                    split_lo(phase, i, 2 * CH + 1)

            dve.wait_ge(act_drain, before("A", "ffn0"))
            with nc.vector.Fori(0, PIECES_F - 1) as p:
                ffn("ffn0", p, 2, HALF0, act_hi0, act_lo0, TILES0)
            dve.wait_ge(dve_drain, before("D", "ffn0", PIECES_F - 1))
            columns("ln0b", 1, 0, 1, 2)
            columns("ln1a", 1, 3, 4, 4)
            ffn("ffn0", PIECES_F - 1, 2, HALF0, act_hi0, act_lo0, TILES0, "ln0b")
            ln_split("ln0b", TILES0, "heads", 0)

            dve.wait_ge(act_drain, before("A", "heads"))
            dve.wait_ge(rope_in, 16)
            dve.wait_ge(dec_in, 32)
            dve.wait_ge(lg_dve, 6)
            def head(h):
                def rotate(r, a, b, scale, j, at_q):
                    t1, t2 = bank[a[1]][:, :], bank[b[1]][:, :]
                    cos, sin = rope[:, 0, :], rope[:, 1, :]
                    dve.wait_ge(pe_step, step_of("heads", h, b[0]))
                    stt(rbuf[:, 0, :], t1, scale, cos, ALU.mult, ALU.mult).then_inc(rope_step, 1)
                    stt(rbuf[:, 1, :], t2, scale, sin, ALU.mult, ALU.mult).then_inc(rope_step, 1)
                    dve.wait_ge(rope_step, h * 4 + (2 * r + 2))
                    st = stage_slot("heads", h, j, TOKL)
                    tt(st, rbuf[:, 0, :], rbuf[:, 1, :], ALU.subtract).then_inc(stage_full, 1)
                    dve.wait_ge(stage_full, count("full", "heads", h, at_q))
                    stt(rbuf[:, 0, :], t1, scale, sin, ALU.mult, ALU.mult).then_inc(dve_drain, 1)
                    stt(rbuf[:, 1, :], t2, scale, cos, ALU.mult, ALU.mult).then_inc(dve_drain, 1)
                    dve.wait_ge(dve_drain, drained("heads", h, b[0])[1])
                    st = stage_slot("heads", h, j + 1, TOKL)
                    tt(st, rbuf[:, 0, :], rbuf[:, 1, :], ALU.add).then_inc(stage_full, 1)

                nc.vector.tensor_copy(lgh[:, :].unsqueeze(2), lg[:, 5, :].rearrange("p (w h) -> p w h", w=2)
                                      [:, :, bass.ds(h, 1)]).then_inc(lgh_ready, 1)
                split_lo("heads", h, 2)
                split_lo("heads", h, 3)
                rotate(0, ("q0", 4), ("q1", 5), 1.0, 0, 0)
                for d in range(2):
                    stage_lo_part("heads", h, d, q_lo[:, d, :], q_hi[:, d, :], TOKL)
                split_lo("heads", h, 4)
                for d in range(2):
                    dve.wait_ge(pe_step, step_of("heads", h, f"kc{d}"))
                    ts(stage_slot("heads", h, 2 + d, CTX * P), bank[2 + d][:, 0:CTX * P], DK ** -0.5, None, ALU.mult)\
                        .then_inc(dve_drain, 1)
                    stage_lo_part("heads", h, 2 + d, k_lo[:, d, TOKL:TOK0], k_hi[:, d, TOKL:TOK0], CTX * P)
                split_lo("heads", h, 5)
                rotate(1, ("k0", 6), ("k1", 7), DK ** -0.5, 4, 2)
                for d in range(2):
                    stage_lo_part("heads", h, 4 + d, k_lo[:, d, 0:TOKL], k_hi[:, d, 0:TOKL], TOKL)
                for k in range(6, 9):
                    split_lo("heads", h, k)
                for way, a in ((0, 0), (1, 768 - P)):
                    dve.wait_ge(exp_done, h * 2 + (way + 1))
                    tt(dec[:, way, a:a + P], dec[:, way, a:a + P], mask[:, way, :], ALU.mult).then_inc(mask_done, 1)
                for t in range(TILES0):
                    dve.wait_ge(psum_hi, h * 10 + (t + 1))
                    tt(v_lo[:, t, :], bank[t][:, :], f32(v_hi[:, t, :]), ALU.subtract).then_inc(dve_drain, 1)
                split_lo("heads", h, 9)

                def decayed(way, j0, full0, keys, splits):
                    for n, (kt, a, m, w) in enumerate(keys):
                        at = 512 * (kt - LAT) if kt >= LAT else (FWD_AT, BWD_AT)[way][kt]
                        st = stage_slot("heads", h, j0 + n, w)
                        if way == 0:
                            dve.wait_ge(act_drain, drained("heads", h, f"s{kt}")[1])
                        tt(st, scr[:, kt, a:a + w], dec[:, way, m:m + w], ALU.mult).then_inc(stage_full, 1)
                        stage_lo_part("heads", h, j0 + n, pa_lo[:, at:at + w], pa_hi[:, at:at + w], w)
                        if n in splits:
                            split_lo("heads", h, splits[n])

                dve.wait_ge(mask_done, h * 2 + 2)
                decayed(0, 6, 4, [(LAT, 0, 256, 512), (LAT + 1, 0, 128, 512)]
                        + [(kt, kt * P, 0, 512 - kt * P) for kt in range(LAT)], {1: 10, 3: 11, 5: 12})
                split_lo("heads", h, 13)
                for t in range(LAT):
                    dve.wait_ge(pe_step, step_of("heads", h, f"of{t}"))
                    statistics([bank[4 + t][:, :]], t, h * 8 + (BASE_STAT["heads"] + t))
                    dve.wait_ge(act_drain, drained("heads", h, f"gf{t}")[1])
                    stt(y[:, t, :], bank[4 + t][:, :], mv[:, t, 0:1], gs[:, t, :], ALU.subtract, ALU.mult)\
                        .then_inc(dve_drain, 1)
                    dve.wait_ge(rstd_ready, h * 8 + (BASE_STAT["heads"] + t + 1))
                    dve.wait_ge(dve_drain, drained("heads", h, f"of{t}")[1])
                    ts(y[:, t, :], y[:, t, :], rstd[:, t:t + 1], None, ALU.mult).then_inc(y_step, 1)
                split_lo("heads", h, 14)
                decayed(1, 12, 10, [(LAT, 0, 128, 512), (LAT + 1, 0, 0, 512)]
                        + [(kt, 0, 640 - kt * P, (kt + 1) * P) for kt in reversed(range(LAT))], {1: 15, 3: 16})
                def y_low(t):
                    dve.wait_ge(psum_hi, h * 10 + (TILES0 + LAT - t))
                    tt(act_lo1[:, :, t * P:(t + 1) * P], bank[4 + t][:, :].rearrange("p (a b) -> p a b", a=CH),
                       f32(act_hi1[:, :, t * P:(t + 1) * P]), ALU.subtract).then_inc(dve_drain, 1)

                for n, t in enumerate(reversed(range(LAT))):
                    if t == 0:
                        y_low(3)
                    dve.wait_ge(pe_step, step_of("heads", h, f"ob{t}"))
                    statistics([bank[4 + t][:, :]], 4 + t, h * 8 + (BASE_STAT["heads"] + LAT + n))
                    dve.wait_ge(act_drain, drained("heads", h, f"gb{t}")[1])
                    if n >= 2:
                        dve.wait_ge(y_step, h * 8 + (LAT + n - 1))
                    stt(rbuf[:, n % 2, :], bank[4 + t][:, :], mv[:, 4 + t, 0:1], gs[:, t, :], ALU.subtract, ALU.mult)\
                        .then_inc(dve_drain, 1)
                    if t == 0:
                        y_low(2)
                    dve.wait_ge(rstd_ready, h * 8 + (BASE_STAT["heads"] + LAT + n + 1))
                    dve.wait_ge(dve_drain, drained("heads", h, f"ob{t}")[1])
                    stt(y[:, t, :], rbuf[:, n % 2, :], rstd[:, 4 + t:5 + t], y[:, t, :], ALU.mult, ALU.add)\
                        .then_inc(y_step, 1)
                y_low(1)
                y_low(0)
                if isinstance(h, int):
                    down_and_rows("heads", h, 16, LAT, "ln1a")
                else:
                    down("heads", h, 16, LAT)
                    split_lo("heads", h, 21)

            with nc.vector.Fori(0, HEADS - 1) as h:
                head(h)
            head(HEADS - 1)
            ln_split("ln1a", LAT, "ffn1")
            dve.wait_ge(act_drain, before("A", "ffn1"))
            with nc.vector.Fori(0, PIECES_F - 1) as p:
                ffn("ffn1", p, 1, TOKL, act_hi1, act_lo1, LAT)
            ffn("ffn1", PIECES_F - 1, 1, TOKL, act_hi1, act_lo1, LAT, "ln1b")

        @block.gpsimd
        def _(pool):
            gt = nc.gpsimd.tensor_tensor

            def power(phase, i, n, s):
                done = BASE_STAT[phase] + n + 1
                if not isinstance(i, int) or i:
                    done = i * 8 + done
                pool.wait_ge(var_ready, done)
                gt(rstd[:, s:s + 1], veps[:, s:s + 1], mhalf[:, s:s + 1], ALU.pow).then_inc(rstd_ready, 1)

            def add_one(phase, i, half, t, tiles):
                j = half * tiles + t
                e = BASE[phase]["add"] + j
                pool.wait_ge(dve_drain, drained(phase, i, f"down{half}.{t}")[1])
                if e >= 2 * tiles or not isinstance(i, int):
                    pool.wait_ge(res_added, count("add", phase, i, j) - 2 * tiles)
                r = res(t)[:, half * 512:(half + 1) * 512]
                gt(r, r, gy[:, e % 2, :], ALU.add).then_inc(res_added, 1)

            def add(phase, i, tiles):
                for half in range(2):
                    for t in range(tiles):
                        add_one(phase, i, half, t, tiles)

            def add_last(phase, i, tiles, ln_phase, between=lambda: None):
                for t in range(tiles):
                    add_one(phase, i, 0, t, tiles)
                between()
                for t in range(tiles):
                    add_one(phase, i, 1, t, tiles)
                    if t >= 1:
                        power(ln_phase, 0, t - 1, t - 1)
                power(ln_phase, 0, tiles - 1, tiles - 1)

            def diagonal(layer, part, j):
                v, half = j // 2, j % 2
                c = 8 * part + 4 * half
                gt(DIAG[j].rearrange("p (a b) -> p a b", a=4), ident[:, :].unsqueeze(1).to_broadcast([P, 4, P]),
                   modc[:, layer, c:c + 4, v:v + 1].to_broadcast([P, 4, P]), ALU.mult).then_inc(diag_ready, 1)

            def diagonals(phase, layer, part, n):
                pool.wait_ge(stage_lo, before("stage", phase))
                for j in range(n):
                    diagonal(layer, part, j)

            def scale_lnbc(k, lnbc):
                pool.wait_ge(lnbc_in, 32 * (k + 1))
                nc.gpsimd.tensor_scalar(lnbc[:, :, :], lnbc[:, :, :], ALPHA, None, ALU.mult)\
                    .then_inc(lnbc_scaled, 1)

            def ln(phase, k, lnbc, tiles, all_tiles):
                pool.wait_ge(lnbc_scaled, k + 1)
                for t in range(tiles):
                    g = [t < t1 for _, t1 in LN_GROUPS[all_tiles]].index(True)
                    pool.wait_ge(pe_step, step_of(phase, 0, f"ln{g}.{KC - 1}"))
                    gt(res(t), res(t), lnbc[:, 0, :], ALU.mult).then_inc(res_mul, 1)
                    pool.wait_ge(res_mul, BASE_RES[phase] - TILES0 + t + 1)
                    gt(res(t), res(t), lnbc[:, 1, :], ALU.add).then_inc(res_base, 1)

            nc.gpsimd.memset(scT[:, :, :], 0.0).then_inc(sc_zero, 1)
            nc.gpsimd.memset(ones[:, :], 1.0).then_inc(pool_const, 1)
            nc.gpsimd.memset(mhalf[:, :], -0.5).then_inc(pool_const, 1)
            pool.wait_ge(res_in, 32)
            for t in range(TILES0):
                nc.gpsimd.tensor_scalar(res(t), res(t), ALPHA, None, ALU.mult).then_inc(res_base, 1)
            pool.wait_ge(pool_const, 2)
            pool.wait_ge(const_in, N_CONST)
            pool.wait_ge(dve_drain, before("D", "gate0a"))
            diagonals("gate0a", 0, 2, 4)
            for t in range(TILES0):
                power("v", 0, t, t)
            pool.wait_ge(res_base, BASE_RES["ln0a"])
            for p in range(PIECES_A - 1):
                add("gmlp", p, TILES0)
            scale_lnbc(0, lnbc0)
            add_last("gmlp", PIECES_A - 1, TILES0, "ln0a", lambda: diagonals("ln0a", 0, 5, 4))
            ln("ln0a", 0, lnbc0, TILES0, TILES0)
            pool.wait_ge(res_base, BASE_RES["ln0b"])
            with nc.gpsimd.Fori(0, PIECES_F - 1) as p:
                add("ffn0", p, TILES0)
            scale_lnbc(1, lnbc0)
            add_last("ffn0", PIECES_F - 1, TILES0, "ln0b", lambda: diagonals("ln0b", 1, 2, 2))
            ln("ln0b", 1, lnbc0, LAT, TILES0)
            pool.wait_ge(res_base, BASE_RES["ln1a"])
            def head_powers(h):
                for t in range(LAT):
                    power("heads", h, t, t)
                for n, t in enumerate(reversed(range(LAT))):
                    power("heads", h, LAT + n, 4 + t)

            with nc.gpsimd.Fori(0, HEADS - 1) as h:
                head_powers(h)
                add("heads", h, LAT)
            head_powers(HEADS - 1)
            pool.wait_ge(y_step, 8 * HEADS)
            add_last("heads", HEADS - 1, LAT, "ln1a", lambda: diagonals("ln1a", 1, 5, 2))
            scale_lnbc(2, lnbc1)
            ln("ln1a", 2, lnbc1, LAT, LAT)
            pool.wait_ge(res_base, BASE_RES["ln1b"])
            with nc.gpsimd.Fori(0, PIECES_F - 1) as p:
                add("ffn1", p, LAT)
            add_last("ffn1", PIECES_F - 1, LAT, "ln1b")
            pool.wait_ge(lnbc_in, 128)
            pool.wait_ge(xn_ready, XN_BASE["ln1b"] + 1)
            gt(res(0), res(0), lnbc1[:, 0, :], ALU.mult).then_inc(res_mul, 1)
            pool.wait_ge(res_mul, BASE_RES["ln1b"] - TILES0 + 1)
            gt(res(0), res(0), lnbc1[:, 1, :], ALU.add).then_inc(res_base, 1)


def kernel(**inputs):
    import numpy as _np
    import concourse.bacc as _bacc
    from concourse import mybir as _mybir
    from concourse.bass_utils import run_bass_kernel_spmd as _run

    a = {k: _np.asarray(v) for k, v in inputs.items()}

    def feature_units(w):
        return w.reshape(KC, P, -1, P).transpose(2, 1, 0, 3).reshape(-1, P, UNIT)

    def token_units(w):
        return w.reshape(w.shape[0] // 256, 2, P, -1, 512).transpose(3, 0, 2, 1, 4).reshape(-1, P, UNIT)

    def mod_units(w, wide):
        return w.reshape(KC, P, -1, wide).transpose(2, 0, 1, 3).reshape(-1, P, wide)

    def ffn_units(w1, w2):
        for p in range(PIECES_F):
            yield feature_units(w1[:, p * 512:(p + 1) * 512])
            yield token_units(w2[p * 512:(p + 1) * 512])

    def units():
        w_in, w_out = a["a_w_in"][0], a["a_w_out"][0]
        yield token_units(w_in[:, 2048:])
        for p in range(PIECES_A):
            yield feature_units(w_in[:, p * 512:(p + 1) * 512])
            yield token_units(w_out[p * 512:(p + 1) * 512])
        yield from ffn_units(a["ffn_w1"][0], a["ffn_w2"][0])
        w_in, w_out = a["b_w_in"][0], a["b_w_out"][0]
        for h in range(HEADS):
            yield feature_units(w_in[:, h * DK:(h + 1) * DK])
            yield feature_units(w_in[:, 1024 + h * DK:1024 + (h + 1) * DK])
            for part in range(3):
                at = 2048 * (part + 1) + h * DV
                yield token_units(w_in[:, at:at + DV])
            yield token_units(w_out[h * DV:(h + 1) * DV])
        yield from ffn_units(a["ffn_w1"][1], a["ffn_w2"][1])

    def columns(v):
        return v.reshape(-1, P).T

    lns = [a[f"ln{n}_{x}"][l] for l in range(DEPTH) for n in (1, 2) for x in "gb"]
    t = _np.arange(TOKL)
    inv = (_np.float32(10000.0) ** (-_np.arange(DK // 4, dtype=_np.float32) / _np.float32(DK // 4)))
    ang = _np.concatenate([inv[:, None] * (t // 64).astype(_np.float32), inv[:, None] * (t % 64).astype(_np.float32)])
    rope = _np.stack([_np.cos(ang), _np.sin(ang)], 1).astype(_np.float32)
    j, m = _np.arange(P)[:, None], _np.arange(768)[None]
    dist = _np.stack([_np.maximum(m - j, 0), _np.maximum(640 + j - m, 0)], 1).astype(_np.float32)
    small = _np.concatenate([_np.eye(P), m[:, :P] >= j, j >= m[:, :P]], 1).astype(_np.float32)
    arrays = {
        "w_units": _np.concatenate(list(units())),
        "mod0_units": _np.concatenate([mod_units(a["ada_w"][0][:, :2048].reshape(D, 2, 2, 512)
                                                 .transpose(0, 2, 1, 3).reshape(D, 2048), WIDE_M0),
                                       mod_units(a["ada_w"][0][:, 2048:], WIDE_M0)]),
        "mod1_units": mod_units(a["ada_w"][1], WIDE_M1),
        "xT": _np.concatenate([a["x"][0], a["ctx"][0]]).T.reshape(KC, P, TOK0).transpose(1, 0, 2),
        "x": a["x"][0],
        "ctx": a["ctx"][0],
        "cols": _np.concatenate([columns(a["ada_b"])] + [columns(v) for v in lns]
                                + [columns(a["a_b_in"][0, :2048]), columns(a["a_ln_g"][0]), columns(a["a_ln_b"][0])], 1),
        "cvec": _np.stack([columns(a["c"][0]), columns(a["c_ctx"])], 2),
        "wsT": a["a_w_s"][0].transpose(2, 0, 1),
        "bs": a["a_b_s"][0].reshape(-1),
        "bv": a["a_b_in"][0, 2048:],
        "ln": _np.stack(lns),
        "decay": a["b_decay"][0].reshape(-1),
        "dist": dist,
        "rope": rope,
        "small": small,
    }
    nc = _bacc.Bacc("TRN2", target_bir_lowering=False, num_devices=1, dynamic_dma_scratch_size=1024)
    args, feeds = [], {}
    for name, v in arrays.items():
        feeds[name + "_d"] = _np.ascontiguousarray(v)
        args.append(nc.dram_tensor(name + "_d", v.shape, _mybir.dt.float32, kind="ExternalInput").ap())
    out = nc.dram_tensor("out_d", (TOKL, D), _mybir.dt.float32, kind="ExternalOutput").ap()
    build(nc, *args, out)
    r = _run(nc, [feeds], core_ids=[0])
    return r.results[0]["out_d"].reshape(1, TOKL, D)
```
